# Optimizing a Trainium2 kernel written in Bass

```python
import math
import jax, jax.numpy as jnp
from jax import lax
import numpy as np

D_MODEL = 1024
BATCH = 1
SEQ = 256
DEPTH = 2

GRID_W = 64
CTX_LEN = 256
N_MIXERS = 2
NORM_EPS = 1e-6

DN_QK_HEADS = 8
DN_V_HEADS = 16
DN_HEAD_K = 128
DN_HEAD_V = 128
DN_KEY_DIM = DN_QK_HEADS * DN_HEAD_K
DN_VAL_DIM = DN_V_HEADS * DN_HEAD_V
DN_CONV_DIM = 2 * DN_KEY_DIM + DN_VAL_DIM
DN_CONV_K = 5
DN_CHUNK = 64
DN_IN_DIM = DN_CONV_DIM + DN_VAL_DIM + 4 * DN_V_HEADS
DT_MIN = 0.001
DT_MAX = 0.1

ATT_Q_HEADS = 8
ATT_KV_HEADS = 2
ATT_HEAD_DIM = 128
ATT_Q_DIM = ATT_Q_HEADS * ATT_HEAD_DIM
ATT_KV_DIM = ATT_KV_HEADS * ATT_HEAD_DIM
ATT_IN_DIM = ATT_Q_DIM + 2 * ATT_KV_DIM + ATT_Q_DIM
ATT_BLOCK = 128
ROPE_THETA = 10000.0

N_DN_LAYERS = (DEPTH + N_MIXERS - 1) // N_MIXERS
N_ATT_LAYERS = DEPTH // N_MIXERS


F32 = jnp.float32

def rms_norm(x, g):
    xf = x.astype(F32)
    y = xf * lax.rsqrt(jnp.mean(xf * xf, axis=-1, keepdims=True) + NORM_EPS)
    return (y * g.astype(F32)).astype(x.dtype)

def l2_norm(x):
    xf = x.astype(F32)
    return (xf * lax.rsqrt(jnp.sum(xf * xf, axis=-1, keepdims=True) + NORM_EPS)).astype(x.dtype)

def centred_dwconv(x, w):
    k = w.shape[0]
    return lax.conv_general_dilated(x, w[:, None, :].astype(x.dtype), window_strides=(1,),
                                    padding=[(k // 2, k // 2)],
                                    dimension_numbers=('NWC', 'WIO', 'NWC'),
                                    feature_group_count=x.shape[-1])

def chunk_gated_delta(q, k, v, g, beta, s0):
    b, h, l, dk = k.shape
    dv = v.shape[-1]
    n = l // DN_CHUNK
    q = q.astype(F32) * (dk ** -0.5)
    k = k.astype(F32)
    v32 = v.astype(F32)
    ch = lambda t: t.reshape(b, h, n, DN_CHUNK, *t.shape[3:])
    qc, kc, vc = ch(q), ch(k), ch(v32)
    gc = jnp.cumsum(ch(g.astype(F32)), axis=-1)
    bc = ch(beta.astype(F32))
    idx = jnp.arange(DN_CHUNK)
    lower = idx[:, None] >= idx[None, :]
    strict = idx[:, None] > idx[None, :]
    decay = jnp.exp(jnp.where(lower, gc[..., :, None] - gc[..., None, :], -jnp.inf))
    kb = kc * bc[..., None]
    vb = vc * bc[..., None]
    a = jnp.where(strict, jnp.einsum('bhncd,bhnsd->bhncs', kb, kc) * decay, 0.0)
    eye = jnp.eye(DN_CHUNK, dtype=F32)
    t_inv = lax.linalg.triangular_solve(eye + a, jnp.broadcast_to(eye, a.shape),
                                        left_side=True, lower=True, unit_diagonal=True)
    u = jnp.einsum('bhncs,bhnse->bhnce', t_inv, vb)
    w = jnp.einsum('bhncs,bhnsd->bhncd', t_inv, kb * jnp.exp(gc)[..., None])
    qk = jnp.einsum('bhncd,bhnsd->bhncs', qc, kc) * decay
    q_dec = qc * jnp.exp(gc)[..., None]
    k_dec = kc * jnp.exp(gc[..., -1:] - gc)[..., None]
    g_last = jnp.exp(gc[..., -1])

    def step(s, xs):
        qk_i, qd_i, kd_i, u_i, w_i, gl_i = xs
        v_new = u_i - jnp.einsum('bhcd,bhde->bhce', w_i, s)
        o = jnp.einsum('bhcd,bhde->bhce', qd_i, s) + jnp.einsum('bhcs,bhse->bhce', qk_i, v_new)
        s = s * gl_i[..., None, None] + jnp.einsum('bhcd,bhce->bhde', kd_i, v_new)
        return s, o

    xs = tuple(jnp.moveaxis(t_, 2, 0) for t_ in (qk, q_dec, k_dec, u, w, g_last))
    s_fin, o = lax.scan(step, s0.astype(F32), xs)
    o = jnp.moveaxis(o, 0, 2).reshape(b, h, l, dv)
    return o.astype(v.dtype), s_fin

def bidir_delta(q, k, v, g, beta, s0_f, s0_b):
    o_f, s_f = chunk_gated_delta(q, k, v, g[:, 0], beta[:, 0], s0_f)
    fl = lambda t: jnp.flip(t, axis=2)
    o_b, s_b = chunk_gated_delta(fl(q), fl(k), fl(v), fl(g[:, 1]), fl(beta[:, 1]), s0_b)
    return o_f + fl(o_b), s_f, s_b

def deltanet_mixer(u_lat, u_ctx, w_in, conv_w, a_log, dt_bias, o_norm_g, w_out, need_ctx):
    def branch_inputs(u):
        b, l, _ = u.shape
        p = u @ w_in
        qkv = jax.nn.silu(centred_dwconv(p[..., :DN_CONV_DIM], conv_w))
        z = p[..., DN_CONV_DIM:DN_CONV_DIM + DN_VAL_DIM]
        ab = p[..., DN_CONV_DIM + DN_VAL_DIM:].reshape(b, l, 2, 2, DN_V_HEADS).astype(F32)
        q, k, v = jnp.split(qkv, [DN_KEY_DIM, 2 * DN_KEY_DIM], axis=-1)
        rep = DN_V_HEADS // DN_QK_HEADS
        q = jnp.repeat(l2_norm(q.reshape(b, l, DN_QK_HEADS, DN_HEAD_K)), rep, axis=2)
        k = jnp.repeat(l2_norm(k.reshape(b, l, DN_QK_HEADS, DN_HEAD_K)), rep, axis=2)
        v = v.reshape(b, l, DN_V_HEADS, DN_HEAD_V)
        beta = jax.nn.sigmoid(ab[:, :, 0])
        g = -jnp.exp(a_log.astype(F32)) * jax.nn.softplus(ab[:, :, 1] + dt_bias.astype(F32))
        bhl = lambda t: jnp.transpose(t, (0, 2, 1, 3))
        return bhl(q), bhl(k), bhl(v), jnp.transpose(g, (0, 2, 3, 1)), jnp.transpose(beta, (0, 2, 3, 1)), z

    def finish(o, z):
        b, h, l, dv = o.shape
        o = rms_norm(jnp.transpose(o, (0, 2, 1, 3)), o_norm_g).astype(z.dtype)
        return (o.reshape(b, l, DN_VAL_DIM) * jax.nn.silu(z)) @ w_out

    qc, kc, vc, gc, bc, zc = branch_inputs(u_ctx)
    s_zero = jnp.zeros((u_ctx.shape[0], DN_V_HEADS, DN_HEAD_K, DN_HEAD_V), F32)
    o_ctx, s_f, s_b = bidir_delta(qc, kc, vc, gc, bc, s_zero, s_zero)
    ql, kl, vl, gl, bl, zl = branch_inputs(u_lat)
    o_lat, _, _ = bidir_delta(ql, kl, vl, gl, bl, s_f, s_b)
    y_lat = finish(o_lat, zl)
    y_ctx = finish(o_ctx, zc) if need_ctx else None
    return y_lat, y_ctx

def axial_rope_angles(n):
    rows = n // GRID_W
    row = jnp.broadcast_to(jnp.arange(rows)[:, None], (rows, GRID_W)).reshape(-1).astype(F32)
    col = jnp.broadcast_to(jnp.arange(GRID_W)[None, :], (rows, GRID_W)).reshape(-1).astype(F32)
    axis_dim = ATT_HEAD_DIM // 2
    inv = ROPE_THETA ** (-jnp.arange(0, axis_dim, 2, dtype=F32) / axis_dim)
    return row[:, None] * inv, col[:, None] * inv

def rope_rotate(x, ang):
    x1, x2 = jnp.split(x, 2, axis=-1)
    cos = jnp.cos(ang)[:, None, :].astype(x.dtype)
    sin = jnp.sin(ang)[:, None, :].astype(x.dtype)
    return jnp.concatenate([x1 * cos - x2 * sin, x2 * cos + x1 * sin], axis=-1)

def apply_axial_rope(x, ang_r, ang_c):
    xr, xc = jnp.split(x, 2, axis=-1)
    return jnp.concatenate([rope_rotate(xr, ang_r), rope_rotate(xc, ang_c)], axis=-1)

def gqa_attend(q, k, v):
    b, lq, hq, d = q.shape
    qg = q.reshape(b, lq, ATT_KV_HEADS, hq // ATT_KV_HEADS, d)
    s = jnp.einsum('bqhgd,bkhd->bhgqk', qg, k).astype(F32) * (d ** -0.5)
    p = jax.nn.softmax(s, axis=-1).astype(v.dtype)
    return jnp.einsum('bhgqk,bkhd->bqhgd', p, v).reshape(b, lq, hq, d)

def blocked_gqa(q, k, v):
    b, lq, hq, d = q.shape
    nb = lq // ATT_BLOCK
    qb = jnp.moveaxis(q.reshape(b, nb, ATT_BLOCK, hq, d), 1, 0)
    ob = lax.map(lambda qi: gqa_attend(qi, k, v), qb)
    return jnp.moveaxis(ob, 0, 1).reshape(b, lq, hq, d)

def attention_mixer(u_lat, u_ctx, w_in, q_norm_g, k_norm_g, w_out, need_ctx):
    def project(u):
        b, l, _ = u.shape
        p = u @ w_in
        q, k, v, z = jnp.split(p, [ATT_Q_DIM, ATT_Q_DIM + ATT_KV_DIM, ATT_Q_DIM + 2 * ATT_KV_DIM], axis=-1)
        q = rms_norm(q.reshape(b, l, ATT_Q_HEADS, ATT_HEAD_DIM), q_norm_g)
        k = rms_norm(k.reshape(b, l, ATT_KV_HEADS, ATT_HEAD_DIM), k_norm_g)
        v = v.reshape(b, l, ATT_KV_HEADS, ATT_HEAD_DIM)
        return q, k, v, z

    def finish(o, z):
        b, l = o.shape[:2]
        return (o.reshape(b, l, ATT_Q_DIM) * jax.nn.silu(z)) @ w_out

    qc, kc, vc, zc = project(u_ctx)
    ql, kl, vl, zl = project(u_lat)
    ang_r, ang_c = axial_rope_angles(u_lat.shape[1])
    ql = apply_axial_rope(ql, ang_r, ang_c)
    kl = apply_axial_rope(kl, ang_r, ang_c)
    k_all = jnp.concatenate([kc, kl], axis=1)
    v_all = jnp.concatenate([vc, vl], axis=1)
    y_lat = finish(blocked_gqa(ql, k_all, v_all), zl)
    y_ctx = finish(gqa_attend(qc, kc, vc), zc) if need_ctx else None
    return y_lat, y_ctx

def first_inputs(seed: int = 0) -> dict:
    key = jax.random.key(seed)
    ks = jax.random.split(key, 20)
    nrm = lambda k, shape, scale: jax.random.normal(k, shape, F32) * scale
    d = D_MODEL
    n_dn, n_att = N_DN_LAYERS, N_ATT_LAYERS
    a_log = jnp.log(jax.random.uniform(ks[8], (n_dn, 2, DN_V_HEADS), F32, 1.0, 16.0))
    dt = jnp.exp(jax.random.uniform(ks[9], (n_dn, 2, DN_V_HEADS), F32, math.log(DT_MIN), math.log(DT_MAX)))
    dt_bias = dt + jnp.log(-jnp.expm1(-dt))
    return {
        'x': nrm(ks[0], (BATCH, SEQ, d), 1.0),
        'c': nrm(ks[1], (BATCH, d), 1.0),
        'ctx': nrm(ks[2], (BATCH, CTX_LEN, d), 1.0),
        'c_ctx': nrm(ks[3], (d,), 1.0),
        'norm_g': 1.0 + nrm(ks[4], (DEPTH, d), 0.02),
        'ada_w': nrm(ks[5], (DEPTH, d, 3 * d), 0.5 * d ** -0.5),
        'ada_b': nrm(ks[6], (DEPTH, 3 * d), 0.02),
        'dn_w_in': nrm(ks[7], (n_dn, d, DN_IN_DIM), d ** -0.5),
        'dn_conv_w': nrm(ks[10], (n_dn, DN_CONV_K, DN_CONV_DIM), DN_CONV_K ** -0.5),
        'dn_a_log': a_log,
        'dn_dt_bias': dt_bias,
        'dn_o_norm_g': 1.0 + nrm(ks[11], (n_dn, DN_HEAD_V), 0.02),
        'dn_w_out': nrm(ks[12], (n_dn, DN_VAL_DIM, d), DN_VAL_DIM ** -0.5),
        'att_w_in': nrm(ks[13], (n_att, d, ATT_IN_DIM), d ** -0.5),
        'att_q_norm_g': 1.0 + nrm(ks[14], (n_att, ATT_HEAD_DIM), 0.02),
        'att_k_norm_g': 1.0 + nrm(ks[15], (n_att, ATT_HEAD_DIM), 0.02),
        'att_w_out': nrm(ks[16], (n_att, ATT_Q_DIM, d), ATT_Q_DIM ** -0.5),
        'final_norm_g': 1.0 + nrm(ks[17], (d,), 0.02),
    }

def first_block(x, c, ctx, c_ctx, norm_g, ada_w, ada_b, dn_w_in, dn_conv_w, dn_a_log, dn_dt_bias,
              dn_o_norm_g, dn_w_out, att_w_in, att_q_norm_g, att_k_norm_g, att_w_out, final_norm_g):
    h_lat, h_ctx = x, ctx
    sc_lat, sc_ctx = jax.nn.silu(c), jax.nn.silu(c_ctx)
    for i in range(DEPTH):
        need_ctx = i < DEPTH - 1
        shift, scale, gate = jnp.split(sc_lat @ ada_w[i] + ada_b[i], 3, axis=-1)
        shift_c, scale_c, gate_c = jnp.split(sc_ctx @ ada_w[i] + ada_b[i], 3, axis=-1)
        u_lat = rms_norm(h_lat, norm_g[i]) * (1.0 + scale[:, None]) + shift[:, None]
        u_ctx = rms_norm(h_ctx, norm_g[i]) * (1.0 + scale_c) + shift_c
        j = i // N_MIXERS
        if i % N_MIXERS == 0:
            y_lat, y_ctx = deltanet_mixer(u_lat, u_ctx, dn_w_in[j], dn_conv_w[j], dn_a_log[j], dn_dt_bias[j],
                                          dn_o_norm_g[j], dn_w_out[j], need_ctx)
        else:
            y_lat, y_ctx = attention_mixer(u_lat, u_ctx, att_w_in[j], att_q_norm_g[j], att_k_norm_g[j],
                                           att_w_out[j], need_ctx)
        h_lat = h_lat + gate[:, None] * y_lat
        if need_ctx:
            h_ctx = h_ctx + gate_c * y_ctx
    return rms_norm(h_lat, final_norm_g)


DEPTH_2 = 1

SSM_INNER = D_MODEL
SSM_HEAD_DIM = 64
SSM_HEADS = SSM_INNER // SSM_HEAD_DIM
SSM_GROUPS = 2
SSM_STATE = 128
SSM_CONV = 5
SSM_CHUNK = 128
SSM_CONV_DIM = SSM_INNER + 2 * SSM_GROUPS * SSM_STATE
RWKV_DIM = D_MODEL // 2
RWKV_HEAD_DIM = 64
RWKV_HEADS = RWKV_DIM // RWKV_HEAD_DIM
RWKV_W_RANK = 64
RWKV_A_RANK = 64
RWKV_G_RANK = 128
RWKV_COLS = 3 * RWKV_DIM + RWKV_W_RANK + RWKV_A_RANK + RWKV_G_RANK
RWKV_DECAY_SCALE = 0.6065306597
RWKV_LN_EPS = 64e-5
HGRN_DIM = D_MODEL // 2
HGRN_HEAD_DIM = 128
HGRN_HEADS = HGRN_DIM // HGRN_HEAD_DIM
HGRN_CHUNK = 64
HGRN_COLS = 5 * HGRN_DIM
N_BRANCH = 3
GATE_COLS = N_BRANCH * D_MODEL
N_IN = SSM_INNER + SSM_CONV_DIM + 2 * SSM_HEADS + RWKV_COLS + HGRN_COLS + GATE_COLS
D_FF = (8 * D_MODEL + 3 * 256 - 1) // (3 * 256) * 256


def _split_points(sizes):
    pts, acc = [], 0
    for s in sizes[:-1]:
        acc += s
        pts.append(acc)
    return pts

def rmsnorm(x, w, eps=NORM_EPS):
    xf = x.astype(jnp.float32)
    y = xf * lax.rsqrt(jnp.mean(xf * xf, axis=-1, keepdims=True) + eps)
    return (y * w.astype(jnp.float32)).astype(x.dtype)

def head_rmsnorm(x, w, n_heads, eps=NORM_EPS):
    b, l, d = x.shape
    xf = x.astype(jnp.float32).reshape(b, l, n_heads, d // n_heads)
    y = xf * lax.rsqrt(jnp.mean(xf * xf, axis=-1, keepdims=True) + eps)
    return (y.reshape(b, l, d) * w.astype(jnp.float32)).astype(x.dtype)

def flip_t(t):
    return jnp.flip(t, axis=1)

def centred_depthwise_conv(x, w, b):
    pad = (w.shape[0] - 1) // 2
    y = lax.conv_general_dilated(x, w, window_strides=(1,), padding=[(pad, pad)],
                                 dimension_numbers=('NWC', 'WIO', 'NWC'),
                                 feature_group_count=x.shape[-1])
    return y + b

def ssd_chunked(x, dt, a, bm, cm):
    b, L, H, P = x.shape
    G, N = bm.shape[2], bm.shape[3]
    hg = H // G
    c = L // SSM_CHUNK
    Q = SSM_CHUNK
    x = x.reshape(b, c, Q, G, hg, P)
    dt = dt.reshape(b, c, Q, G, hg)
    bm = bm.reshape(b, c, Q, G, N)
    cm = cm.reshape(b, c, Q, G, N)
    a_cum = jnp.cumsum(dt * a.reshape(G, hg), axis=2)
    xdt = x * dt[..., None]
    seg = a_cum[:, :, :, None] - a_cum[:, :, None]
    mask = jnp.tril(jnp.ones((Q, Q), dtype=bool))[:, :, None, None]
    lmat = jnp.exp(jnp.where(mask, seg, -jnp.inf))
    cb = jnp.einsum('bcqgn,bcsgn->bcqsg', cm, bm)
    y_diag = jnp.einsum('bcqsgh,bcsghp->bcqghp', cb[..., None] * lmat, xdt)
    decay_to_end = jnp.exp(a_cum[:, :, -1:] - a_cum)
    chunk_states = jnp.einsum('bcsgn,bcsghp->bcghpn', bm, xdt * decay_to_end[..., None])
    chunk_decay = jnp.exp(a_cum[:, :, -1])

    def step(s, inp):
        st, dec = inp
        return dec[..., None, None] * s + st, s

    s0 = jnp.zeros((b, G, hg, P, N), dtype=x.dtype)
    _, prev = lax.scan(step, s0, (jnp.moveaxis(chunk_states, 1, 0), jnp.moveaxis(chunk_decay, 1, 0)))
    prev = jnp.moveaxis(prev, 0, 1)
    y_off = jnp.einsum('bcqgn,bcghpn->bcqghp', cm, prev) * jnp.exp(a_cum)[..., None]
    return (y_diag + y_off).reshape(b, L, H, P)

def ssd_branch(z, xbc, dt_raw, conv_w, conv_b, dt_bias, a_log, d_skip, norm_w):
    b, L, _ = z.shape
    xbc = jax.nn.silu(centred_depthwise_conv(xbc, conv_w, conv_b))
    xs, bm, cm = jnp.split(xbc, [SSM_INNER, SSM_INNER + SSM_GROUPS * SSM_STATE], axis=-1)
    xs = xs.reshape(b, L, SSM_HEADS, SSM_HEAD_DIM)
    bm = bm.reshape(b, L, SSM_GROUPS, SSM_STATE)
    cm = cm.reshape(b, L, SSM_GROUPS, SSM_STATE)
    dt = jax.nn.softplus(dt_raw.reshape(b, L, 2, SSM_HEADS) + dt_bias)
    a = -jnp.exp(a_log)
    y_f = ssd_chunked(xs, dt[:, :, 0], a[0], bm, cm)
    y_b = flip_t(ssd_chunked(flip_t(xs), flip_t(dt[:, :, 1]), a[1], flip_t(bm), flip_t(cm)))
    y = y_f + y_b + xs * d_skip[:, None]
    y = y.reshape(b, L, SSM_INNER) * jax.nn.silu(z)
    return rmsnorm(y, norm_w)

def token_shift_bidir(p, mu):
    prev = jnp.pad(p[:, :-1], ((0, 0), (1, 0), (0, 0)))
    nxt = jnp.pad(p[:, 1:], ((0, 0), (0, 1), (0, 0)))
    return p + mu[0] * (prev - p) + mu[1] * (nxt - p)

def rwkv7_scan(r, w, k, v, kk, a, reverse):
    b = r.shape[0]
    s0 = jnp.zeros((b, RWKV_HEADS, RWKV_HEAD_DIM, RWKV_HEAD_DIM), dtype=r.dtype)

    def step(s, inp):
        r_t, w_t, k_t, v_t, kk_t, a_t = inp
        sa = jnp.einsum('bhvk,bhk->bhv', s, -kk_t)
        s = (s * w_t[:, :, None, :] + sa[..., None] * (kk_t * a_t)[:, :, None, :]
             + v_t[..., None] * k_t[:, :, None, :])
        return s, jnp.einsum('bhvk,bhk->bhv', s, r_t)

    xs = (jnp.moveaxis(r, 1, 0), jnp.moveaxis(w, 1, 0), jnp.moveaxis(k, 1, 0),
          jnp.moveaxis(v, 1, 0), jnp.moveaxis(kk, 1, 0), jnp.moveaxis(a, 1, 0))
    _, y = lax.scan(step, s0, xs, reverse=reverse)
    return jnp.moveaxis(y, 0, 1)

def rwkv7_branch(p, mu, w0, w_up, a0, a_up, g_up, k_k, k_a, r_k, ln_w, ln_b):
    b, L, _ = p.shape
    p = token_shift_bidir(p, mu)
    r, k, v, wd, ad, gd = jnp.split(p, _split_points(
        [RWKV_DIM, RWKV_DIM, RWKV_DIM, RWKV_W_RANK, RWKV_A_RANK, RWKV_G_RANK]), axis=-1)

    def heads(t):
        return t.reshape(b, L, RWKV_HEADS, RWKV_HEAD_DIM)

    tw = jnp.tanh(wd)
    w_f = jnp.exp(-RWKV_DECAY_SCALE * jax.nn.sigmoid(w0[0] + tw @ w_up[0]))
    w_b = jnp.exp(-RWKV_DECAY_SCALE * jax.nn.sigmoid(w0[1] + tw @ w_up[1]))
    a = jax.nn.sigmoid(a0 + ad @ a_up)
    g = jax.nn.sigmoid(gd) @ g_up
    kk = heads(k * k_k).astype(jnp.float32)
    kk = (kk * lax.rsqrt(jnp.sum(kk * kk, axis=-1, keepdims=True) + 1e-12)).astype(p.dtype)
    k = k * (1.0 + (a - 1.0) * k_a)
    r, k, v, a = heads(r), heads(k), heads(v), heads(a)
    y = (rwkv7_scan(r, heads(w_f), k, v, kk, a, False)
         + rwkv7_scan(r, heads(w_b), k, v, kk, a, True))
    yf = y.astype(jnp.float32)
    mean = jnp.mean(yf, axis=-1, keepdims=True)
    var = jnp.mean(jnp.square(yf - mean), axis=-1, keepdims=True)
    yn = ((yf - mean) * lax.rsqrt(var + RWKV_LN_EPS)).reshape(b, L, RWKV_DIM)
    yn = (yn * ln_w.astype(jnp.float32) + ln_b.astype(jnp.float32)).astype(p.dtype)
    r_k_h = r_k.reshape(RWKV_HEADS, RWKV_HEAD_DIM)
    bonus = jnp.sum(r * k * r_k_h, axis=-1, keepdims=True) * v
    return (yn + bonus.reshape(b, L, RWKV_DIM)) * g

def hgrn2_chunk_scan(q, k, v, log_f):
    b, L, h, dk = q.shape
    dv = v.shape[-1]
    c = L // HGRN_CHUNK

    def chunks(t):
        return jnp.transpose(t.reshape(b, c, HGRN_CHUNK, h, t.shape[-1]), (1, 0, 3, 2, 4))

    mask = jnp.tril(jnp.ones((HGRN_CHUNK, HGRN_CHUNK), dtype=bool))[:, :, None]

    def step(s, inp):
        q_c, k_c, v_c, g_c = inp
        cum = jnp.cumsum(g_c, axis=2)
        o_inter = jnp.einsum('bhtk,bhkv->bhtv', q_c * jnp.exp(cum), s)
        diff = cum[:, :, :, None, :] - cum[:, :, None, :, :]
        decay = jnp.exp(jnp.where(mask, diff, -jnp.inf))
        scores = jnp.einsum('bhtsk,bhsk->bhts', q_c[:, :, :, None, :] * decay, k_c)
        o_intra = jnp.einsum('bhts,bhsv->bhtv', scores, v_c)
        last = cum[:, :, -1:, :]
        s = (jnp.exp(last[:, :, 0, :])[..., None] * s
             + jnp.einsum('bhsk,bhsv->bhkv', k_c * jnp.exp(last - cum), v_c))
        return s, o_inter + o_intra

    s0 = jnp.zeros((b, h, dk, dv), dtype=q.dtype)
    _, o = lax.scan(step, s0, (chunks(q), chunks(k), chunks(v), chunks(log_f)))
    return jnp.transpose(o, (1, 0, 3, 2, 4)).reshape(b, L, h, dv)

def hgrn2_branch(p, lb, norm_w):
    b, L, _ = p.shape
    q, f_fwd, f_bwd, i, g = jnp.split(p, 5, axis=-1)

    def heads(t):
        return t.reshape(b, L, HGRN_HEADS, HGRN_HEAD_DIM)

    def forget(f):
        ff = lb + (1.0 - lb) * jax.nn.sigmoid(f)
        return heads(jnp.log(ff)), heads(1.0 - ff)

    logf_f, k_f = forget(f_fwd)
    logf_b, k_b = forget(f_bwd)
    qh, ih = heads(q), heads(i)
    o_f = hgrn2_chunk_scan(qh, k_f, ih, logf_f)
    o_b = flip_t(hgrn2_chunk_scan(flip_t(qh), flip_t(k_b), flip_t(ih), flip_t(logf_b)))
    o = (o_f + o_b).reshape(b, L, HGRN_DIM)
    return head_rmsnorm(o, norm_w, HGRN_HEADS) * jax.nn.silu(g)

def second_inputs(seed: int = 0) -> dict:
    key = jax.random.key(seed)
    ks = iter(jax.random.split(key, 48))
    f32 = jnp.float32

    def nrm(shape, fan_in, scale=1.0):
        return scale * fan_in ** -0.5 * jax.random.normal(next(ks), shape, f32)

    def unif(shape, lo, hi):
        return jax.random.uniform(next(ks), shape, f32, lo, hi)

    def gain(shape):
        return 1.0 + 0.05 * jax.random.normal(next(ks), shape, f32)

    x = jax.random.normal(next(ks), (BATCH, SEQ, D_MODEL), f32)
    norm1_w = gain((DEPTH_2, D_MODEL))
    w_in = nrm((DEPTH_2, D_MODEL, N_IN), D_MODEL)
    ssm_conv_w = nrm((DEPTH_2, SSM_CONV, 1, SSM_CONV_DIM), SSM_CONV)
    ssm_conv_b = 0.02 * jax.random.normal(next(ks), (DEPTH_2, SSM_CONV_DIM), f32)
    dt0 = jnp.exp(unif((DEPTH_2, 2, SSM_HEADS), float(np.log(1e-3)), float(np.log(1e-1))))
    ssm_dt_bias = dt0 + jnp.log(-jnp.expm1(-dt0))
    ssm_a_log = jnp.log(unif((DEPTH_2, 2, SSM_HEADS), 1.0, 16.0))
    ssm_d = gain((DEPTH_2, SSM_HEADS))
    ssm_norm_w = gain((DEPTH_2, SSM_INNER))
    rwkv_mu = unif((DEPTH_2, 2, RWKV_COLS), 0.0, 0.5)
    rwkv_w0 = 0.5 * jax.random.normal(next(ks), (DEPTH_2, 2, RWKV_DIM), f32)
    rwkv_w_up = nrm((DEPTH_2, 2, RWKV_W_RANK, RWKV_DIM), RWKV_W_RANK, 0.5)
    rwkv_a0 = 0.1 * jax.random.normal(next(ks), (DEPTH_2, RWKV_DIM), f32)
    rwkv_a_up = nrm((DEPTH_2, RWKV_A_RANK, RWKV_DIM), RWKV_A_RANK, 0.1)
    rwkv_g_up = nrm((DEPTH_2, RWKV_G_RANK, RWKV_DIM), RWKV_G_RANK)
    rwkv_k_k = 0.85 + 0.05 * jax.random.normal(next(ks), (DEPTH_2, RWKV_DIM), f32)
    rwkv_k_a = gain((DEPTH_2, RWKV_DIM))
    rwkv_r_k = 0.1 * jax.random.normal(next(ks), (DEPTH_2, RWKV_DIM), f32)
    rwkv_ln_w = gain((DEPTH_2, RWKV_DIM))
    rwkv_ln_b = 0.02 * jax.random.normal(next(ks), (DEPTH_2, RWKV_DIM), f32)
    hgrn_lb_logits = 0.1 * jax.random.normal(next(ks), (DEPTH_2, HGRN_DIM), f32)
    hgrn_norm_w = gain((DEPTH_2, HGRN_DIM))
    w_branch_ssm = nrm((DEPTH_2, SSM_INNER, D_MODEL), SSM_INNER)
    w_branch_rwkv = nrm((DEPTH_2, RWKV_DIM, D_MODEL), RWKV_DIM)
    w_branch_hgrn = nrm((DEPTH_2, HGRN_DIM, D_MODEL), HGRN_DIM)
    w_out = nrm((DEPTH_2, D_MODEL, D_MODEL), D_MODEL)
    norm2_w = gain((DEPTH_2, D_MODEL))
    ffn_w_in = nrm((DEPTH_2, D_MODEL, 2 * D_FF), D_MODEL)
    ffn_w_down = nrm((DEPTH_2, D_FF, D_MODEL), D_FF)
    final_norm_w = gain((D_MODEL,))
    return {"x": x, "norm1_w": norm1_w, "w_in": w_in,
            "ssm_conv_w": ssm_conv_w, "ssm_conv_b": ssm_conv_b, "ssm_dt_bias": ssm_dt_bias,
            "ssm_a_log": ssm_a_log, "ssm_d": ssm_d, "ssm_norm_w": ssm_norm_w,
            "rwkv_mu": rwkv_mu, "rwkv_w0": rwkv_w0, "rwkv_w_up": rwkv_w_up, "rwkv_a0": rwkv_a0,
            "rwkv_a_up": rwkv_a_up, "rwkv_g_up": rwkv_g_up, "rwkv_k_k": rwkv_k_k,
            "rwkv_k_a": rwkv_k_a, "rwkv_r_k": rwkv_r_k, "rwkv_ln_w": rwkv_ln_w,
            "rwkv_ln_b": rwkv_ln_b, "hgrn_lb_logits": hgrn_lb_logits, "hgrn_norm_w": hgrn_norm_w,
            "w_branch_ssm": w_branch_ssm, "w_branch_rwkv": w_branch_rwkv,
            "w_branch_hgrn": w_branch_hgrn, "w_out": w_out, "norm2_w": norm2_w,
            "ffn_w_in": ffn_w_in, "ffn_w_down": ffn_w_down, "final_norm_w": final_norm_w}

def second_block(x, norm1_w, w_in, ssm_conv_w, ssm_conv_b, ssm_dt_bias, ssm_a_log, ssm_d,
              ssm_norm_w, rwkv_mu, rwkv_w0, rwkv_w_up, rwkv_a0, rwkv_a_up, rwkv_g_up,
              rwkv_k_k, rwkv_k_a, rwkv_r_k, rwkv_ln_w, rwkv_ln_b, hgrn_lb_logits, hgrn_norm_w,
              w_branch_ssm, w_branch_rwkv, w_branch_hgrn, w_out, norm2_w, ffn_w_in,
              ffn_w_down, final_norm_w):
    b, L, _ = x.shape
    lb_p = jax.nn.softmax(hgrn_lb_logits.astype(jnp.float32), axis=0)
    lower_bounds = (jnp.cumsum(lb_p, axis=0) - lb_p[0]).astype(x.dtype)
    in_splits = _split_points([SSM_INNER, SSM_CONV_DIM, 2 * SSM_HEADS, RWKV_COLS, HGRN_COLS,
                               GATE_COLS])
    for l in range(DEPTH_2):
        xn = rmsnorm(x, norm1_w[l])
        p = xn @ w_in[l]
        z, xbc, dt_raw, p_rwkv, p_hgrn, p_gate = jnp.split(p, in_splits, axis=-1)
        y_ssm = ssd_branch(z, xbc, dt_raw, ssm_conv_w[l], ssm_conv_b[l], ssm_dt_bias[l],
                           ssm_a_log[l], ssm_d[l], ssm_norm_w[l]) @ w_branch_ssm[l]
        y_rwkv = rwkv7_branch(p_rwkv, rwkv_mu[l], rwkv_w0[l], rwkv_w_up[l], rwkv_a0[l],
                              rwkv_a_up[l], rwkv_g_up[l], rwkv_k_k[l], rwkv_k_a[l],
                              rwkv_r_k[l], rwkv_ln_w[l], rwkv_ln_b[l]) @ w_branch_rwkv[l]
        y_hgrn = hgrn2_branch(p_hgrn, lower_bounds[l], hgrn_norm_w[l]) @ w_branch_hgrn[l]
        gates = jax.nn.sigmoid(p_gate).reshape(b, L, N_BRANCH, D_MODEL)
        mixed = gates[:, :, 0] * y_ssm + gates[:, :, 1] * y_rwkv + gates[:, :, 2] * y_hgrn
        x = x + mixed @ w_out[l]
        h_gate, h_up = jnp.split(rmsnorm(x, norm2_w[l]) @ ffn_w_in[l], 2, axis=-1)
        x = x + (jax.nn.silu(h_gate) * h_up) @ ffn_w_down[l]
    return rmsnorm(x, final_norm_w)


def setup_inputs(seed=0):
    out = dict(first_inputs(seed))
    for name, value in second_inputs(seed + 1).items():
        if name != "x":
            out[name + "_2"] = value
    return out


def reference(
    x, c, ctx, c_ctx, norm_g, ada_w, ada_b, dn_w_in, dn_conv_w, dn_a_log, dn_dt_bias,
    dn_o_norm_g, dn_w_out, att_w_in, att_q_norm_g, att_k_norm_g, att_w_out, final_norm_g,
    norm1_w_2, w_in_2, ssm_conv_w_2, ssm_conv_b_2, ssm_dt_bias_2, ssm_a_log_2, ssm_d_2,
    ssm_norm_w_2, rwkv_mu_2, rwkv_w0_2, rwkv_w_up_2, rwkv_a0_2, rwkv_a_up_2, rwkv_g_up_2,
    rwkv_k_k_2, rwkv_k_a_2, rwkv_r_k_2, rwkv_ln_w_2, rwkv_ln_b_2, hgrn_lb_logits_2,
    hgrn_norm_w_2, w_branch_ssm_2, w_branch_rwkv_2, w_branch_hgrn_2, w_out_2, norm2_w_2,
    ffn_w_in_2, ffn_w_down_2, final_norm_w_2,
):
    x = first_block(
        x, c, ctx, c_ctx, norm_g, ada_w, ada_b, dn_w_in, dn_conv_w, dn_a_log, dn_dt_bias,
        dn_o_norm_g, dn_w_out, att_w_in, att_q_norm_g, att_k_norm_g, att_w_out, final_norm_g,
    )
    return second_block(
        x, norm1_w_2, w_in_2, ssm_conv_w_2, ssm_conv_b_2, ssm_dt_bias_2, ssm_a_log_2, ssm_d_2,
        ssm_norm_w_2, rwkv_mu_2, rwkv_w0_2, rwkv_w_up_2, rwkv_a0_2, rwkv_a_up_2, rwkv_g_up_2,
        rwkv_k_k_2, rwkv_k_a_2, rwkv_r_k_2, rwkv_ln_w_2, rwkv_ln_b_2, hgrn_lb_logits_2,
        hgrn_norm_w_2, w_branch_ssm_2, w_branch_rwkv_2, w_branch_hgrn_2, w_out_2, norm2_w_2,
        ffn_w_in_2, ffn_w_down_2, final_norm_w_2,
    )


_drawn_inputs = setup_inputs


def setup_inputs(seed=0):
    import zlib

    import numpy as np

    out = dict(_drawn_inputs(seed))
    spreads = {}
    factors = {'norm_g': 6.199,
     'dn_o_norm_g': 8.0,
     'att_q_norm_g': 8.0,
     'att_k_norm_g': 8.0,
     'ssm_conv_b_2': 3.872,
     'ssm_d_2': 25.423,
     'rwkv_w_up_2': 3.593,
     'rwkv_a0_2': 3.328,
     'rwkv_a_up_2': 5.298,
     'rwkv_k_k_2': 101.581,
     'rwkv_k_a_2': 2.794,
     'rwkv_ln_w_2': 4.522,
     'rwkv_ln_b_2': 22.853,
     'hgrn_norm_w_2': 3.966,
     'ssm_norm_w_2': 4.314,
     'norm2_w_2': 2.899}
    for name, (base, spread) in spreads.items():
        noise = np.random.default_rng([zlib.crc32(name.encode()), seed]).standard_normal(out[name].shape)
        drawn = base * np.exp(spread * noise) if base else spread * noise
        out[name] = __import__('jax').numpy.asarray(drawn.astype(out[name].dtype))
    for name, factor in factors.items():
        out[name] = (out[name] * factor).astype(out[name].dtype)
    return out
```

```python
import math
from contextlib import ExitStack, contextmanager

import numpy as np

import concourse.bass as bass
from concourse import mybir

F32 = mybir.dt.float32
ALU = mybir.AluOpType
ACT = mybir.ActivationFunctionType
AX = mybir.AxisListType

P = 128
D = 1024
KT = D // P
CTX = 256
SEQ = 256
TOK = CTX + SEQ
TT = TOK // P
CHUNK = 1024
SLOTS = 6
EPS = 1e-6
LEVELS = 7

QK_HEADS = 8
V_HEADS = 16
DN_GROUP = 6
ATT_Q = 8
ATT_KV = 2

NEG = -1e30


def level_mask(b):
    i = np.arange(P)
    return ((i[:, None] // b) % 2 == 1) & (i[None, :] // b == i[:, None] // b - 1)


def const_tiles():
    i = np.arange(P)
    s, t = i[:, None], i[None, :]
    half = s // 64 == t // 64
    out = {"ident": s == t, "ones": np.ones((P, P)), "mhalf": np.full((P, P), -0.5), "tri_f": s <= t, "tri_b": s >= t}
    for n in range(LEVELS):
        out[f"lev_f{n}"] = level_mask(2 ** n)
    for n in range(LEVELS):
        out[f"lev_b{n}"] = level_mask(2 ** n).T
    out["neg_f"] = np.where(s <= t, 0.0, NEG)
    out["neg_b"] = np.where(s >= t, 0.0, NEG)
    rot = np.zeros((P, P))
    for f in range(P):
        if f % 64 < 32:
            rot[f + 32, f] = -1.0
        else:
            rot[f - 32, f] = 1.0
    out["rot"] = rot
    return out


def second_tiles():
    i = np.arange(P)
    s, t = i[:, None], i[None, :]
    half = s // 64 == t // 64
    zero, nega, ones = np.zeros((P, P)), np.full((P, P), NEG), np.ones((P, P))
    first = const_tiles()
    out = {n: first[n] for n in ("ident", "ones", "mhalf", "tri_f", "tri_b")}
    for d in "bf":
        for n in range(LEVELS):
            out[f"lev_{d}{n}"] = first[f"lev_{d}{n}"]
    for n, m in enumerate((first["neg_f"], zero, nega, first["neg_f"], first["neg_b"], nega, zero, first["neg_b"])):
        out[f"ssd_neg{n}"] = m
    for n, m in enumerate((s <= t, ones, zero, s <= t, s >= t, zero, ones, s >= t)):
        out[f"ssd_sum{n}"] = m
    for n, m in enumerate((s < t, s <= t, s < t, s <= t, s > t, s >= t, s > t, s >= t)):
        out[f"rw{n}"] = half & m
    out["half"] = half
    out["halves"] = (t < 2) & (s // 64 == t)
    for n in range(LEVELS):
        b = 2 ** n
        odd = (t // b) % 2 == 1
        out[f"hg_f{n}"] = (s // b == t // b) & np.where(odd, s <= t, s > t)
    for n in range(LEVELS):
        out[f"hg_b{n}"] = out[f"hg_f{n}"][::-1, ::-1]
    out["aft"] = s > t
    out["bef"] = s < t
    return out


N_BASE = 5 + 2 * LEVELS
FF = 22

CONST_NAMES = list(const_tiles())
SECOND_NAMES = list(second_tiles())


def const_array(tiles):
    return np.concatenate([np.asarray(m, np.float32) for m in tiles.values()], axis=1)


def rope_tables():
    pos = np.arange(SEQ)
    inv = 10000.0 ** (-np.arange(0, 64, 2, dtype=np.float32) / np.float32(64))
    ang = np.zeros((P, SEQ), np.float32)
    for f in range(P):
        where = (pos // 64) if f < 64 else (pos % 64)
        ang[f] = where.astype(np.float32) * inv[f % 32]
    return np.concatenate([np.cos(ang), np.sin(ang)], axis=1).astype(np.float32)


class Chain:

    def __init__(self, eng, sem):
        self.eng, self.sem, self.n = eng, sem, {}

    def __call__(self, ins, event=None):
        event = event or self.sem
        ins.then_inc(event, 1)
        self.n[event.num] = self.n.get(event.num, 0) + 1
        self.eng.wait_ge(event, self.n[event.num])


def inverse_root(nc, pool, C, x, ready, done, n=1):
    pool.wait_ge(ready, n)
    nc.gpsimd.tensor_tensor(x, x, C("mhalf")[:, 0:1].to_broadcast(list(x.shape)), ALU.pow).then_inc(done, 1)
    pool.wait_ge(done, n)


def column_sums(nc, C, out, x, n):
    for i in range(n):
        last = nc.tensor.matmul(out[:, i:i + 1], x[:, P * i:P * i + P], C("ones")[:, 0:1], start=True, stop=True)
    return last


def spread(nc, C, out, cols, n):
    for i in range(n):
        last = nc.tensor.matmul(out[:, P * i:P * i + P], cols[:, i:i + 1].to_broadcast([P, P]), C("ident"),
                                start=True, stop=True)
    return last


@contextmanager
def stage(nc, names):
    with ExitStack() as es:
        s = {n: es.enter_context(nc.semaphore(n)) for n in (names + " act_own dve_own pool_own").split()}
        with nc.Block() as block:
            yield s, block
        for n in s:
            nc.sync.sem_clear(s[n])
        nc.all_engine_barrier()


class Stream:

    def __init__(self, nc, w, sbuf, sems):
        self.nc, self.w, self.sbuf, self.sems = nc, w, sbuf, sems
        self.at, self.set, self.ready = 0, 0, 0

    def slot(self, c):
        return self.sbuf[:, self.set, c, :]

    def loaded(self, c):
        return self.sems[self.set][c]

    def load(self, sp, which, c, index):
        src = self.w[bass.ds(index, 1)].rearrange("a p n -> p (a n)")
        sp.dma_start(self.sbuf[:, which, c, :], src).then_inc(self.sems[which][c], 16)

    def begin(self, per_body):
        sp = self.nc.sync
        for c in range(per_body, self.ready):
            sp.wait_ge(self.sems[self.set][c], 16)
            sp.sem_clear(self.sems[self.set][c])
        self.nc.all_engine_barrier()
        for c in range(self.ready, per_body):
            self.load(sp, self.set, c, self.at + c)
        self.ready = per_body

    def ahead(self, sp, n, offset):
        for c in range(n):
            self.load(sp, 1 - self.set, c, offset + self.at + n + c)

    def turn(self, n):
        for c in range(n):
            self.nc.sync.sem_clear(self.sems[self.set][c])
        self.set = 1 - self.set

    def drain(self):
        for c in range(self.ready):
            self.nc.sync.wait_ge(self.sems[self.set][c], 16)
            self.nc.sync.sem_clear(self.sems[self.set][c])
        self.nc.all_engine_barrier()

    def bodies(self, count, per_body, body):
        self.begin(per_body)
        pairs = count // 2 if count >= 4 else 0
        if pairs:
            with self.nc.Fori(0, pairs) as i:
                for half in range(2):
                    body(i * 2 + half, (i * 2 + half) * per_body)
                    self.turn(per_body)
        for n in range(2 * pairs, count):
            body(n, n * per_body)
            self.turn(per_body)
        self.at += count * per_body


def accumulate(nc, out, lhs, rhs):
    n = len(lhs)
    for k in range(n):
        last = nc.tensor.matmul(out, lhs[k], rhs[k], start=(k == 0), stop=(k == n - 1))
    return last


def modulation(nc, st, bank, C, layer, silu_c, rows, mod, bias_cols):

    def body(n, offset):
        with stage(nc, "summed rows_out turned") as (s, block):
            @block.sync
            def _(sp):
                st.ahead(sp, 4, offset)

            @block.tensor
            def _(pe):
                for k in range(KT):
                    if k % 2 == 0:
                        pe.wait_ge(st.loaded(k // 2), 16)
                    at = 512 * (k % 2)
                    mm = nc.tensor.matmul(bank[0][0:2, :], silu_c[:, k, :], st.slot(k // 2)[:, at:at + 512],
                                          start=(k == 0), stop=(k == KT - 1))
                mm.then_inc(s["summed"], 1)
                pe.wait_ge(s["rows_out"], 1)
                for j in range(4):
                    mm = nc.tensor.matmul(bank[1][:, 2 * j:2 * j + 2], rows[:, P * j:P * j + P], C("ident")[0:2, 0:2],
                                          start=(j == 0), stop=(j == 3), skip_group_check=True)
                mm.then_inc(s["turned"], 1)

            @block.vector
            def _(dve):
                link = Chain(dve, s["dve_own"])
                dve.wait_ge(s["summed"], 1)
                link(nc.vector.tensor_copy(rows[:, :], bank[0][0:2, :]), s["rows_out"])
                dve.wait_ge(s["turned"], 1)
                link(nc.vector.tensor_tensor(mod[:, bass.ds(n * 4, 4), :], bank[1][:, 0:8].rearrange("p (j c) -> p j c", c=2),
                                             bias_cols(n).unsqueeze(2).to_broadcast([P, 4, 2]), ALU.add))

    st.bodies(6, 4, body)


def feature_norm(nc, bank, C, h, u, g_cols, mod, streams, sq, rs, gs):
    lo, n = streams[0][0], sum(x[1] for x in streams)
    tiles = n // P
    with stage(nc, "squared summed mean root spread") as (s, block):
        @block.gpsimd
        def _(pool):
            inverse_root(nc, pool, C, rs[:, 0:tiles], s["mean"], s["root"])

        @block.scalar
        def _(act):
            for k in range(KT):
                nc.scalar.activation(sq[:, k, 0:n], h[:, k, lo:lo + n], ACT.Square).then_inc(s["squared"], 1)

        @block.tensor
        def _(pe):
            for t in range(tiles):
                for k in range(KT):
                    if t == 0:
                        pe.wait_ge(s["squared"], k + 1)
                    mm = nc.tensor.matmul(bank[0][:, t:t + 1], sq[:, k, P * t:P * t + P], C("ones")[:, 0:1],
                                          start=(k == 0), stop=(k == KT - 1))
            mm.then_inc(s["summed"], 1)
            pe.wait_ge(s["root"], 1)
            spread(nc, C, bank[1], rs, tiles).then_inc(s["spread"], 1)

        @block.vector
        def _(dve):
            link = Chain(dve, s["dve_own"])
            if mod is not None:
                for _, _, m in streams:
                    link(nc.vector.tensor_scalar(gs[:, :, m], mod[:, 8:16, m], 1.0, None, ALU.add))
                    link(nc.vector.tensor_tensor(gs[:, :, m], gs[:, :, m], g_cols, ALU.mult))
            dve.wait_ge(s["summed"], 1)
            link(nc.vector.tensor_scalar(rs[:, 0:tiles], bank[0][:, 0:tiles], 1.0 / D, EPS, ALU.mult, ALU.add), s["mean"])
            dve.wait_ge(s["spread"], 1)
            for k in range(KT):
                for t0, tn, m in streams:
                    scale = gs[:, k, m:m + 1] if mod is not None else g_cols[:, k:k + 1]
                    link(nc.vector.scalar_tensor_tensor(u[:, k, t0:t0 + tn], h[:, k, t0:t0 + tn], scale,
                                                        bank[1][:, t0 - lo:t0 - lo + tn], ALU.mult, ALU.mult))
                    if mod is not None:
                        link(nc.vector.tensor_scalar(u[:, k, t0:t0 + tn], u[:, k, t0:t0 + tn], mod[:, k, m:m + 1],
                                                     None, ALU.add))


def linear(nc, st, bank, count, per_body, src, n_tok, evacuate, k_tiles=KT):
    held = k_tiles if k_tiles < 8 else -(-k_tiles // 8) * 8
    tiles = per_body * 8 // held

    def body(n, offset):
        with stage(nc, "summed evacuated") as (s, block):
            @block.sync
            def _(sp):
                st.ahead(sp, per_body, offset)

            @block.tensor
            def _(pe):
                blocks = 0
                for m in range(tiles):
                    if m >= 4:
                        pe.wait_ge(s["evacuated"], m - 3)
                    for k in range(k_tiles):
                        c, b = blocks // 8, blocks % 8
                        if b == 0:
                            pe.wait_ge(st.loaded(c), 16)
                        mm = nc.tensor.matmul(bank[m % 4][:, 0:n_tok], st.slot(c)[:, P * b:P * b + P], src(k),
                                              start=(k == 0), stop=(k == k_tiles - 1))
                        blocks += 1
                    blocks = (m + 1) * held
                    mm.then_inc(s["summed"], 1)

            @block.vector
            def _(dve):
                for m in range(tiles):
                    dve.wait_ge(s["summed"], m + 1)
                    evacuate(n * tiles + m, bank[m % 4]).then_inc(s["evacuated"], 1)
                dve.wait_ge(s["evacuated"], tiles)

    st.bodies(count, per_body, body)


G, NGC, BETA, NEG_EG, EG, BEND, GL = range(7)
QUANT = 7
PER_HEAD = QUANT * 4 * TT


def delta_gates(nc, bank, C, u, w_ab, dt_rows, a_rows, sc, tmp):
    x, e, r, lg, gx = (tmp[:, i, :] for i in range(5))
    q3 = lambda a: a.rearrange("p (t c) -> p t c", t=TT)

    def put(q, src, direction):
        out = sc[:, :, :].rearrange("p h (q j d t) -> p h q j d t", q=QUANT, j=2, d=2)[:, :, q, :, direction, :]
        inp = src.rearrange("p (t d h j) -> p d h j t", t=TT, d=2, j=2)[:, direction]
        return nc.vector.tensor_copy(out, inp)

    with stage(nc, "ab x_ready e_ready ln_ready g_ready sums ex th_ready a_ready done") as (s, block):
        @block.tensor
        def _(pe):
            for t in range(TT):
                for k in range(KT):
                    mm = nc.tensor.matmul(bank[0][:, 64 * t:64 * t + 64], u[:, k, P * t:P * t + P], w_ab[:, k, :],
                                          start=(t == 0 and k == 0), stop=(k == KT - 1), skip_group_check=True)
            mm.then_inc(s["ab"], 1)
            pe.wait_ge(s["g_ready"], 1)
            for t in range(TT):
                for d in range(2):
                    col = 32 * t + 16 * d
                    nc.tensor.matmul(bank[1][:, col:col + 16], C("tri_b" if d else "tri_f"), lg[:, col:col + 16],
                                     start=(col == 0), stop=True, skip_group_check=True)
            mm = nc.tensor.matmul(bank[2][:, 0:128], C("ones"), lg, start=True, stop=True)
            mm.then_inc(s["sums"], 1)

        ab = bank[0][:, 0:256].rearrange("p (t b c) -> p t b c", t=TT, b=2)

        @block.scalar
        def _(act):
            link = Chain(act, s["act_own"])
            act.wait_ge(s["ab"], 1)
            link(nc.scalar.activation(q3(r), ab[:, :, 0, :], ACT.Tanh, scale=0.5), s["th_ready"])
            link(nc.scalar.activation(a_rows, a_rows, ACT.Exp), s["a_ready"])
            act.wait_ge(s["x_ready"], 1)
            link(nc.scalar.activation(e, gx, ACT.Exp), s["e_ready"])
            act.wait_ge(s["x_ready"], 2)
            link(nc.scalar.activation(gx, lg, ACT.Ln), s["ln_ready"])
            act.wait_ge(s["ex"], 1)
            link(nc.scalar.activation(e, bank[1][:, 0:128], ACT.Exp), s["e_ready"])
            link(nc.scalar.activation(x, gx, ACT.Exp), s["e_ready"])
            link(nc.scalar.activation(gx, bank[2][:, 0:128], ACT.Exp), s["e_ready"])

        @block.vector
        def _(dve):
            link = Chain(dve, s["dve_own"])
            dve.wait_ge(s["th_ready"], 1)
            link(nc.vector.tensor_tensor(q3(x), ab[:, :, 1, :], dt_rows.unsqueeze(1).to_broadcast([P, TT, 32]), ALU.add))
            link(nc.vector.scalar_tensor_tensor(gx, x, -1.0, x, ALU.mult, ALU.min), s["x_ready"])
            dve.wait_ge(s["e_ready"], 1)
            link(nc.vector.tensor_scalar(lg, e, 1.0, None, ALU.add), s["x_ready"])
            dve.wait_ge(s["ln_ready"], 1)
            link(nc.vector.tensor_scalar(lg, lg, -1.0, 1.0, ALU.mult, ALU.add))
            link(nc.vector.tensor_tensor(lg, lg, e, ALU.add))
            link(nc.vector.tensor_tensor(lg, lg, gx, ALU.add))
            link(nc.vector.scalar_tensor_tensor(lg, x, 0.0, lg, ALU.max, ALU.add))
            dve.wait_ge(s["a_ready"], 1)
            link(nc.vector.scalar_tensor_tensor(q3(lg), q3(lg), -1.0, a_rows.unsqueeze(1).to_broadcast([P, TT, 32]),
                                                ALU.mult, ALU.mult), s["g_ready"])
            link(nc.vector.tensor_scalar(r, r, 0.5, 0.5, ALU.mult, ALU.add))
            dve.wait_ge(s["sums"], 1)
            for d in range(2):
                link(put(G, lg, d))
                link(put(BETA, r, d))
            link(nc.vector.tensor_scalar(lg, bank[1][:, 0:128], -1.0, None, ALU.mult))
            for d in range(2):
                link(put(NGC, lg, d))
            link(nc.vector.tensor_tensor(gx, lg, bank[2][:, 0:128], ALU.add), s["ex"])
            dve.wait_ge(s["e_ready"], 4)
            for d in range(2):
                link(put(EG, e, d))
                link(put(GL, gx, d))
            link(nc.vector.tensor_scalar(e, e, -1.0, None, ALU.mult))
            link(nc.vector.tensor_tensor(x, x, r, ALU.mult))
            for d in range(2):
                link(put(NEG_EG, e, d))
                link(put(BEND, x, d))


def delta_heads(nc, st, bank, C, u, sc, conv_cols, o_cols, gated, spare):
    order = ((0, 1, 2, 3), (1, 0, 3, 2))
    with ExitStack() as es:
        sb = lambda name, shape: es.enter_context(nc.sbuf_tensor(name, shape, F32))
        raw = sb("raw", [P, 4, 2, SEQ + 4])
        acc = sb("acc", [P, 4, TOK])
        y = sb("y", [P, 4, TOK])
        zs = sb("zs", [P, 2, TOK])
        zt = sb("zt", [P, 2, TOK])
        rn = sb("rn", [P, 2, TOK])
        qn = sb("qn", [P, TOK])
        kn = sb("kn", [P, TOK])
        v_t = sb("v_t", [P, TT, 2, P])
        k_t = sb("k_t", [P, TT, P])
        gram = sb("gram", [P, TOK])
        kq = sb("kq", [P, TOK])
        dec = sb("dec", [P, 2, TOK])
        a_t = sb("a_t", [P, 4, TOK])
        qkd = spare[:, 4:8, :]
        inv = acc
        inv_t = sb("inv_t", [P, 4, TOK])
        prod = y
        hs = sb("hs", [P, PER_HEAD])
        hc = sb("hc", [P, 20])
        state = sb("state", [P, 2, 2 * P])
        resid = rn[:, 0, :].rearrange("p (d e) -> p d e", d=2)
        vn = sb("vn", [P, 2, 2 * P])
        ve = sb("ve", [P, 2, 2 * P])
        qs = rn[:, 1, :].rearrange("p (d e) -> p d e", d=2)
        od = spare[:, 0:4, :].rearrange("p (d a) t -> p d (a t)", d=2).rearrange("p d (t e) -> p d t e", t=TT)
        ms = sb("ms", [P, 2 * TT])
        rc = sb("rc", [P, 2 * TT])
        th = y
        sq = od[:, 0, :, :].rearrange("p t e -> p (t e)")
        o_sq = acc[:, 0:2, :].rearrange("p a e -> p (a e)")

        def col(q, c, t):
            at = q * 4 * TT + c * TT + t
            return hs[:, at:at + 1]

        def tile(a, t):
            return a[:, P * t:P * t + P]

        four = lambda a: a.rearrange("p (t e) -> p t e", t=TT)
        wide = lambda name: C(name).unsqueeze(1).to_broadcast([P, TT, P])

        with stage(nc, "padded") as (s, block):
            @block.gpsimd
            def _(pool):
                nc.gpsimd.memset(raw[:, :, :, :], 0.0).then_inc(s["padded"], 1)
                pool.wait_ge(s["padded"], 1)

        def body(n, offset):
            names = ("proj raw_out conv tanh silu squared ssum kq_norm turned turned_out grams kq_done scal "
                     "rows dec_ready dec_used a_done p_ready bc_done t_ready zero ks_done qs_done r_ready "
                     "qs_out x_done vn_ready os_done s_ready o_sum o_sqd o_norm o_turned z_ready z_raw mean root spread o_mean o_root")
            with stage(nc, names) as (s, block):
                @block.sync
                def _(sp):
                    st.ahead(sp, DN_GROUP, offset)

                @block.gpsimd
                def _(pool):
                    link = Chain(pool, s["pool_own"])
                    link(nc.gpsimd.memset(state[:, :, :], 0.0), s["zero"])
                    inverse_root(nc, pool, C, rc[:, :], s["mean"], s["root"])
                    for j in range(2):
                        pool.wait_ge(s["z_raw"], j + 1)
                        link(nc.gpsimd.tensor_tensor(zt[:, j, :], zt[:, j, :], zs[:, j, :], ALU.mult))
                        link(nc.gpsimd.tensor_tensor(zs[:, j, :], zs[:, j, :], zt[:, j, :], ALU.add), s["z_ready"])
                    inverse_root(nc, pool, C, ms[:, :], s["o_mean"], s["o_root"])

                @block.tensor
                def _(pe):
                    for m in range(DN_GROUP):
                        pe.wait_ge(st.loaded(m), 16)
                        if m >= 2:
                            pe.wait_ge(s["raw_out"], m - 1)
                        accumulate(nc, bank[m % 2][:, :], [st.slot(m)[:, P * k:P * k + P] for k in range(KT)],
                                   [u[:, k, :] for k in range(KT)]).then_inc(s["proj"], 1)
                    pe.wait_ge(s["squared"], 2)
                    column_sums(nc, C, bank[2], sq, 2 * TT).then_inc(s["ssum"], 1)
                    for j in range(2):
                        pe.wait_ge(s["silu"], 3 + j)
                        for t in range(TT):
                            mm = nc.tensor.transpose(tile(bank[4 + j], t), tile(y[:, 2 + j, :], t), C("ident"))
                        mm.then_inc(s["turned"], 1)
                    pe.wait_ge(s["root"], 1)
                    for m in range(2):
                        spread(nc, C, bank[2 + m], rc[:, TT * m:TT * m + TT], TT).then_inc(s["spread"], 1)
                    pe.wait_ge(s["kq_norm"], 1)
                    for t in range(TT):
                        mm = nc.tensor.transpose(tile(bank[6], t), tile(kn, t), C("ident"))
                    mm.then_inc(s["turned"], 1)
                    for t in range(TT):
                        mm = nc.tensor.matmul(tile(bank[7], t), tile(kn, t), tile(kn, t), start=True, stop=True)
                    mm.then_inc(s["grams"], 1)
                    pe.wait_ge(s["kq_norm"], 2)
                    for t in range(TT):
                        mm = nc.tensor.matmul(tile(bank[2], t), tile(kn, t), tile(qn, t), start=True, stop=True)
                    mm.then_inc(s["grams"], 1)
                    for c in range(4):
                        d = c % 2
                        if c >= 2:
                            pe.wait_ge(s["dec_ready"], c - 1)
                        else:
                            pe.wait_ge(s["turned_out"], 1)
                            pe.wait_ge(s["scal"], 1)
                        b = bank[3 + d]
                        nc.tensor.matmul(four(b[:, :]), C("ident"), wide("neg_b" if d else "neg_f"),
                                         start=True, stop=False, skip_group_check=True)
                        for t in range(TT):
                            mm = nc.tensor.matmul(tile(b, t), col(G, c, t).to_broadcast([P, P]),
                                                  C("tri_b" if d else "tri_f"), start=False, stop=True,
                                                  skip_group_check=True)
                        mm.then_inc(s["rows"], 1)
                    for lv in range(LEVELS):
                        for c in range(4):
                            q = 4 * lv + c
                            if lv == 0:
                                pe.wait_ge(s["dec_used"], c + 1)
                                pe.wait_ge(s["z_raw"], 2)
                                pe.wait_ge(s["kq_done"], 2)
                                pe.wait_ge(s["dec_ready"], 4)
                            else:
                                pe.wait_ge(s["t_ready"], q - 3)
                            for t in range(TT):
                                rhs = C("ident") if lv == 0 else tile(inv[:, c, :], t)
                                mm = nc.tensor.matmul(tile(bank[c], t), tile(a_t[:, c, :], t), rhs, start=True, stop=True)
                            mm.then_inc(s["a_done"], 1)
                        for c in range(4):
                            q = 4 * lv + c
                            pe.wait_ge(s["p_ready"], q + 1)
                            if q >= 2:
                                pe.wait_ge(s["t_ready"], q - 1)
                            elif q == 0:
                                pe.wait_ge(s["turned_out"], 3)
                            if 0 < lv < LEVELS - 1:
                                for t in range(TT):
                                    nc.tensor.matmul(tile(bank[4 + c % 2], t), tile(inv_t[:, c, :], t),
                                                     tile(prod[:, c, :], t), start=True, stop=True)
                            for t in range(TT):
                                rhs = C("ident") if lv == 0 else tile(inv_t[:, c, :], t)
                                mm = nc.tensor.matmul(tile(bank[6 + c % 2], t), tile(prod[:, c, :], t), rhs,
                                                      start=True, stop=True)
                            mm.then_inc(s["bc_done"], 1)
                    pe.wait_ge(s["t_ready"], 4 * LEVELS)
                    for step in range(TT):
                        for d in range(2):
                            r, t = 2 * step + d, order[d][step]
                            if step == 0:
                                pe.wait_ge(s["zero"], 1)
                            else:
                                pe.wait_ge(s["s_ready"], r - 1)
                                pe.wait_ge(s["qs_out"], r - 1)
                            nc.tensor.matmul(bank[d][:, 0:2 * P], tile(kn, t), state[:, d, :],
                                             start=True, stop=True).then_inc(s["ks_done"], 1)
                            nc.tensor.matmul(bank[2 + d][:, 0:2 * P], tile(qn, t), state[:, d, :],
                                             start=True, stop=True).then_inc(s["qs_done"], 1)
                        for d in range(2):
                            r, t = 2 * step + d, order[d][step]
                            pe.wait_ge(s["r_ready"], r + 1)
                            for j in range(2):
                                mm = nc.tensor.matmul(tile(bank[4 + d], j), tile(inv_t[:, 2 * j + d, :], t),
                                                      tile(resid[:, d, :], j), start=True, stop=True)
                            mm.then_inc(s["x_done"], 1)
                        for d in range(2):
                            r, t = 2 * step + d, order[d][step]
                            pe.wait_ge(s["vn_ready"], r + 1)
                            for j in range(2):
                                nc.tensor.matmul(tile(bank[6 + d], j), tile(qkd[:, 2 * j + d, :], t),
                                                 tile(vn[:, d, :], j), start=True, stop=True)
                            nc.tensor.matmul(bank[6 + d][:, 2 * P:4 * P], k_t[:, t, :], ve[:, d, :],
                                             start=True, stop=True).then_inc(s["os_done"], 1)
                    pe.wait_ge(s["o_norm"], 1)
                    for j in range(2):
                        for t in range(TT):
                            mm = nc.tensor.transpose(tile(bank[j], t), od[:, 0, t, P * j:P * j + P], C("ident"))
                        mm.then_inc(s["o_turned"], 1)

                @block.scalar
                def _(act):
                    link = Chain(act, s["act_own"])

                    def keep(m):
                        act.wait_ge(s["proj"], m + 1)
                        link(nc.scalar.activation(raw[:, m, :, 2:SEQ + 2], bank[m % 2][:, :].rearrange("p (a t) -> p a t", a=2),
                                                  ACT.Copy), s["raw_out"])

                    def tanh(m):
                        act.wait_ge(s["conv"], m + 1)
                        link(nc.scalar.activation(th[:, m, :], acc[:, m, :], ACT.Tanh, scale=0.5), s["tanh"])

                    def square(m):
                        act.wait_ge(s["silu"], m + 1)
                        link(nc.scalar.activation(sq[:, TOK * m:TOK * m + TOK], y[:, m, :], ACT.Square), s["squared"])

                    def gate(j):
                        act.wait_ge(s["proj"], 5 + j)
                        link(nc.scalar.activation(zs[:, j, :], bank[j][:, :], ACT.Copy))
                        link(nc.scalar.activation(zt[:, j, :], bank[j][:, :], ACT.Tanh, scale=0.5), s["z_raw"])

                    keep(0)
                    keep(1)
                    tanh(0)
                    keep(2)
                    tanh(1)
                    square(0)
                    keep(3)
                    square(1)
                    tanh(2)
                    gate(0)
                    tanh(3)
                    gate(1)
                    for j in range(2):
                        act.wait_ge(s["turned"], j + 1)
                        link(nc.scalar.activation(v_t[:, :, j, :], four(bank[4 + j][:, :]), ACT.Copy, scale=0.5), s["turned_out"])
                    act.wait_ge(s["turned"], 3)
                    link(nc.scalar.activation(k_t[:, :, :], four(bank[6][:, :]), ACT.Copy), s["turned_out"])
                    act.wait_ge(s["grams"], 1)
                    link(nc.scalar.activation(gram[:, :], bank[7][:, :], ACT.Copy), s["kq_done"])
                    act.wait_ge(s["grams"], 2)
                    link(nc.scalar.activation(kq[:, :], bank[2][:, :], ACT.Copy), s["kq_done"])
                    for c in range(4):
                        act.wait_ge(s["rows"], c + 1)
                        if c >= 2:
                            act.wait_ge(s["dec_used"], c - 1)
                        for t in range(TT):
                            link(nc.scalar.activation(tile(dec[:, c % 2, :], t), tile(bank[3 + c % 2], t), ACT.Exp,
                                                      bias=col(NGC, c, t)), s["dec_ready"] if t == TT - 1 else None)
                    for step in range(TT):
                        for d in range(2):
                            r, t = 2 * step + d, order[d][step]
                            act.wait_ge(s["qs_done"], r + 1)
                            for j in range(2):
                                link(nc.scalar.activation(tile(qs[:, d, :], j), tile(bank[2 + d], j), ACT.Copy,
                                                          scale=col(EG, 2 * j + d, t)), s["qs_out"] if j else None)
                        for d in range(2):
                            r, t = 2 * step + d, order[d][step]
                            act.wait_ge(s["x_done"], r + 1)
                            for j in range(2):
                                link(nc.scalar.activation(tile(vn[:, d, :], j), tile(bank[4 + d], j), ACT.Copy,
                                                          scale=col(BETA, 2 * j + d, t)))
                                link(nc.scalar.activation(tile(ve[:, d, :], j), tile(bank[4 + d], j), ACT.Copy,
                                                          scale=col(BEND, 2 * j + d, t)), s["vn_ready"] if j else None)
                    act.wait_ge(s["o_sum"], 1)
                    link(nc.scalar.activation(o_sq, od[:, 0, :, :].rearrange("p t e -> p (t e)"), ACT.Square), s["o_sqd"])

                @block.vector
                def _(dve):
                    link = Chain(dve, s["dve_own"])
                    link(nc.vector.tensor_copy(hs[:, :], sc[:, bass.ds(n, 1), :].rearrange("p a c -> p (a c)")), s["scal"])
                    link(nc.vector.tensor_copy(hc[:, :], conv_cols[:, bass.ds(n * 20, 20)]))

                    def conv(m):
                        dve.wait_ge(s["raw_out"], m + 1)
                        out = acc[:, m, :].rearrange("p (a t) -> p a t", a=2)
                        link(nc.vector.tensor_scalar(out, raw[:, m, :, 0:SEQ], hc[:, 5 * m:5 * m + 1], None, ALU.mult))
                        for i in range(1, 5):
                            link(nc.vector.scalar_tensor_tensor(out, raw[:, m, :, i:i + SEQ], hc[:, 5 * m + i:5 * m + i + 1],
                                                                out, ALU.mult, ALU.add), s["conv"] if i == 4 else None)

                    def silu(m):
                        dve.wait_ge(s["tanh"], m + 1)
                        link(nc.vector.scalar_tensor_tensor(y[:, m, :], th[:, m, :], 1.0, acc[:, m, :], ALU.add, ALU.mult),
                             s["silu"])

                    def scale(m, out, factor):
                        dve.wait_ge(s["spread"], m + 1)
                        link(nc.vector.scalar_tensor_tensor(out[:, :], y[:, m, :], factor, bank[2 + m][:, :], ALU.mult, ALU.mult),
                             s["kq_norm"])

                    conv(0)
                    conv(1)
                    silu(0)
                    conv(2)
                    silu(1)
                    conv(3)
                    silu(2)
                    silu(3)
                    dve.wait_ge(s["ssum"], 1)
                    link(nc.vector.tensor_scalar(rc[:, :], bank[2][:, 0:2 * TT], 4 * EPS, None, ALU.add), s["mean"])
                    scale(0, kn, 1.0)
                    scale(1, qn, P ** -0.5)
                    for c in range(4):
                        if c == 0:
                            dve.wait_ge(s["kq_done"], 2)
                        dve.wait_ge(s["dec_ready"], c + 1)
                        for t in range(TT):
                            link(nc.vector.scalar_tensor_tensor(tile(a_t[:, c, :], t), tile(gram, t), col(BETA, c, t),
                                                                tile(dec[:, c % 2, :], t), ALU.mult, ALU.mult))
                        link(nc.vector.tensor_tensor(qkd[:, c, :], kq[:, :], dec[:, c % 2, :], ALU.mult), s["dec_used"])
                    for lv in range(LEVELS):
                        for c in range(4):
                            dve.wait_ge(s["a_done"], 4 * lv + c + 1)
                            link(nc.vector.tensor_tensor(four(prod[:, c, :]), four(bank[c][:, :]),
                                                         wide(f"lev_{'fb'[c % 2]}{lv}"), ALU.mult), s["p_ready"])
                        for c in range(4):
                            dve.wait_ge(s["bc_done"], 4 * lv + c + 1)
                            if lv == 0:
                                link(nc.vector.tensor_tensor(four(inv[:, c, :]), wide("ident"), four(prod[:, c, :]), ALU.subtract))
                            elif lv < LEVELS - 1:
                                link(nc.vector.tensor_tensor(inv[:, c, :], inv[:, c, :], bank[4 + c % 2][:, :], ALU.subtract))
                            link(nc.vector.tensor_tensor(four(inv_t[:, c, :]), wide("ident") if lv == 0 else four(inv_t[:, c, :]),
                                                         four(bank[6 + c % 2][:, :]), ALU.subtract), s["t_ready"])
                    for step in range(TT):
                        for d in range(2):
                            r, t = 2 * step + d, order[d][step]
                            dve.wait_ge(s["ks_done"], r + 1)
                            for j in range(2):
                                link(nc.vector.scalar_tensor_tensor(tile(resid[:, d, :], j), tile(bank[d], j),
                                                                    col(NEG_EG, 2 * j + d, t), v_t[:, t, j, :], ALU.mult, ALU.add),
                                     s["r_ready"] if j else None)
                        for d in range(2):
                            r, t = 2 * step + d, order[d][step]
                            dve.wait_ge(s["os_done"], r + 1)
                            dve.wait_ge(s["qs_out"], r + 1)
                            link(nc.vector.tensor_tensor(od[:, d, t, :], bank[6 + d][:, 0:2 * P], qs[:, d, :], ALU.add))
                            for j in range(2):
                                link(nc.vector.scalar_tensor_tensor(tile(state[:, d, :], j), tile(state[:, d, :], j),
                                                                    col(GL, 2 * j + d, t), tile(bank[6 + d], 2 + j), ALU.mult, ALU.add),
                                     s["s_ready"] if j else None)
                    o3 = od[:, 0, :, :].rearrange("p t (j e) -> p (t j) e", j=2)
                    link(nc.vector.tensor_tensor(od[:, 0, :, :], od[:, 0, :, :], od[:, 1, :, :], ALU.add), s["o_sum"])
                    dve.wait_ge(s["o_sqd"], 1)
                    link(nc.vector.tensor_reduce(ms[:, :], o_sq.rearrange("p (a e) -> p a e", e=P), AX.X, ALU.add))
                    link(nc.vector.tensor_scalar(ms[:, :], ms[:, :], 1.0 / P, EPS, ALU.mult, ALU.add), s["o_mean"])
                    dve.wait_ge(s["o_root"], 1)
                    link(nc.vector.tensor_tensor(o3, o3, ms[:, :].unsqueeze(2).to_broadcast([P, 2 * TT, P]), ALU.mult), s["o_norm"])
                    for j in range(2):
                        dve.wait_ge(s["o_turned"], j + 1)
                        dve.wait_ge(s["z_ready"], j + 1)
                        out = gated[:, bass.ds(n * 2 + j, 1), :].rearrange("p a t -> p (a t)")
                        link(nc.vector.scalar_tensor_tensor(out, bank[j][:, :], o_cols, zs[:, j, :], ALU.mult, ALU.mult))

        st.bodies(QK_HEADS, DN_GROUP, body)


def attention_keys(nc, bank, C, pkv, kg, rope, kf, v_t, sq, rs):
    with stage(nc, "sq sm kn rot turned mean root") as (s, block):
        @block.gpsimd
        def _(pool):
            inverse_root(nc, pool, C, rs[:, 0:ATT_KV * TT], s["mean"], s["root"])

        @block.scalar
        def _(act):
            link = Chain(act, s["act_own"])
            for h in range(ATT_KV):
                link(nc.scalar.activation(sq[:, TOK * h:TOK * h + TOK], pkv[:, h, :], ACT.Square), s["sq"])
            for h in range(ATT_KV):
                act.wait_ge(s["turned"], h + 1)
                link(nc.scalar.activation(v_t[:, h, :, :], bank[4 + h][:, :].rearrange("p (t e) -> p t e", t=TT), ACT.Copy))

        @block.tensor
        def _(pe):
            for h in range(ATT_KV):
                for t in range(TT):
                    mm = nc.tensor.transpose(bank[4 + h][:, P * t:P * t + P], pkv[:, ATT_KV + h, P * t:P * t + P], C("ident"))
                mm.then_inc(s["turned"], 1)
            pe.wait_ge(s["sq"], 2)
            column_sums(nc, C, bank[7], sq, ATT_KV * TT).then_inc(s["sm"], 1)
            pe.wait_ge(s["root"], 1)
            for h in range(ATT_KV):
                spread(nc, C, bank[h], rs[:, TT * h:TT * h + TT], TT).then_inc(s["sm"], 1)
            for h in range(ATT_KV):
                pe.wait_ge(s["kn"], h + 1)
                nc.tensor.matmul(bank[2 + h][:, 0:SEQ], C("rot"), kf[:, h, CTX:TOK], start=True, stop=True).then_inc(s["rot"], 1)

        @block.vector
        def _(dve):
            link = Chain(dve, s["dve_own"])
            dve.wait_ge(s["sm"], 1)
            link(nc.vector.tensor_scalar(rs[:, 0:ATT_KV * TT], bank[7][:, 0:ATT_KV * TT], 1.0 / P, EPS, ALU.mult, ALU.add), s["mean"])
            for h in range(ATT_KV):
                dve.wait_ge(s["sm"], h + 2)
                link(nc.vector.scalar_tensor_tensor(kf[:, h, :], pkv[:, h, :], kg, bank[h][:, :], ALU.mult, ALU.mult), s["kn"])
            for h in range(ATT_KV):
                dve.wait_ge(s["rot"], h + 1)
                link(nc.vector.tensor_tensor(rs[:, 0:SEQ], bank[2 + h][:, 0:SEQ], rope[:, SEQ:2 * SEQ], ALU.mult))
                link(nc.vector.tensor_tensor(kf[:, h, CTX:TOK], kf[:, h, CTX:TOK], rope[:, 0:SEQ], ALU.mult))
                link(nc.vector.tensor_tensor(kf[:, h, CTX:TOK], kf[:, h, CTX:TOK], rs[:, 0:SEQ], ALU.add))


def attention_heads(nc, bank, C, pqz, qg, rope, kf, v_t, gated):
    with ExitStack() as es:
        sb = lambda name, shape: es.enter_context(nc.sbuf_tensor(name, shape, F32))
        q = sb("att_q", [P, 2, SEQ])
        qsq = sb("att_qsq", [P, 2 * SEQ])
        rs = sb("att_rs", [P, 2 * SEQ])
        z = sb("att_z", [P, 2, SEQ])
        zt = sb("att_zt", [P, 2, SEQ])
        v = sb("att_v", [P, TT, P])
        pr = sb("att_pr", [P, 4, TOK])
        pt = sb("att_pt", [P, 2, TT, SEQ])
        mx = sb("att_mx", [P, 4])
        sm = sb("att_sm", [P, 4])
        flat = lambda a: a[:, :, :].rearrange("p a t -> p (a t)")
        two = lambda a: a.rearrange("p (a t) -> p a t", a=2)

        with nc.Fori(0, ATT_Q // 2) as i:
            names = "q_in q_sq q_sum q_norm q_rot q_ready scores negmax exped probs turned turned_out out z_ready mean root"
            with stage(nc, names) as (s, block):
                @block.gpsimd
                def _(pool):
                    inverse_root(nc, pool, C, rs[:, 0:4], s["mean"], s["root"])

                @block.tensor
                def _(pe):
                    pe.wait_ge(s["q_sq"], 1)
                    column_sums(nc, C, bank[2], qsq, 4).then_inc(s["q_sum"], 1)
                    pe.wait_ge(s["root"], 1)
                    spread(nc, C, bank[0], rs, 4).then_inc(s["q_sum"], 1)
                    pe.wait_ge(s["q_norm"], 1)
                    nc.tensor.matmul(bank[1][:, :], C("rot"), flat(q), start=True, stop=True).then_inc(s["q_rot"], 1)
                    pe.wait_ge(s["q_ready"], 1)
                    for n in range(4):
                        nc.tensor.matmul(bank[n][:, :], q[:, n // 2, P * (n % 2):P * (n % 2) + P],
                                         kf[:, bass.ds(i // 2, 1), :].rearrange("p a t -> p (a t)"),
                                         start=True, stop=True).then_inc(s["scores"], 1)
                    for n in range(4):
                        pe.wait_ge(s["probs"], n + 1)
                        if n >= 2:
                            pe.wait_ge(s["turned_out"], n - 1)
                        for t in range(TT):
                            mm = nc.tensor.transpose(bank[4 + n % 2][:, P * t:P * t + P], pr[:, n, P * t:P * t + P], C("ident"))
                        mm.then_inc(s["turned"], 1)
                    for j in range(2):
                        pe.wait_ge(s["turned_out"], 2 * j + 2)
                        accumulate(nc, bank[6 + j][:, 0:SEQ], [v[:, t, :] for t in range(TT)],
                                   [pt[:, j, t, :] for t in range(TT)]).then_inc(s["out"], 1)

                @block.scalar
                def _(act):
                    link = Chain(act, s["act_own"])
                    act.wait_ge(s["q_in"], 1)
                    link(nc.scalar.activation(qsq[:, :], flat(q), ACT.Square), s["q_sq"])
                    link(nc.scalar.activation(flat(zt), flat(z), ACT.Tanh, scale=0.5), s["z_ready"])
                    for n in range(4):
                        act.wait_ge(s["negmax"], n + 1)
                        link(nc.scalar.activation(pr[:, n, :], bank[n][:, :], ACT.Exp, bias=mx[:, n:n + 1],
                                                  scale=P ** -0.5, accum_out=sm[:, n:n + 1]), s["exped"])
                    for n in range(4):
                        act.wait_ge(s["turned"], n + 1)
                        t0 = P * (n % 2)
                        link(nc.scalar.activation(pt[:, n // 2, :, t0:t0 + P], bank[4 + n % 2][:, :].rearrange("p (t e) -> p t e", t=TT),
                                                  ACT.Copy), s["turned_out"])

                @block.vector
                def _(dve):
                    link = Chain(dve, s["dve_own"])
                    link(nc.vector.tensor_copy(q[:, :, :], pqz[:, bass.ds(i * 2, 2), :]))
                    link(nc.vector.tensor_copy(z[:, :, :], pqz[:, bass.ds(i * 2 + ATT_Q, 2), :]), s["q_in"])
                    link(nc.vector.tensor_copy(v[:, :, :], v_t[:, bass.ds(i // 2, 1), :, :].rearrange("p a t e -> p (a t) e")))
                    dve.wait_ge(s["q_sum"], 1)
                    link(nc.vector.tensor_scalar(rs[:, 0:4], bank[2][:, 0:4], 1.0 / P, EPS, ALU.mult, ALU.add), s["mean"])
                    dve.wait_ge(s["q_sum"], 2)
                    link(nc.vector.scalar_tensor_tensor(flat(q), flat(q), qg, bank[0][:, :], ALU.mult, ALU.mult), s["q_norm"])
                    dve.wait_ge(s["q_rot"], 1)
                    link(nc.vector.tensor_tensor(two(rs[:, :]), two(bank[1][:, :]), rope[:, SEQ:2 * SEQ].unsqueeze(1).to_broadcast([P, 2, SEQ]), ALU.mult))
                    link(nc.vector.tensor_tensor(q[:, :, :], q[:, :, :], rope[:, 0:SEQ].unsqueeze(1).to_broadcast([P, 2, SEQ]), ALU.mult))
                    link(nc.vector.tensor_tensor(flat(q), flat(q), rs[:, :], ALU.add), s["q_ready"])
                    for n in range(4):
                        dve.wait_ge(s["scores"], n + 1)
                        link(nc.vector.reduce_max(mx[:, n:n + 1], bank[n][:, :], AX.X))
                        link(nc.vector.tensor_scalar(mx[:, n:n + 1], mx[:, n:n + 1], -P ** -0.5, None, ALU.mult), s["negmax"])
                    dve.wait_ge(s["z_ready"], 1)
                    link(nc.vector.scalar_tensor_tensor(flat(z), flat(zt), 1.0, flat(z), ALU.add, ALU.mult))
                    for n in range(4):
                        dve.wait_ge(s["exped"], n + 1)
                        link(nc.vector.reciprocal(sm[:, n:n + 1], sm[:, n:n + 1]))
                        link(nc.vector.tensor_scalar(pr[:, n, :], pr[:, n, :], sm[:, n:n + 1], None, ALU.mult), s["probs"])
                    for j in range(2):
                        dve.wait_ge(s["out"], j + 1)
                        link(nc.vector.scalar_tensor_tensor(gated[:, bass.ds(i * 2 + j, 1), 0:SEQ].rearrange("p a t -> p (a t)"),
                                                            bank[6 + j][:, 0:SEQ], 0.5, z[:, j, :], ALU.mult, ALU.mult))


SSM_HEADS = 16
RW = 4
HG = 4
ST = SEQ // P
RWKV_DECAY = 0.6065306597
RWKV_LN_EPS = 64e-5


def flat(a):
    return a.rearrange("p a b -> p (a b)")


def sigmoid_of_tanh(nc, out, th):
    return nc.vector.tensor_scalar(out, th, 0.5, 0.5, ALU.mult, ALU.add)


S_G, S_NAC, S_DT = range(3)
S_PER_HEAD = 3 * 2 * ST


def ssd_steps(nc, bank, C, u, w_dt, dt_rows, a_rows, sc, tmp):
    n = ST * 32
    x, e, lg, gx, dt = (tmp[:, i, 0:n] for i in range(5))
    q3 = lambda a: a.rearrange("p (t c) -> p t c", t=ST)

    def put(q, src, d):
        out = sc[:, :, :].rearrange("p h (q d t) -> p q d h t", q=3, d=2)[:, q, d, :, :]
        return nc.vector.tensor_copy(out, src.rearrange("p (t d h) -> p d h t", t=ST, d=2)[:, d])

    with stage(nc, "raw x_ready e_ready ln_ready g_ready sums a_ready") as (s, block):
        @block.tensor
        def _(pe):
            for t in range(ST):
                for k in range(KT):
                    mm = nc.tensor.matmul(bank[0][:, 32 * t:32 * t + 32], u[:, k, CTX + P * t:CTX + P * t + P], w_dt[:, k, :],
                                          start=(t == 0 and k == 0), stop=(k == KT - 1), skip_group_check=True)
            mm.then_inc(s["raw"], 1)
            pe.wait_ge(s["g_ready"], 1)
            for d in range(2):
                for t in range(ST):
                    for src in range(ST):
                        if (src > t) if d == 0 else (src < t):
                            continue
                        w = "ones" if src != t else ("tri_b" if d else "tri_f")
                        at = 32 * t + 16 * d
                        mm = nc.tensor.matmul(bank[1][:, at:at + 16], C(w), gx[:, 32 * src + 16 * d:32 * src + 16 * d + 16],
                                              start=(d == 0 and t == 0 and src == 0), stop=True, skip_group_check=True)
            mm.then_inc(s["sums"], 1)

        @block.scalar
        def _(act):
            link = Chain(act, s["act_own"])
            link(nc.scalar.activation(a_rows, a_rows, ACT.Exp), s["a_ready"])
            act.wait_ge(s["x_ready"], 1)
            link(nc.scalar.activation(e, gx, ACT.Exp), s["e_ready"])
            act.wait_ge(s["x_ready"], 2)
            link(nc.scalar.activation(gx, lg, ACT.Ln), s["ln_ready"])

        @block.vector
        def _(dve):
            link = Chain(dve, s["dve_own"])
            dve.wait_ge(s["raw"], 1)
            link(nc.vector.tensor_tensor(q3(x), q3(bank[0][:, 0:n]), dt_rows.unsqueeze(1).to_broadcast([P, ST, 32]), ALU.add))
            link(nc.vector.scalar_tensor_tensor(gx, x, -1.0, x, ALU.mult, ALU.min), s["x_ready"])
            dve.wait_ge(s["e_ready"], 1)
            link(nc.vector.tensor_scalar(lg, e, 1.0, None, ALU.add), s["x_ready"])
            dve.wait_ge(s["ln_ready"], 1)
            link(nc.vector.tensor_scalar(lg, lg, -1.0, 1.0, ALU.mult, ALU.add))
            link(nc.vector.tensor_tensor(lg, lg, e, ALU.add))
            link(nc.vector.tensor_tensor(lg, lg, gx, ALU.add))
            link(nc.vector.scalar_tensor_tensor(dt, x, 0.0, lg, ALU.max, ALU.add))
            dve.wait_ge(s["a_ready"], 1)
            link(nc.vector.scalar_tensor_tensor(q3(gx), q3(dt), -1.0, a_rows.unsqueeze(1).to_broadcast([P, ST, 32]),
                                                ALU.mult, ALU.mult), s["g_ready"])
            dve.wait_ge(s["sums"], 1)
            link(nc.vector.tensor_scalar(x, bank[1][:, 0:n], -1.0, None, ALU.mult))
            for d in range(2):
                link(put(S_G, gx, d))
                link(put(S_NAC, x, d))
                link(put(S_DT, dt, d))


def ssd_conv(nc, p, conv_cols, bias_cols, raw, acc, th, hc):
    with stage(nc, "padded") as (s, block):
        @block.gpsimd
        def _(pool):
            nc.gpsimd.memset(raw[:, :, :], 0.0).then_inc(s["padded"], 1)
            pool.wait_ge(s["padded"], 1)

    with nc.Fori(0, 3) as i:
        with stage(nc, "kept conv tanh") as (s, block):
            @block.scalar
            def _(act):
                link = Chain(act, s["act_own"])
                for m in range(4):
                    link(nc.scalar.activation(raw[:, m, 2:SEQ + 2], p[:, bass.ds(i * 4 + (8 + m), 1), :].rearrange("p a t -> p (a t)"),
                                              ACT.Copy), s["kept"])
                for m in range(4):
                    act.wait_ge(s["conv"], m + 1)
                    link(nc.scalar.activation(th[:, m, :], acc[:, m, :], ACT.Tanh, scale=0.5), s["tanh"])

            @block.vector
            def _(dve):
                link = Chain(dve, s["dve_own"])
                link(nc.vector.tensor_copy(hc[:, 0:20], conv_cols(i)))
                link(nc.vector.tensor_copy(hc[:, 20:24], bias_cols(i)))
                for m in range(4):
                    dve.wait_ge(s["kept"], m + 1)
                    w = lambda j: hc[:, 5 * m + j:5 * m + j + 1]
                    link(nc.vector.tensor_scalar(acc[:, m, :], raw[:, m, 0:SEQ], w(0), hc[:, 20 + m:21 + m], ALU.mult, ALU.add))
                    for j in range(1, 5):
                        link(nc.vector.scalar_tensor_tensor(acc[:, m, :], raw[:, m, j:j + SEQ], w(j), acc[:, m, :],
                                                            ALU.mult, ALU.add), s["conv"] if j == 4 else None)
                for m in range(4):
                    dve.wait_ge(s["tanh"], m + 1)
                    link(sigmoid_of_tanh(nc, th[:, m, :], th[:, m, :]))
                    link(nc.vector.tensor_tensor(p[:, bass.ds(i * 4 + (8 + m), 1), :].rearrange("p a t -> p (a t)"),
                                                 th[:, m, :], acc[:, m, :], ALU.mult))


def ssd_heads(nc, bank, C, cs, p, sc, d_cols, ys, work):
    cb, x_t, e, m_t, xl, hs, th, z, dl = work
    with stage(nc, "cb_done turned out") as (s, block):
        @block.tensor
        def _(pe):
            for g in range(2):
                for t in range(ST):
                    mm = nc.tensor.matmul(bank[g][:, SEQ * t:SEQ * t + SEQ], p[:, 16 + g, P * t:P * t + P], p[:, 18 + g, :],
                                          start=True, stop=True)
                mm.then_inc(s["cb_done"], 1)
            for t in range(ST):
                for k in range(KT):
                    mm = nc.tensor.transpose(bank[2 + 2 * t + k // 4][:, P * (k % 4):P * (k % 4) + P], p[:, 8 + k, P * t:P * t + P],
                                             C("ident"))
                    if k % 4 == 3:
                        mm.then_inc(s["turned"], 1)

        @block.scalar
        def _(act):
            link = Chain(act, s["act_own"])
            for n in range(4):
                act.wait_ge(s["turned"], n + 1)
                link(nc.scalar.activation(x_t[:, n // 2, 512 * (n % 2):512 * (n % 2) + 512], bank[2 + n][:, :], ACT.Copy))

        @block.vector
        def _(dve):
            link = Chain(dve, s["dve_own"])
            for g in range(2):
                dve.wait_ge(s["cb_done"], g + 1)
                link(nc.vector.tensor_copy(cb[:, g, :], bank[g][:, :]))

    def col(hh, q, d, t):
        at = hh * S_PER_HEAD + q * 2 * ST + d * ST + t
        return hs[:, at:at + 1]

    wide = lambda a: a.rearrange("p (s t) -> p s t", s=2)

    with nc.Fori(0, SSM_HEADS // 2) as i:
        with stage(nc, "local rows decays weights ys_done tanh z_in") as (s, block):
            @block.tensor
            def _(pe):
                pe.wait_ge(s["local"], 1)
                for hh in range(2):
                    for d in range(2):
                        b = bank[2 * hh + d]
                        nc.tensor.matmul(b[:, :], C("ident"), cs(f"ssd_neg{4 * d}", 4), start=True, stop=False)
                        for t in range(ST):
                            mm = nc.tensor.matmul(wide(b[:, :]), col(hh, S_G, d, t).to_broadcast([P, P]),
                                                  cs(f"ssd_sum{4 * d + 2 * t}", 2).unsqueeze(1).to_broadcast([P, 2, SEQ]),
                                                  start=False, stop=(t == ST - 1))
                        mm.then_inc(s["rows"], 1)
                for hh in range(2):
                    pe.wait_ge(s["weights"], hh + 1)
                    for t in range(ST):
                        mm = nc.tensor.matmul(bank[4][64 * hh:64 * hh + 64, 0:SEQ], xl[:, t, 64 * hh:64 * hh + 64],
                                              m_t[:, hh, SEQ * t:SEQ * t + SEQ], start=(t == 0), stop=(t == ST - 1))
                mm.then_inc(s["ys_done"], 1)

            @block.scalar
            def _(act):
                link = Chain(act, s["act_own"])
                act.wait_ge(s["z_in"], 1)
                link(nc.scalar.activation(th[:, :], z[:, :], ACT.Tanh, scale=0.5), s["tanh"])
                for n in range(4):
                    act.wait_ge(s["rows"], n + 1)
                    for t in range(ST):
                        link(nc.scalar.activation(e[:, n, SEQ * t:SEQ * t + SEQ], bank[n][:, SEQ * t:SEQ * t + SEQ], ACT.Exp,
                                                  bias=col(n // 2, S_NAC, n % 2, t)), s["decays"] if t else None)

            @block.vector
            def _(dve):
                link = Chain(dve, s["dve_own"])
                link(nc.vector.tensor_copy(hs[:, :], sc[:, bass.ds(i * 2, 2), :].rearrange("p a c -> p (a c)")))
                link(nc.vector.tensor_copy(xl[:, :, :], x_t[:, :, bass.ds(i * P, P)]), s["local"])
                link(nc.vector.tensor_copy(z[:, :], p[:, bass.ds(i, 1), :].rearrange("p a t -> p (a t)")), s["z_in"])
                link(nc.vector.tensor_copy(dl[:, :], d_cols(i)))
                dve.wait_ge(s["tanh"], 1)
                link(sigmoid_of_tanh(nc, th[:, :], th[:, :]))
                link(nc.vector.tensor_tensor(z[:, :], z[:, :], th[:, :], ALU.mult))
                for hh in range(2):
                    dve.wait_ge(s["decays"], 2 * hh + 2)
                    for t in range(ST):
                        at = slice(SEQ * t, SEQ * t + SEQ)
                        link(nc.vector.tensor_scalar(m_t[:, hh, at], e[:, 2 * hh, at], col(hh, S_DT, 0, t), None, ALU.mult))
                        link(nc.vector.scalar_tensor_tensor(m_t[:, hh, at], e[:, 2 * hh + 1, at], col(hh, S_DT, 1, t),
                                                            m_t[:, hh, at], ALU.mult, ALU.add))
                    link(nc.vector.tensor_tensor(m_t[:, hh, :], m_t[:, hh, :], cb[:, bass.ds(i // 4, 1), :].rearrange("p a t -> p (a t)"),
                                                 ALU.mult), s["weights"])
                dve.wait_ge(s["ys_done"], 1)
                link(nc.vector.scalar_tensor_tensor(th[:, :], p[:, bass.ds(i + 8, 1), :].rearrange("p a t -> p (a t)"), dl[:, 0:1],
                                                    bank[4][:, 0:SEQ], ALU.mult, ALU.add))
                link(nc.vector.tensor_tensor(ys[:, bass.ds(i, 1), :].rearrange("p a t -> p (a t)"), th[:, :], z[:, :], ALU.mult))


def rwkv_inputs(nc, bank, C, p, ps, tmp, mu0, mu1, w_up, g_up, a_up, vecs, w0_rows, lw, g_t, aa, kk, rc, bonus):
    a0, k_k, k_a, r_k = vecs
    n = 14
    c0 = rc[:, 16:30]
    r, k = ps[:, 0:4, :], ps[:, 4:8, :]
    over = lambda v, w: v.unsqueeze(2).to_broadcast([P, v.shape[1], w])
    names = ("shifted tanh gd lw_raw lw_in lw_th a_raw a_in a_th g_raw kk_raw kk_sq kk_sum mean root spread rk_ready "
             "bonus_done")
    with stage(nc, names) as (s, block):
        @block.gpsimd
        def _(pool):
            inverse_root(nc, pool, C, rc[:, 0:16], s["mean"], s["root"])

        @block.tensor
        def _(pe):
            pe.wait_ge(s["tanh"], 1)
            for q in range(4):
                nc.tensor.matmul(bank[q][:, :], ps[0:64, 12, P * (q % 2):P * (q % 2) + P], w_up[:, q // 2, :],
                                 start=True, stop=True).then_inc(s["lw_raw"], 1)
            for m in range(RW):
                if m % 2 == 0:
                    pe.wait_ge(s["lw_in"], 2 + m)
                nc.tensor.matmul(bank[4 + m // 2][:, SEQ * (m % 2):SEQ * (m % 2) + SEQ], a_up[64:128, P * m:P * m + P],
                                 ps[64:128, 12, :], start=True, stop=True).then_inc(s["a_raw"], 1)
            pe.wait_ge(s["gd"], 1)
            for t in range(ST):
                nc.tensor.matmul(bank[6 + t][:, :], ps[:, 13, P * t:P * t + P], g_up[:, :], start=True, stop=True).then_inc(s["g_raw"], 1)
            pe.wait_ge(s["kk_sq"], 1)
            pe.wait_ge(s["lw_in"], 4)
            for t in range(ST):
                for m in range(RW):
                    mm = nc.tensor.matmul(bank[0][:, 8 * t + 2 * m:8 * t + 2 * m + 2], tmp[:, m, P * t:P * t + P],
                                          C("halves")[:, 0:2], start=True, stop=True)
            mm.then_inc(s["kk_sum"], 1)
            pe.wait_ge(s["root"], 1)
            for m in range(RW):
                for t in range(ST):
                    at = SEQ * (m % 2) + P * t
                    for hh in range(2):
                        mm = nc.tensor.matmul(bank[1 + m // 2][64 * hh:64 * hh + 64, at:at + P],
                                              rc[:, 8 * t + 2 * m + hh:8 * t + 2 * m + hh + 1].to_broadcast([P, 64]), C("ident"),
                                              start=True, stop=True)
                if m % 2:
                    mm.then_inc(s["spread"], 1)
            pe.wait_ge(s["rk_ready"], 1)
            for t in range(ST):
                for m in range(RW):
                    mm = nc.tensor.matmul(bank[3][:, 8 * t + 2 * m:8 * t + 2 * m + 2], tmp[:, m, P * t:P * t + P],
                                          C("halves")[:, 0:2], start=True, stop=True)
            mm.then_inc(s["bonus_done"], 1)

        @block.scalar
        def _(act):
            link = Chain(act, s["act_own"])
            act.wait_ge(s["shifted"], 1)
            link(nc.scalar.activation(ps[0:64, 12, :], ps[0:64, 12, :], ACT.Tanh), s["tanh"])
            link(nc.scalar.activation(ps[:, 13, :], ps[:, 13, :], ACT.Tanh, scale=0.5), s["tanh"])
            for q in range(4):
                act.wait_ge(s["lw_in"], q + 1)
                link(nc.scalar.activation(lw[:, q // 2, q % 2, :], lw[:, q // 2, q % 2, :], ACT.Tanh, scale=0.5), s["lw_th"])
            act.wait_ge(s["a_in"], 4)
            link(nc.scalar.activation(aa, aa, ACT.Tanh, scale=0.5), s["a_th"])
            for t in range(ST):
                act.wait_ge(s["g_raw"], t + 1)
                link(nc.scalar.activation(g_t[:, t, :], bank[6 + t][:, :], ACT.Copy))
            act.wait_ge(s["kk_raw"], 1)
            link(nc.scalar.activation(tmp[:, 0:4, :], kk, ACT.Square), s["kk_sq"])

        @block.vector
        def _(dve):
            link = Chain(dve, s["dve_own"])
            link(nc.vector.tensor_tensor(c0, mu0, mu1, ALU.add))
            link(nc.vector.tensor_scalar(c0, c0, -1.0, 1.0, ALU.mult, ALU.add))
            link(nc.vector.tensor_tensor(ps[:, :, :], p[:, 0:n, :], over(c0, SEQ), ALU.mult))
            link(nc.vector.tensor_tensor(tmp[:, :, 0:SEQ - 1], p[:, 0:n, 0:SEQ - 1], over(mu0, SEQ - 1), ALU.mult))
            link(nc.vector.tensor_tensor(ps[:, :, 1:SEQ], ps[:, :, 1:SEQ], tmp[:, :, 0:SEQ - 1], ALU.add))
            link(nc.vector.tensor_tensor(tmp[:, :, 0:SEQ - 1], p[:, 0:n, 1:SEQ], over(mu1, SEQ - 1), ALU.mult))
            link(nc.vector.tensor_tensor(ps[:, :, 0:SEQ - 1], ps[:, :, 0:SEQ - 1], tmp[:, :, 0:SEQ - 1], ALU.add), s["shifted"])
            link(nc.vector.tensor_tensor(kk[:, :, :], k, over(k_k, SEQ), ALU.mult), s["kk_raw"])
            dve.wait_ge(s["tanh"], 2)
            link(sigmoid_of_tanh(nc, ps[:, 13, :], ps[:, 13, :]), s["gd"])
            for q in range(4):
                dve.wait_ge(s["lw_raw"], q + 1)
                link(nc.vector.tensor_tensor(lw[:, q // 2, q % 2, :], bank[q][:, :], w0_rows[:, q // 2, :], ALU.add), s["lw_in"])
            for m in range(RW):
                dve.wait_ge(s["a_raw"], 2 * (m // 2) + 2)
                link(nc.vector.tensor_scalar(aa[:, m, :], bank[4 + m // 2][:, SEQ * (m % 2):SEQ * (m % 2) + SEQ], a0[:, m:m + 1], None,
                                             ALU.add), s["a_in"])
            dve.wait_ge(s["lw_th"], 4)
            every = lw[:, :, :, :].rearrange("p d t c -> p (d t c)")
            link(nc.vector.tensor_scalar(every, every, -0.5 * RWKV_DECAY, -0.5 * RWKV_DECAY, ALU.mult, ALU.add))
            dve.wait_ge(s["a_th"], 1)
            link(sigmoid_of_tanh(nc, aa, aa))
            dve.wait_ge(s["kk_sum"], 1)
            link(nc.vector.tensor_scalar(rc[:, 0:16], bank[0][:, 0:16], 1e-12, None, ALU.add), s["mean"])
            link(nc.vector.scalar_tensor_tensor(tmp[:, 0:4, :], aa[:, :, :], 1.0, over(k_a, SEQ), ALU.subtract, ALU.mult))
            link(nc.vector.scalar_tensor_tensor(k, tmp[:, 0:4, :], 1.0, k, ALU.add, ALU.mult))
            link(nc.vector.tensor_tensor(tmp[:, 0:4, :], r, k, ALU.mult))
            link(nc.vector.tensor_tensor(tmp[:, 0:4, :], tmp[:, 0:4, :], over(r_k, SEQ), ALU.mult), s["rk_ready"])
            for m in range(0, RW, 2):
                dve.wait_ge(s["spread"], m // 2 + 1)
                link(nc.vector.tensor_tensor(kk[:, m:m + 2, :], kk[:, m:m + 2, :],
                                             bank[1 + m // 2][:, :].rearrange("p (a t) -> p a t", a=2), ALU.mult))
            link(nc.vector.tensor_tensor(aa[:, :, :], aa[:, :, :], kk[:, :, :], ALU.mult))
            dve.wait_ge(s["bonus_done"], 1)
            link(nc.vector.tensor_copy(bonus[:, :], bank[3][:, 0:16]))


def rwkv_heads(nc, bank, C, cs, ps, lw, aa, kk, y_all, v_all, work):
    (lwl, e_in, e_ex, e_neg, ka, ki, kw_rw, grams, inv, inv_t, prod, ka_t, k_t, v_t, v_half, p_half, rr, sb, yd) = work
    chunks = 4
    levels = LEVELS - 1
    order = (range(chunks), range(chunks - 1, -1, -1))
    with stage(nc, "clear") as (s, block):
        @block.gpsimd
        def _(pool):
            for x in (v_half, p_half, rr):
                nc.gpsimd.memset(x[:, :], 0.0).then_inc(s["clear"], 1)
            pool.wait_ge(s["clear"], 3)

    def unit(d, hh, t):
        return (d * 2 + hh) * 2 + t

    def tile(a, n):
        return a[:, P * n:P * n + P]

    def part(a, at, half):
        return a[64 * half:64 * half + 64, at:at + P]

    row = lambda src, i: src[:, bass.ds(i, 1), :].rearrange("p a t -> p (a t)")
    four = lambda a: a.rearrange("p (t e) -> p t e", t=4)

    with nc.Fori(0, RW) as i:
        names = ("local sums exps keys_ready masked grams_done turned turned_out v_ready a_done p_ready bc_done t_ready "
                 "zero z_done r_ready pm_done ph_ready y_done y_out ds_done s_ready summed k_used")
        with stage(nc, names) as (s, block):
            @block.gpsimd
            def _(pool):
                link = Chain(pool, s["pool_own"])
                link(nc.gpsimd.memset(sb[:, :, :], 0.0), s["zero"])

            @block.tensor
            def _(pe):
                pe.wait_ge(s["local"], 1)
                for d in range(2):
                    for x in range(2):
                        for t in range(ST):
                            at = SEQ * x + P * t
                            mm = nc.tensor.matmul(bank[d][:, at:at + P], lwl[:, d, t, :], C(f"rw{4 * d + x}"), start=True, stop=True)
                    mm.then_inc(s["sums"], 1)
                pe.wait_ge(s["local"], 2)
                for t in range(ST):
                    mm = nc.tensor.transpose(tile(bank[2], t), v_half[:, P * (4 + t):P * (5 + t)], C("ident"))
                mm.then_inc(s["turned"], 1)
                for d in range(2):
                    pe.wait_ge(s["keys_ready"], d + 1)
                    for t in range(ST):
                        nc.tensor.transpose(tile(bank[3 + d], t), tile(ka[:, d, :], t), C("ident"))
                        mm = nc.tensor.transpose(tile(bank[3 + d], 2 + t), tile(ki[:, d, :], t), C("ident"))
                    mm.then_inc(s["turned"], 1)
                for d in range(2):
                    for hh in range(2):
                        for t in range(ST):
                            n = unit(d, hh, t)
                            if n >= 3:
                                pe.wait_ge(s["masked"], n - 2)
                            b = bank[5 + n % 3]
                            lo = slice(64 * hh, 64 * hh + 64)
                            rhs = kw_rw[lo, d, :, P * t:P * t + P]
                            nc.tensor.matmul(b[:, 0:SEQ].rearrange("p (x t) -> p x t", x=2), ka[lo, d, P * t:P * t + P], rhs,
                                             start=True, stop=True)
                            nc.tensor.matmul(b[:, SEQ:2 * SEQ].rearrange("p (x t) -> p x t", x=2), ki[lo, d, P * t:P * t + P], rhs,
                                             start=True, stop=True).then_inc(s["grams_done"], 1)
                pe.wait_ge(s["masked"], 8)
                pe.wait_ge(s["turned_out"], 3)
                for lv in range(levels):
                    for d in range(2):
                        if lv:
                            pe.wait_ge(s["t_ready"], 2 * (lv - 1) + d + 1)
                        for n in range(4):
                            rhs = C("ident") if lv == 0 else tile(inv[:, d, :], n)
                            mm = nc.tensor.matmul(tile(bank[d], n), grams[:, 4 * d + n, 0:P], rhs, start=True, stop=True)
                        mm.then_inc(s["a_done"], 1)
                    for d in range(2):
                        pe.wait_ge(s["p_ready"], 2 * lv + d + 1)
                        if 0 < lv < levels - 1:
                            for n in range(4):
                                nc.tensor.matmul(tile(bank[2 + d], n), tile(inv_t[:, d, :], n), tile(prod[:, d, :], n), start=True, stop=True)
                        for n in range(4):
                            rhs = C("ident") if lv == 0 else tile(inv_t[:, d, :], n)
                            mm = nc.tensor.matmul(tile(bank[4 + d], n), tile(prod[:, d, :], n), rhs, start=True, stop=True)
                        mm.then_inc(s["bc_done"], 1)
                pe.wait_ge(s["t_ready"], 2 * levels)
                for step in range(chunks):
                    for d in range(2):
                        r, c = 2 * step + d, order[d][step]
                        t = c // 2
                        if step == 0:
                            pe.wait_ge(s["zero"], 1)
                        else:
                            pe.wait_ge(s["s_ready"], r - 1)
                        nc.tensor.matmul(bank[d][:, 0:P], kw_rw[:, d, 0, P * t:P * t + P], sb[:, d, :], start=True, stop=False,
                                         skip_group_check=True)
                        for hh in range(2):
                            mm = nc.tensor.matmul(bank[d][:, 64 * hh:64 * hh + 64], grams[:, unit(d, hh, t), SEQ:SEQ + P],
                                                  v_t[:, t, 64 * hh:64 * hh + 64], start=False, stop=True, skip_group_check=True)
                        mm.then_inc(s["z_done"], 1)
                    for d in range(2):
                        r, c = 2 * step + d, order[d][step]
                        t = c // 2
                        pe.wait_ge(s["r_ready"], r + 1)
                        for hh in range(2):
                            mm = nc.tensor.matmul(bank[2 + d][:, 64 * hh:64 * hh + 64], tile(inv_t[:, d, :], 2 * hh + t),
                                                  rr[:, P * d + 64 * hh:P * d + 64 * hh + 64], start=(hh == 0), stop=True,
                                                  skip_group_check=True)
                        mm.then_inc(s["pm_done"], 1)
                    for d in range(2):
                        r, c = 2 * step + d, order[d][step]
                        t, half = c // 2, c % 2
                        ph = P * (2 * d + half)
                        pe.wait_ge(s["ph_ready"], r + 1)
                        nc.tensor.matmul(bank[6 + d][:, 0:P], C("ident"), sb[:, d, :], start=True, stop=False)
                        nc.tensor.matmul(bank[6 + d][:, 0:P], ka_t[:, d, t, :], p_half[:, ph:ph + P], start=False, stop=False)
                        nc.tensor.matmul(bank[6 + d][:, 0:P], k_t[:, d, t, :], v_half[:, P * c:P * c + P], start=False,
                                         stop=True).then_inc(s["ds_done"], 1)
                        nc.tensor.matmul(bank[4 + d][:, 0:P], kw_rw[:, d, 1, P * t:P * t + P], sb[:, d, :], start=True, stop=False,
                                         skip_group_check=True)
                        for hh in range(2):
                            n, cols = unit(d, hh, t), slice(64 * hh, 64 * hh + 64)
                            nc.tensor.matmul(bank[4 + d][:, cols], grams[:, n, P:2 * P], p_half[:, ph + 64 * hh:ph + 64 * hh + 64],
                                             start=False, stop=False, skip_group_check=True)
                            mm = nc.tensor.matmul(bank[4 + d][:, cols], grams[:, n, 3 * P:4 * P], v_t[:, t, cols],
                                                  start=False, stop=True, skip_group_check=True)
                        mm.then_inc(s["y_done"], 1)

            @block.scalar
            def _(act):
                link = Chain(act, s["act_own"])
                for d in range(2):
                    act.wait_ge(s["sums"], d + 1)
                    link(nc.scalar.activation(e_ex[:, d, :], bank[d][:, 0:SEQ], ACT.Exp))
                    link(nc.scalar.activation(e_in[:, d, :], bank[d][:, SEQ:2 * SEQ], ACT.Exp))
                    link(nc.scalar.activation(e_neg[:, d, :], bank[d][:, SEQ:2 * SEQ], ACT.Exp, scale=-1.0), s["exps"])
                act.wait_ge(s["turned"], 1)
                link(nc.scalar.activation(v_t[:, :, :], bank[2][:, 0:SEQ].rearrange("p (t e) -> p t e", t=ST), ACT.Copy), s["turned_out"])
                for d in range(2):
                    act.wait_ge(s["turned"], d + 2)
                    link(nc.scalar.activation(ka_t[:, d, :, :], bank[3 + d][:, 0:SEQ].rearrange("p (t e) -> p t e", t=ST), ACT.Copy))
                    link(nc.scalar.activation(k_t[:, d, :, :], bank[3 + d][:, SEQ:2 * SEQ].rearrange("p (t e) -> p t e", t=ST), ACT.Copy),
                         s["turned_out"])
                for step in range(chunks):
                    for d in range(2):
                        r, c = 2 * step + d, order[d][step]
                        half = c % 2
                        act.wait_ge(s["pm_done"], r + 1)
                        ph = P * (2 * d + half)
                        if r >= 4:
                            act.wait_ge(s["y_done"], r - 3)
                        link(nc.scalar.activation(part(p_half, ph, half), part(bank[2 + d], 0, half), ACT.Copy), s["ph_ready"])
                    for d in range(2):
                        r, c = 2 * step + d, order[d][step]
                        t, half = c // 2, c % 2
                        act.wait_ge(s["y_done"], r + 1)
                        link(nc.scalar.activation(yd[64 * half:64 * half + 64, d, t, :], part(bank[4 + d], 0, half), ACT.Copy), s["y_out"])

            @block.vector
            def _(dve):
                link = Chain(dve, s["dve_own"])
                link(nc.vector.tensor_copy(lwl[:, :, :, :].rearrange("p d t c -> p (d t) c"),
                                           lw[:, :, :, bass.ds(i * P, P)].rearrange("p d t c -> p (d t) c")), s["local"])
                link(nc.vector.tensor_copy(v_half[:, 4 * P:4 * P + SEQ], row(ps[:, 8:12, :], i)), s["local"])
                for d in range(2):
                    dve.wait_ge(s["exps"], d + 1)
                    link(nc.vector.tensor_tensor(ka[:, d, :], row(aa, i), e_neg[:, d, :], ALU.mult))
                    link(nc.vector.tensor_tensor(ki[:, d, :], row(ps[:, 4:8, :], i), e_neg[:, d, :], ALU.mult))
                    link(nc.vector.tensor_tensor(kw_rw[:, d, 0, :], row(kk, i), e_ex[:, d, :], ALU.mult))
                    link(nc.vector.tensor_tensor(kw_rw[:, d, 1, :], row(ps[:, 0:4, :], i), e_in[:, d, :], ALU.mult), s["keys_ready"])
                for n in range(8):
                    dve.wait_ge(s["grams_done"], n + 1)
                    link(nc.vector.tensor_tensor(grams[:, n, :], bank[5 + n % 3][:, :], cs(f"rw{4 * (n // 4)}", 4), ALU.mult), s["masked"])
                dve.wait_ge(s["turned_out"], 1)
                for t in range(ST):
                    for half in range(2):
                        link(nc.vector.tensor_copy(part(v_half, P * (2 * t + half), half), v_t[64 * half:64 * half + 64, t, :]))
                link(nc.vector.tensor_copy(v_all[:, :, bass.ds(i * P, P)], v_t[:, :, :]))
                for lv in range(levels):
                    for d in range(2):
                        dve.wait_ge(s["a_done"], 2 * lv + d + 1)
                        link(nc.vector.tensor_tensor(four(prod[:, d, :]), four(bank[d][:, :]),
                                                     C(f"lev_{'fb'[d]}{lv}").unsqueeze(1).to_broadcast([P, 4, P]), ALU.mult), s["p_ready"])
                    for d in range(2):
                        dve.wait_ge(s["bc_done"], 2 * lv + d + 1)
                        eye = C("ident").unsqueeze(1).to_broadcast([P, 4, P])
                        if lv == 0:
                            link(nc.vector.tensor_tensor(four(inv[:, d, :]), eye, four(prod[:, d, :]), ALU.subtract))
                        elif lv < levels - 1:
                            link(nc.vector.tensor_tensor(inv[:, d, :], inv[:, d, :], bank[2 + d][:, :], ALU.subtract))
                        link(nc.vector.tensor_tensor(four(inv_t[:, d, :]), eye if lv == 0 else four(inv_t[:, d, :]),
                                                     four(bank[4 + d][:, :]), ALU.subtract), s["t_ready"])
                for step in range(chunks):
                    for d in range(2):
                        r, c = 2 * step + d, order[d][step]
                        half = c % 2
                        dve.wait_ge(s["z_done"], r + 1)
                        link(nc.vector.tensor_scalar(part(rr, P * d, half), part(bank[d], 0, half), -1.0, None, ALU.mult), s["r_ready"])
                    for d in range(2):
                        r, c = 2 * step + d, order[d][step]
                        last = 64 * c + (0 if d else 63)
                        dve.wait_ge(s["ds_done"], r + 1)
                        dve.wait_ge(s["y_done"], r + 1)
                        link(nc.vector.scalar_tensor_tensor(sb[:, d, :], bank[6 + d][:, 0:P], e_in[:, d, last:last + 1], C("half"),
                                                            ALU.mult, ALU.mult), s["s_ready"])
                dve.wait_ge(s["y_out"], 8)
                link(nc.vector.tensor_tensor(y_all[:, :, bass.ds(i * P, P)], yd[:, 0, :, :], yd[:, 1, :, :], ALU.add))


def rwkv_output(nc, bank, C, y, v_all, g_t, bonus, ln_rows, sq, st16, out):
    heads = ST * 8
    y3 = y[:, :, :].rearrange("p t (h e) -> p (t h) e", e=64)
    v3 = v_all[:, :, :].rearrange("p t (h e) -> p (t h) e", e=64)
    s3 = sq[:, :, :].rearrange("p t (h e) -> p (t h) e", e=64)
    over = lambda c: c.unsqueeze(2).to_broadcast([P, heads, 64])
    rows = lambda j: ln_rows[:, j, :].unsqueeze(1).to_broadcast([P, ST, 512])
    with stage(nc, "centred squared mean root ready turned") as (s, block):
        @block.gpsimd
        def _(pool):
            inverse_root(nc, pool, C, st16[:, 0:16], s["mean"], s["root"])

        @block.scalar
        def _(act):
            link = Chain(act, s["act_own"])
            act.wait_ge(s["centred"], 1)
            link(nc.scalar.activation(flat(sq[:, :, :]), flat(y[:, :, :]), ACT.Square), s["squared"])
            for n in range(2):
                act.wait_ge(s["turned"], n + 1)
                link(nc.scalar.activation(flat(out[:, 2 * n:2 * n + 2, :]), bank[n][:, :], ACT.Copy))

        @block.tensor
        def _(pe):
            pe.wait_ge(s["ready"], 1)
            for m in range(RW):
                for t in range(ST):
                    at = SEQ * (m % 2) + P * t
                    mm = nc.tensor.transpose(bank[m // 2][:, at:at + P], y[:, t, P * m:P * m + P], C("ident"))
                if m % 2:
                    mm.then_inc(s["turned"], 1)

        @block.vector
        def _(dve):
            link = Chain(dve, s["dve_own"])
            link(nc.vector.tensor_reduce(st16[:, 16:32], y3, AX.X, ALU.add))
            link(nc.vector.tensor_scalar(st16[:, 16:32], st16[:, 16:32], 1.0 / 64, None, ALU.mult))
            link(nc.vector.tensor_tensor(y3, y3, over(st16[:, 16:32]), ALU.subtract), s["centred"])
            link(nc.vector.tensor_tensor(v3, v3, over(bonus[:, :]), ALU.mult))
            dve.wait_ge(s["squared"], 1)
            link(nc.vector.tensor_reduce(st16[:, 0:16], s3, AX.X, ALU.add))
            link(nc.vector.tensor_scalar(st16[:, 0:16], st16[:, 0:16], 1.0 / 64, RWKV_LN_EPS, ALU.mult, ALU.add), s["mean"])
            dve.wait_ge(s["root"], 1)
            link(nc.vector.tensor_tensor(y3, y3, over(st16[:, 0:16]), ALU.mult))
            link(nc.vector.tensor_tensor(y[:, :, :], y[:, :, :], rows(0), ALU.mult))
            link(nc.vector.tensor_tensor(y[:, :, :], y[:, :, :], rows(1), ALU.add))
            link(nc.vector.tensor_tensor(y[:, :, :], y[:, :, :], v_all[:, :, :], ALU.add))
            link(nc.vector.tensor_tensor(y[:, :, :], y[:, :, :], g_t[:, :, :], ALU.mult), s["ready"])


def hgrn_gates(nc, st, bank, u, ff):
    def body(n, offset):
        with stage(nc, "summed out") as (s, block):
            @block.sync
            def _(sp):
                st.ahead(sp, 4, offset)

            @block.tensor
            def _(pe):
                for k in range(KT):
                    if k % 2 == 0:
                        pe.wait_ge(st.loaded(k // 2), 16)
                    at = 512 * (k % 2)
                    for t in range(ST):
                        mm = nc.tensor.matmul(bank[t][:, :], u[:, k, CTX + P * t:CTX + P * t + P], st.slot(k // 2)[:, at:at + 512],
                                              start=(k == 0), stop=(k == KT - 1))
                mm.then_inc(s["summed"], 1)

            @block.vector
            def _(dve):
                link = Chain(dve, s["dve_own"])
                dve.wait_ge(s["summed"], 1)
                for t in range(ST):
                    link(nc.vector.tensor_copy(ff[:, n, t, :], bank[t][:, :]))

    st.bodies(2, 4, body)


def hgrn_forget(nc, bank, C, ff, lf, kf, lb, om):
    with stage(nc, "diff exped lb_ready sig ff_ready one_less turned kept") as (s, block):
        @block.tensor
        def _(pe):
            for d in range(2):
                pe.wait_ge(s["one_less"], d + 1)
                for m in range(HG):
                    for t in range(ST):
                        at = SEQ * (m % 2) + P * t
                        mm = nc.tensor.transpose(bank[2 * d + m // 2][:, at:at + P], lf[:, d, t, P * m:P * m + P], C("ident"))
                    if m % 2:
                        mm.then_inc(s["turned"], 1)

        @block.scalar
        def _(act):
            link = Chain(act, s["act_own"])
            every = lambda a, d: a[:, d, :, :].rearrange("p t c -> p (t c)")
            for d in range(2):
                link(nc.scalar.activation(every(ff, d), every(ff, d), ACT.Sigmoid), s["sig"])
            act.wait_ge(s["diff"], 1)
            link(nc.scalar.activation(lb, lb, ACT.Exp), s["exped"])
            for n in range(4):
                act.wait_ge(s["turned"], n + 1)
                link(nc.scalar.activation(flat(kf[:, n // 2, 2 * (n % 2):2 * (n % 2) + 2, :]), bank[n][:, :], ACT.Copy), s["kept"])
            act.wait_ge(s["ff_ready"], 2)
            for d in range(2):
                link(nc.scalar.activation(every(lf, d), every(ff, d), ACT.Ln))

        @block.vector
        def _(dve):
            link = Chain(dve, s["dve_own"])
            link(nc.vector.tensor_tensor(lb, lb, lb, ALU.subtract), s["diff"])
            dve.wait_ge(s["exped"], 1)
            link(nc.vector.reciprocal(om, lb))
            link(nc.vector.tensor_tensor(om, om, lb, ALU.mult))
            link(nc.vector.tensor_tensor(lb, om, om, ALU.subtract))
            link(nc.vector.tensor_scalar(om, lb, -1.0, 1.0, ALU.mult, ALU.add))
            wide = lambda a: a.unsqueeze(1).to_broadcast([P, ST, 512])
            for d in range(2):
                dve.wait_ge(s["sig"], d + 1)
                x = ff[:, d, :, :]
                link(nc.vector.tensor_tensor(x, x, wide(om), ALU.mult))
                link(nc.vector.tensor_tensor(x, x, wide(lb), ALU.add))
                link(nc.vector.tensor_scalar(lf[:, d, :, :], x, -1.0, 1.0, ALU.mult, ALU.add), s["one_less"])
                link(nc.vector.tensor_scalar(x, x, 2.0 ** -63, None, ALU.max))
            dve.wait_ge(s["kept"], 4)
            link(nc.vector.tensor_scalar(ff[:, :, :, :], ff[:, :, :, :], 1.0, None, ALU.mult), s["ff_ready"])
            link(nc.vector.tensor_copy(om, lb), s["ff_ready"])


def hgrn_heads(nc, bank, C, cs, p, lf, kf, w_cols, yh, work):
    lfl, q2, kl, e, qe, ke, sc, tmp, it, ib, ob, osq, rc, gg, gt, wl = work
    d2 = lambda a: a.rearrange("p (d t) -> p d t", d=2)
    row = lambda src, i: src[:, bass.ds(i, 1), :].rearrange("p a t -> p (a t)")
    with nc.Fori(0, HG) as i:
        names = ("local sums exped pair scored masked added turned turned_out x_ready out o_in o_sq o_sum mean root "
                 "spread g_in tanh e_used done")
        with stage(nc, names) as (s, block):
            @block.gpsimd
            def _(pool):
                link = Chain(pool, s["pool_own"])
                for n in range(LEVELS + 1):
                    pool.wait_ge(s["masked"], n + 1)
                    if n == 0:
                        link(nc.gpsimd.tensor_copy(sc[:, :], tmp[:, 0, :]), s["added"])
                    else:
                        link(nc.gpsimd.tensor_tensor(sc[:, :], sc[:, :], tmp[:, n % 2, :], ALU.add), s["added"])
                inverse_root(nc, pool, C, rc[:, :], s["mean"], s["root"])

            @block.tensor
            def _(pe):
                pe.wait_ge(s["local"], 4)
                for t in range(ST):
                    mm = nc.tensor.transpose(bank[6][:, P * t:P * t + P], it[:, P * t:P * t + P], C("ident"))
                mm.then_inc(s["turned"], 1)

                def sums(n):
                    if n >= 2:
                        pe.wait_ge(s["exped"], n - 1)
                    for d in range(2):
                        for t in range(ST):
                            at = SEQ * d + P * t
                            if n < LEVELS:
                                rhs = C(f"hg_{'fb'[d]}{n}")
                            elif d == 0:
                                rhs = C("tri_f") if t else C("aft")
                            else:
                                rhs = C("bef") if t else C("tri_b")
                            mm = nc.tensor.matmul(bank[n % 2][:, at:at + P], lfl[:, d, t, :], rhs, start=True, stop=True)
                    mm.then_inc(s["sums"], 1)

                def scores(n, ks, qs):
                    if n >= 2:
                        pe.wait_ge(s["masked"], n - 1)
                    for d in range(2):
                        for t in range(ST):
                            at = SEQ * d + P * t
                            mm = nc.tensor.matmul(bank[2 + n % 2][:, at:at + P], ks[:, at:at + P], qs[:, at:at + P], start=True, stop=True)
                    mm.then_inc(s["scored"], 1)

                scores(0, kl, q2)
                sums(0)
                for n in range(LEVELS):
                    sums(n + 1)
                    pe.wait_ge(s["pair"], n + 1)
                    scores(n + 1, ke[:, n % 2, :], qe[:, n % 2, :])
                pe.wait_ge(s["pair"], LEVELS + 1)
                pe.wait_ge(s["masked"], LEVELS)
                kx, qx = ke[:, LEVELS % 2, :], qe[:, LEVELS % 2, :]
                nc.tensor.matmul(bank[4][:, 0:P], kx[:, 0:P], qx[:, P:2 * P], start=True, stop=True)
                nc.tensor.matmul(bank[4][:, P:2 * P], kx[:, 3 * P:4 * P], qx[:, 2 * P:3 * P], start=True, stop=True).then_inc(s["scored"], 1)
                pe.wait_ge(s["x_ready"], 1)
                pe.wait_ge(s["turned_out"], 1)
                for t in range(ST):
                    nc.tensor.matmul(bank[5][:, P * t:P * t + P], ib[:, t, :], tmp[:, 0, P * t:P * t + P], start=(t == 0), stop=False,
                                     skip_group_check=True)
                    cross = tmp[:, 1, P:2 * P] if t == 0 else tmp[:, 1, 0:P]
                    mm = nc.tensor.matmul(bank[5][:, P * t:P * t + P], ib[:, 1 - t, :], cross, start=False, stop=True, skip_group_check=True)
                mm.then_inc(s["out"], 1)
                pe.wait_ge(s["o_sq"], 1)
                column_sums(nc, C, bank[6], osq, ST).then_inc(s["o_sum"], 1)
                pe.wait_ge(s["root"], 1)
                spread(nc, C, bank[7], rc, ST).then_inc(s["spread"], 1)

            @block.scalar
            def _(act):
                link = Chain(act, s["act_own"])
                act.wait_ge(s["turned"], 1)
                link(nc.scalar.activation(ib[:, :, :], bank[6][:, 0:SEQ].rearrange("p (t e) -> p t e", t=ST), ACT.Copy), s["turned_out"])
                act.wait_ge(s["g_in"], 1)
                link(nc.scalar.activation(gt[:, :], gg[:, :], ACT.Tanh, scale=0.5), s["tanh"])
                for n in range(LEVELS + 1):
                    act.wait_ge(s["sums"], n + 1)
                    if n >= 2:
                        act.wait_ge(s["pair"], n - 1)
                    link(nc.scalar.activation(e[:, n % 2, :], bank[n % 2][:, :], ACT.Exp), s["exped"])
                act.wait_ge(s["o_in"], 1)
                link(nc.scalar.activation(osq[:, :], ob[:, :], ACT.Square), s["o_sq"])

            @block.vector
            def _(dve):
                link = Chain(dve, s["dve_own"])
                link(nc.vector.tensor_copy(lfl[:, :, :, :].rearrange("p d t c -> p (d t) c"),
                                           lf[:, :, :, bass.ds(i * P, P)].rearrange("p d t c -> p (d t) c")), s["local"])
                link(nc.vector.tensor_copy(d2(q2[:, :]), row(p[:, 0:4, :], i).unsqueeze(1).to_broadcast([P, 2, SEQ])), s["local"])
                link(nc.vector.tensor_copy(d2(kl[:, :]), kf[:, :, bass.ds(i, 1), :].rearrange("p d a t -> p (d a) t")), s["local"])
                link(nc.vector.tensor_copy(it[:, :], row(p[:, 4:8, :], i)), s["local"])
                link(nc.vector.tensor_copy(gg[:, :], row(p[:, 8:12, :], i)), s["g_in"])
                link(nc.vector.tensor_copy(wl[:, :], w_cols(i)))
                dve.wait_ge(s["scored"], 1)
                link(nc.vector.tensor_tensor(tmp[:, 0, :].rearrange("p (t e) -> p t e", t=4), bank[2][:, :].rearrange("p (t e) -> p t e", t=4),
                                             C("ident").unsqueeze(1).to_broadcast([P, 4, P]), ALU.mult), s["masked"])
                for n in range(LEVELS + 1):
                    dve.wait_ge(s["exped"], n + 1)
                    if n >= 2:
                        dve.wait_ge(s["scored"], n)
                    link(nc.vector.tensor_tensor(qe[:, n % 2, :], q2[:, :], e[:, n % 2, :], ALU.mult))
                    link(nc.vector.tensor_tensor(ke[:, n % 2, :], kl[:, :], e[:, n % 2, :], ALU.mult), s["pair"])
                    if n < LEVELS:
                        m = n + 1
                        dve.wait_ge(s["scored"], m + 1)
                        if m >= 2:
                            dve.wait_ge(s["added"], m - 1)
                        for d in range(2):
                            lev = C(f"lev_{'bf'[d]}{n}").unsqueeze(1).to_broadcast([P, 2, P])
                            at = slice(SEQ * d, SEQ * d + SEQ)
                            link(nc.vector.tensor_tensor(tmp[:, m % 2, at].rearrange("p (t e) -> p t e", t=2),
                                                         bank[2 + m % 2][:, at].rearrange("p (t e) -> p t e", t=2), lev, ALU.mult),
                                 s["masked"] if d else None)
                dve.wait_ge(s["added"], LEVELS + 1)
                link(nc.vector.tensor_tensor(tmp[:, 0, 0:SEQ], sc[:, 0:SEQ], sc[:, SEQ:2 * SEQ], ALU.add))
                dve.wait_ge(s["scored"], LEVELS + 2)
                link(nc.vector.tensor_copy(tmp[:, 1, 0:SEQ], bank[4][:, 0:SEQ]), s["x_ready"])
                dve.wait_ge(s["tanh"], 1)
                link(sigmoid_of_tanh(nc, gt[:, :], gt[:, :]))
                link(nc.vector.tensor_tensor(gg[:, :], gg[:, :], gt[:, :], ALU.mult))
                dve.wait_ge(s["out"], 1)
                link(nc.vector.tensor_copy(ob[:, :], bank[5][:, 0:SEQ]), s["o_in"])
                dve.wait_ge(s["o_sum"], 1)
                link(nc.vector.tensor_scalar(rc[:, :], bank[6][:, 0:ST], 1.0 / P, EPS, ALU.mult, ALU.add), s["mean"])
                dve.wait_ge(s["spread"], 1)
                link(nc.vector.scalar_tensor_tensor(ob[:, :], ob[:, :], wl[:, 0:1], bank[7][:, 0:SEQ], ALU.mult, ALU.mult))
                link(nc.vector.tensor_tensor(row(yh, i), ob[:, :], gg[:, :], ALU.mult))


COLS = ("c", "norm_g", "ada_b", "conv", "dn_o", "qg", "kg", "final_g")


def load_all(nc, pairs, sem):
    for dst, src in pairs:
        nc.sync.dma_start(dst, src).then_inc(sem, 16)
    nc.sync.wait_ge(sem, 16 * len(pairs))
    nc.sync.sem_clear(sem)
    nc.all_engine_barrier()


def build(nc, a, out, col_at):
    with ExitStack() as top:
        used = {}

        def sb(name, shape, es=top):
            used[name] = used.get(name, 0) + 1
            return es.enter_context(nc.sbuf_tensor(f"{name}_{used[name]}", shape, F32))

        bank = [top.enter_context(nc.psum_tensor(f"bank{i}", [P, 512], F32)) for i in range(8)]
        w_sems = [[top.enter_context(nc.semaphore(f"w{i}_{c}")) for c in range(SLOTS)] for i in range(2)]
        small = top.enter_context(nc.semaphore("small"))
        w_ring = sb("w_ring", [P, 2, SLOTS, CHUNK])
        h = sb("h", [P, KT, TOK])
        u = sb("u", [P, KT, TOK])
        cols = sb("cols", [P, a["cols"].shape[1]])
        st = Stream(nc, a["w"], w_ring, w_sems)

        def cc(name, n0=0, n1=None):
            lo, n = col_at[name]
            return cols[:, lo + n0:lo + (n if n1 is None else n1)]

        with ExitStack() as es:
            const = sb("const", [P, len(CONST_NAMES) * P], es)
            names = CONST_NAMES
            C = lambda name: const[:, P * names.index(name):P * names.index(name) + P]
            gated = sb("gated", [P, 2 * KT, TOK], es)
            load_all(nc, [(h[:, :, :], a["h"].rearrange("p (k t) -> p k t", k=KT)), (cols[:, :], a["cols"]),
                          (const[:, :], a["const"])], small)

            def modulate(layer, es2):
                with ExitStack() as e3:
                    mod = sb(f"mod{layer}", [P, 24, 2], es2)
                    rows = sb("mod_rows", [2, 512], e3)
                    sc_t = sb("silu_c", [P, KT, 2], e3)
                    sq = sb("sq", [P, KT, TOK], e3)
                    rs = sb("rs", [P, TOK], e3)
                    gs = sb("gs", [P, KT, 2], e3)
                    with stage(nc, "th") as (s, block):
                        @block.scalar
                        def _(act):
                            nc.scalar.activation(sc_t[:, :, :].rearrange("p k c -> p (k c)"), cc("c"), ACT.Tanh, scale=0.5).then_inc(s["th"], 1)

                        @block.vector
                        def _(dve):
                            link = Chain(dve, s["dve_own"])
                            dve.wait_ge(s["th"], 1)
                            f = sc_t[:, :, :].rearrange("p k c -> p (k c)")
                            link(nc.vector.tensor_scalar(f, f, 0.5, 0.5, ALU.mult, ALU.add))
                            link(nc.vector.tensor_tensor(f, f, cc("c"), ALU.mult))
                    modulation(nc, st, bank, C, layer, sc_t, rows, mod, 
                               lambda n: cols[:, bass.ds(n * 4 + (col_at["ada_b"][0] + 24 * layer), 4)])
                    feature_norm(nc, bank, C, h, u, cc("norm_g", 8 * layer, 8 * layer + 8), mod,
                                 ((0, CTX, 1), (CTX, SEQ, 0)), sq, rs, gs)
                return mod

            with ExitStack() as l0:
                mod = modulate(0, l0)
                sc = sb("sc", [P, QK_HEADS, PER_HEAD], l0)
                o_cols = sb("o_cols", [P, 1], l0)
                with ExitStack() as e3:
                    w_ab = sb("w_ab", [P, KT, 64], e3)
                    gate_rows = sb("gate_rows", [P, 2, 32], e3)
                    tmp = sb("gate_tmp", [P, 5, P], e3)
                    load_all(nc, [(w_ab[:, :, :], a["w_ab"].rearrange("p (k c) -> p k c", k=KT)),
                                  (gate_rows[:, :, :].rearrange("p a c -> p (a c)"), a["rows"][:, 0:64].to_broadcast([P, 64]))], small)
                    delta_gates(nc, bank, C, u, w_ab, gate_rows[:, 0, :], gate_rows[:, 1, :], sc, tmp)
                with stage(nc, "half") as (s, block):
                    @block.vector
                    def _(dve):
                        nc.vector.tensor_scalar(o_cols[:, :], cc("dn_o"), 0.5, None, ALU.mult).then_inc(s["half"], 1)
                        dve.wait_ge(s["half"], 1)
                delta_heads(nc, st, bank, C, u, sc, cc("conv"), o_cols[:, 0:1], gated, h)
                load_all(nc, [(h[:, :, :], a["h"].rearrange("p (k t) -> p k t", k=KT))], small)
                residual_linear(nc, st, bank, 4, 4, gated, 16, h, mod, ((0, CTX, 1), (CTX, SEQ, 0)), 0)
            with ExitStack() as l1:
                mod = modulate(1, l1)
                pqz = sb("pqz", [P, 2 * ATT_Q, SEQ], l1)
                pkv = sb("pkv", [P, 2 * ATT_KV, TOK], l1)
                kf = sb("kf", [P, ATT_KV, TOK], l1)
                v_t = sb("v_t1", [P, ATT_KV, TT, P], l1)
                rope = sb("rope", [P, 2 * SEQ], l1)
                load_all(nc, [(rope[:, :], a["rope"])], small)
                project(nc, st, bank, 4, 4, lambda k: u[:, k, CTX:TOK], SEQ, pqz)
                project(nc, st, bank, 1, 4, lambda k: u[:, k, :], TOK, pkv)
                with ExitStack() as e3:
                    sq = sb("sq1", [P, 2 * TOK], e3)
                    rs = sb("rs1", [P, TOK], e3)
                    attention_keys(nc, bank, C, pkv, cc("kg"), rope, kf, v_t, sq, rs)
                attention_heads(nc, bank, C, pqz, cc("qg"), rope, kf, v_t, gated)
                residual_linear(nc, st, bank, 2, 4, gated, 8, h, mod, ((CTX, SEQ, 0),), CTX)
            with ExitStack() as e3:
                sq = sb("sq2", [P, KT, TOK], e3)
                rs = sb("rs2", [P, TOK], e3)
                feature_norm(nc, bank, C, h, h, cc("final_g"), None, ((CTX, SEQ, 0),), sq, rs, None)

        latent = lambda k: u[:, k, CTX:TOK]
        ys = u[:, :, 0:CTX]
        spare = h[:, :, 0:CTX]
        base = sb("const_base", [P, N_BASE * P])
        yr = sb("yr", [P, RW, SEQ])
        yh = sb("yh", [P, HG, SEQ])

        def constants(part=None, at=0):
            def cs(name, n):
                k = SECOND_NAMES.index(name)
                return base[:, P * k:P * (k + n)] if k < N_BASE else part[:, P * (k - at):P * (k - at + n)]
            return (lambda name: cs(name, 1)), cs

        def const_part(first, n, es2):
            at = SECOND_NAMES.index(first)
            part = sb("const_part", [P, n * P], es2)
            C, cs = constants(part, at)
            return C, cs, (part[:, :], a["const2"][:, P * at:P * (at + n)])

        load_all(nc, [(base[:, :], a["const2"][:, 0:N_BASE * P])], small)
        C, _ = constants()

        def norm(src, dst, g, first):
            with ExitStack() as e3:
                sq = sb("sq3", [P, KT, SEQ], e3)
                rs = sb("rs3", [P, SEQ], e3)
                feature_norm(nc, bank, C, src, dst, g, None, ((first, SEQ, 0),), sq, rs, None)

        norm(h, u, cc("norm1_w"), CTX)

        with ExitStack() as es:
            C2, cs, pair = const_part("ssd_neg0", 16, es)
            p = sb("p_ssd", [P, 20, SEQ], es)
            sc = sb("sc_ssd", [P, SSM_HEADS, S_PER_HEAD], es)
            with ExitStack() as e3:
                w_dt = sb("w_dt", [P, KT, 32], e3)
                dt_rows = sb("dt_rows", [P, 2, 32], e3)
                tmp = sb("dt_tmp", [P, 5, 32 * ST], e3)
                load_all(nc, [pair, (w_dt[:, :, :].rearrange("p k c -> p (k c)"), a["w_dt"]),
                              (dt_rows[:, :, :].rearrange("p a c -> p (a c)"), a["rows"][:, 64:128].to_broadcast([P, 64]))], small)
                ssd_steps(nc, bank, C2, u, w_dt, dt_rows[:, 0, :], dt_rows[:, 1, :], sc, tmp)
            project(nc, st, bank, 4, 5, latent, SEQ, p)
            with ExitStack() as e3:
                raw = sb("raw_ssd", [P, 4, SEQ + 4], e3)
                acc = sb("acc_ssd", [P, 4, SEQ], e3)
                th = sb("th_ssd", [P, 4, SEQ], e3)
                hc = sb("hc_ssd", [P, 24], e3)
                ssd_conv(nc, p, lambda i: cols[:, bass.ds(i * 20 + col_at["ssm_conv"][0], 20)],
                         lambda i: cols[:, bass.ds(i * 4 + col_at["ssm_conv_b"][0], 4)], raw, acc, th, hc)
            with ExitStack() as e3:
                work = [sb(n, [P] + d, e3) for n, d in (
                    ("ssd_cb", [2, 512]), ("ssd_x", [ST, D]), ("ssd_e", [4, 512]), ("ssd_m", [2, 512]), ("ssd_xl", [ST, P]),
                    ("ssd_hs", [2 * S_PER_HEAD]), ("ssd_th", [SEQ]), ("ssd_z", [SEQ]), ("ssd_d", [1]))]
                ssd_heads(nc, bank, C2, cs, p, sc, lambda i: cols[:, bass.ds(i + col_at["ssm_d"][0], 1)], ys, work)
            norm(u, u, cc("ssm_norm_w"), 0)

        with ExitStack() as es:
            C2, cs, pair = const_part("rw0", 10, es)
            ps = sb("ps_rw", [P, 14, SEQ], es)
            lw = sb("lw_rw", [P, 2, ST, 512], es)
            g_t = sb("g_rw", [P, ST, 512], es)
            bonus = sb("bonus_rw", [P, 16], es)
            aa, kk = spare[:, 0:4, :], spare[:, 4:8, :]
            with ExitStack() as e3:
                p = sb("p_rw", [P, 16, SEQ], e3)
                tmp = sb("tmp_rw", [P, 14, SEQ], e3)
                up = sb("up_rw", [P, 2, 512], e3)
                a_up = sb("a_up", [P, 512], e3)
                g_up = sb("g_up", [P, 512], e3)
                w0_rows = sb("w0_rows", [P, 2, 512], e3)
                rc = sb("rc_rw", [P, 32], e3)
                load_all(nc, [pair, (up[0:64, :, :].rearrange("p a c -> p (a c)"), a["w_up"]), (a_up[64:128, :], a["a_up"]),
                              (g_up[:, :], a["g_up"]),
                              (w0_rows[:, :, :].rearrange("p a c -> p (a c)"), a["rows"][:, 128:1152].to_broadcast([P, 1024]))], small)
                project(nc, st, bank, 4, 4, latent, SEQ, p)
                rwkv_inputs(nc, bank, C2, p, ps, tmp, cc("rwkv_mu", 0, 14), cc("rwkv_mu", 14, 28), up[0:64], g_up, a_up,
                            [cc(n) for n in ("a0", "k_k", "k_a", "r_k")], w0_rows, lw, g_t, aa, kk, rc, bonus)
            y_all = sb("y_rw", [P, ST, 512], es)
            v_all = sb("v_rw", [P, ST, 512], es)
            with ExitStack() as e3:
                work = [sb("rw_" + n, [P] + d, e3) for n, d in (
                    ("lwl", [2, ST, P]), ("e_in", [2, SEQ]), ("e_ex", [2, SEQ]), ("e_neg", [2, SEQ]), ("ka", [2, SEQ]),
                    ("ki", [2, SEQ]), ("kw_rw", [2, 2, SEQ]), ("grams", [8, 512]), ("inv", [2, 512]), ("inv_t", [2, 512]),
                    ("prod", [2, 512]), ("ka_t", [2, ST, P]), ("k_t", [2, ST, P]), ("v_t", [ST, P]), ("v_half", [6 * P]),
                    ("p_half", [4 * P]), ("rr", [2 * P]), ("sb", [2, P]), ("yd", [2, ST, P]))]
                rwkv_heads(nc, bank, C2, cs, ps, lw, aa, kk, y_all, v_all, work)
            with ExitStack() as e3:
                ln_rows = sb("ln_rows", [P, 2, 512], e3)
                sq = sb("sq_rw", [P, ST, 512], e3)
                st16 = sb("st_rw", [P, 32], e3)
                load_all(nc, [(ln_rows[:, :, :].rearrange("p a c -> p (a c)"), a["rows"][:, 1152:2176].to_broadcast([P, 1024]))], small)
                rwkv_output(nc, bank, C2, y_all, v_all, g_t, bonus, ln_rows, sq, st16, yr)

        with ExitStack() as es:
            C2, cs, pair = const_part("hg_f0", 16, es)
            p = sb("p_hg", [P, 12, SEQ], es)
            lf = sb("lf_hg", [P, 2, ST, 512], es)
            kf = sb("kf_hg", [P, 2, HG, SEQ], es)
            with ExitStack() as e3:
                ff = sb("ff_hg", [P, 2, ST, 512], e3)
                lb = sb("lb_hg", [P, 512], e3)
                om = sb("om_hg", [P, 512], e3)
                load_all(nc, [pair, (lb[:, :], a["rows"][:, 2176:2688].to_broadcast([P, 512]))], small)
                project(nc, st, bank, 4, 3, latent, SEQ, p)
                hgrn_gates(nc, st, bank, u, ff)
                hgrn_forget(nc, bank, C2, ff, lf, kf, lb[:, :], om[:, :])
            with ExitStack() as e3:
                work = [sb("hg_" + n, [P] + d, e3) for n, d in (
                    ("lfl", [2, ST, P]), ("q2", [512]), ("kl", [512]), ("e", [2, 512]), ("qe", [2, 512]), ("ke", [2, 512]),
                    ("sc", [512]), ("tmp", [2, 512]), ("it", [SEQ]), ("ib", [ST, P]), ("ob", [SEQ]), ("osq", [SEQ]),
                    ("rc", [ST]), ("gg", [SEQ]), ("gt", [SEQ]), ("wl", [1]))]
                hgrn_heads(nc, bank, C2, cs, p, lf, kf, lambda i: cols[:, bass.ds(i + col_at["hgrn_norm_w"][0], 1)], yh, work)

        with ExitStack() as es:
            gates = sb("gates", [P, 24, SEQ], es)
            project(nc, st, bank, 4, 6, latent, SEQ, gates)
            with stage(nc, "tanh") as (s, block):
                every = gates[:, :, :].rearrange("p a t -> p (a t)")

                @block.scalar
                def _(act):
                    nc.scalar.activation(every, every, ACT.Tanh, scale=0.5).then_inc(s["tanh"], 1)

                @block.vector
                def _(dve):
                    link = Chain(dve, s["dve_own"])
                    dve.wait_ge(s["tanh"], 1)
                    link(sigmoid_of_tanh(nc, every, every))
            for b, (src, tiles, count) in enumerate(((ys, 8, 2), (yr, 4, 1), (yh, 4, 1))):
                gated_linear(nc, st, bank, count, 4, src, tiles, gates[:, 8 * b:8 * b + 8, :])
            mixed = gates[:, 0:8, :]
            with stage(nc, "") as (s, block):
                @block.vector
                def _(dve):
                    link = Chain(dve, s["dve_own"])
                    link(nc.vector.tensor_tensor(mixed, mixed, gates[:, 8:16, :], ALU.add))
                    link(nc.vector.tensor_tensor(mixed, mixed, gates[:, 16:24, :], ALU.add))
            residual_linear(nc, st, bank, 2, 4, mixed, KT, h, None, ((CTX, SEQ, 0),), CTX)

        norm(h, u, cc("norm2_w"), CTX)
        with ExitStack() as es:
            ffn = sb("ffn", [P, 2 * FF, SEQ], es)
            project(nc, st, bank, 11, 4, latent, SEQ, ffn)
            with stage(nc, "tanh") as (s, block):
                gate, up = flat(ffn[:, 0:FF, :]), flat(ffn[:, FF:2 * FF, :])
                with nc.sbuf_tensor("ffn_tanh", [P, FF * SEQ], F32) as th:
                    @block.scalar
                    def _(act):
                        nc.scalar.activation(th[:, :], gate, ACT.Tanh, scale=0.5).then_inc(s["tanh"], 1)

                    @block.vector
                    def _(dve):
                        link = Chain(dve, s["dve_own"])
                        link(nc.vector.scalar_tensor_tensor(up, gate, 0.5, up, ALU.mult, ALU.mult))
                        dve.wait_ge(s["tanh"], 1)
                        link(nc.vector.scalar_tensor_tensor(gate, th[:, :], 1.0, up, ALU.add, ALU.mult))
            residual_linear(nc, st, bank, 4, 6, ffn, FF, h, None, ((CTX, SEQ, 0),), CTX)
        norm(h, u, cc("final_norm_w"), CTX)
        st.drain()
        finish(nc, out, u[:, :, CTX:TOK])


def gated_linear(nc, st, bank, count, per_body, src, k_tiles, gates):
    def evacuate(m, ps):
        dst = gates[:, bass.ds(m, 1), :].rearrange("p a t -> p (a t)")
        return nc.vector.tensor_tensor(dst, ps[:, 0:SEQ], dst, ALU.mult)
    linear(nc, st, bank, count, per_body, lambda k: src[:, k, :], SEQ, evacuate, k_tiles)


def project(nc, st, bank, count, per_body, src, n_tok, dst):
    def evacuate(m, ps):
        out = dst[:, bass.ds(m, 1), 0:n_tok].rearrange("p a t -> p (a t)")
        return nc.vector.tensor_copy(out, ps[:, 0:n_tok])
    linear(nc, st, bank, count, per_body, src, n_tok, evacuate)


def residual_linear(nc, st, bank, count, per_body, src, k_tiles, h, mod, streams, lo):
    n_tok = sum(x[1] for x in streams)

    def evacuate(m, ps):
        for t0, tn, c in streams:
            dst = h[:, bass.ds(m, 1), t0:t0 + tn].rearrange("p a t -> p (a t)")
            if mod is None:
                last = nc.vector.tensor_tensor(dst, ps[:, t0 - lo:t0 - lo + tn], dst, ALU.add)
            else:
                last = nc.vector.scalar_tensor_tensor(dst, ps[:, t0 - lo:t0 - lo + tn],
                                                      mod[:, bass.ds(m + 16, 1), c], dst, ALU.mult, ALU.add)
        return last
    linear(nc, st, bank, count, per_body, lambda k: src[:, k, 0:n_tok], n_tok, evacuate, k_tiles)


def finish(nc, out, src):
    n = src.shape[1] * SEQ
    with stage(nc, "stored") as (s, block):
        @block.sync
        def _(sp):
            sp.dma_start(out[:, 0:n].rearrange("p (k t) -> p k t", t=SEQ), src).then_inc(s["stored"], 16)
            sp.wait_ge(s["stored"], 16)


def fm(w, cols=None):
    k, m = w.shape
    return w.reshape(k // P, P, m // P, P).transpose(2, 1, 0, 3).reshape(m // P, P, k)


def fm_tiles(w):
    k, m = w.shape
    t = w.reshape(k // P, P, m // P, P).transpose(2, 0, 1, 3).reshape(-1, 8, P, P)
    return t.transpose(0, 2, 1, 3).reshape(-1, P, CHUNK)


def half_chunks(w):
    k, m = w.shape
    t = w.reshape(4, P, m // P, P).transpose(2, 0, 1, 3).reshape(-1, 8, P, P)
    return t.transpose(0, 2, 1, 3).reshape(-1, P, CHUNK)


def row_chunks(w):
    k, m = w.shape
    return w.reshape(k // 256, 2, P, m // 512, 512).transpose(3, 0, 2, 1, 4).reshape(-1, P, CHUNK)


def vec(v):
    return np.asarray(v).reshape(-1, P).T


def layout(x):
    f = lambda n: np.asarray(x[n])
    w_in = f("dn_w_in")[0]
    heads = []
    for h in range(QK_HEADS):
        at = [1024 + P * h, P * h, 2048 + 2 * P * h, 2048 + 2 * P * h + P, 4096 + 2 * P * h, 4096 + 2 * P * h + P]
        heads.append(np.concatenate([w_in[:, c:c + P] for c in at], axis=1))
    ada = f("ada_w")
    att = f("att_w_in")[0]
    stream = [row_chunks(ada[0]), fm(np.concatenate(heads, axis=1)), fm_tiles(f("dn_w_out")[0]), row_chunks(ada[1]),
              fm(att[:, 0:1024]), fm(att[:, 1536:2560]), fm(att[:, 1024:1536]), fm(f("att_w_out")[0])]
    stream += second_stream(f)
    stream.append(np.zeros((SLOTS, P, CHUNK), np.float32))
    conv = f("dn_conv_w")[0].T.reshape(32, P, 5)
    order = [t for h in range(QK_HEADS) for t in (8 + h, h, 16 + 2 * h, 17 + 2 * h)]
    conv = conv[order].transpose(1, 0, 2).reshape(P, 160)
    parts = {"c": np.stack([vec(x["c"]), vec(x["c_ctx"])], axis=2).reshape(P, 16), "norm_g": vec(x["norm_g"]),
             "ada_b": vec(x["ada_b"]), "conv": conv, "dn_o": vec(x["dn_o_norm_g"]), "qg": vec(x["att_q_norm_g"]),
             "kg": vec(x["att_k_norm_g"]), "final_g": vec(x["final_norm_g"])}
    parts.update(second_cols(f))
    col_at, at = {}, 0
    for n, v in parts.items():
        col_at[n] = (at, v.shape[1])
        at += v.shape[1]
    rows = [f("dn_dt_bias").reshape(-1), f("dn_a_log").reshape(-1)] + second_rows(f)
    both = np.concatenate([f("ctx")[0], f("x")[0]], axis=0)
    arrays = {
        "w": np.concatenate(stream, axis=0),
        "h": both.T.reshape(KT, P, TOK).transpose(1, 0, 2).reshape(P, KT * TOK),
        "cols": np.concatenate(list(parts.values()), axis=1),
        "rows": np.concatenate(rows)[None, :],
        "w_ab": w_in[:, 6144:6208].reshape(KT, P, 64).transpose(1, 0, 2).reshape(P, KT * 64),
        "const": const_array(const_tiles()),
        "rope": rope_tables(),
    }
    arrays.update(second_arrays(f))
    return {n: np.ascontiguousarray(v) for n, v in arrays.items()}, col_at


def second_stream(f):
    w = f("w_in_2")[0]
    rw, hg = 2592, 4384
    pad = np.zeros((D, 2 * P), np.float32)
    down = np.concatenate([f("ffn_w_down_2")[0], np.zeros((2 * P, D), np.float32)], axis=0)
    return [fm(w[:, 0:2560]), fm(np.concatenate([w[:, rw:rw + 1792], pad], axis=1)),
            fm(np.concatenate([w[:, hg:hg + 512], w[:, hg + 1536:hg + 2560]], axis=1)), row_chunks(w[:, hg + 512:hg + 1536]),
            fm(w[:, 6944:10016]), fm(f("w_branch_ssm_2")[0]), half_chunks(f("w_branch_rwkv_2")[0]),
            half_chunks(f("w_branch_hgrn_2")[0]), fm(f("w_out_2")[0]), fm(f("ffn_w_in_2")[0]), fm_tiles(down)]


def second_cols(f):
    conv = f("ssm_conv_w_2")[0][:, 0, :].T.reshape(12, P, 5).transpose(1, 0, 2).reshape(P, 60)
    out = {"norm1_w": vec(f("norm1_w_2")), "ssm_conv": conv, "ssm_conv_b": vec(f("ssm_conv_b_2")),
           "ssm_d": vec(np.repeat(f("ssm_d_2")[0], 64)), "ssm_norm_w": vec(f("ssm_norm_w_2")),
           "rwkv_mu": vec(f("rwkv_mu_2")[0])}
    for n in ("a0", "k_k", "k_a", "r_k"):
        out[n] = vec(f(f"rwkv_{n}_2"))
    for n in ("hgrn_norm_w", "norm2_w", "final_norm_w"):
        out[n] = vec(f(n + "_2"))
    return out


def second_rows(f):
    names = ("ssm_dt_bias", "ssm_a_log", "rwkv_w0", "rwkv_ln_w", "rwkv_ln_b", "hgrn_lb_logits")
    return [f(n + "_2").reshape(-1) for n in names]


def second_arrays(f):
    return {"w_dt": f("w_in_2")[0][:, 2560:2592].reshape(KT, P, 32).transpose(1, 0, 2).reshape(P, KT * 32),
            "w_up": f("rwkv_w_up_2")[0].transpose(1, 0, 2).reshape(64, 1024), "a_up": f("rwkv_a_up_2")[0],
            "g_up": f("rwkv_g_up_2")[0], "const2": const_array(second_tiles())}


def kernel(**inputs):
    from concourse import bacc
    from concourse.bass_utils import run_bass_kernel_spmd

    arrays, col_at = layout(inputs)
    nc = bacc.Bacc("TRN2", target_bir_lowering=False, num_devices=1)
    a = {n: nc.dram_tensor(f"in_{n}", v.shape, F32, kind="ExternalInput").ap() for n, v in arrays.items()}
    out = nc.dram_tensor("out", (P, KT * SEQ), F32, kind="ExternalOutput").ap()
    build(nc, a, out, col_at)
    r = run_bass_kernel_spmd(nc, [{f"in_{n}": v for n, v in arrays.items()}], core_ids=[0])
    got = r.results[0]["out"]
    return got.reshape(P, KT, SEQ).transpose(1, 0, 2).reshape(D, SEQ).T[None]
```

```python
import math
from contextlib import ExitStack, contextmanager

import numpy as np

import concourse.bass as bass
from concourse import mybir

F32 = mybir.dt.float32
ALU = mybir.AluOpType
ACT = mybir.ActivationFunctionType
AX = mybir.AxisListType

P = 128
D = 1024
KT = D // P
CTX = 256
SEQ = 256
TOK = CTX + SEQ
TT = TOK // P
CHUNK = 1024
SLOTS = 6
EPS = 1e-6
LEVELS = 7

QK_HEADS = 8
V_HEADS = 16
DN_GROUP = 6
ATT_Q = 8
ATT_KV = 2

NEG = -1e30


def level_mask(b):
    i = np.arange(P)
    return ((i[:, None] // b) % 2 == 1) & (i[None, :] // b == i[:, None] // b - 1)


def const_tiles():
    i = np.arange(P)
    s, t = i[:, None], i[None, :]
    half = s // 64 == t // 64
    out = {"ident": s == t, "ones": np.ones((P, P)), "mhalf": np.full((P, P), -0.5), "tri_f": s <= t, "tri_b": s >= t}
    for n in range(LEVELS):
        out[f"lev_f{n}"] = level_mask(2 ** n)
    for n in range(LEVELS):
        out[f"lev_b{n}"] = level_mask(2 ** n).T
    out["neg_f"] = np.where(s <= t, 0.0, NEG)
    out["neg_b"] = np.where(s >= t, 0.0, NEG)
    rot = np.zeros((P, P))
    for f in range(P):
        if f % 64 < 32:
            rot[f + 32, f] = -1.0
        else:
            rot[f - 32, f] = 1.0
    out["rot"] = rot
    return out


def second_tiles():
    i = np.arange(P)
    s, t = i[:, None], i[None, :]
    half = s // 64 == t // 64
    zero, ones = np.zeros((P, P)), np.ones((P, P))
    first = const_tiles()
    out = {n: first[n] for n in ("ident", "ones", "mhalf", "tri_f", "tri_b")}
    for d in "bf":
        for n in range(LEVELS):
            out[f"lev_{d}{n}"] = first[f"lev_{d}{n}"]
    for n, m in enumerate((s <= t, ones, zero, s <= t, s >= t, zero, ones, s >= t)):
        out[f"ssd_order{n}"] = m
    for n, m in enumerate((s < t, s <= t, s < t, s <= t, s > t, s >= t, s > t, s >= t)):
        out[f"rw{n}"] = half & m
    out["half"] = half
    out["halves"] = (t < 2) & (s // 64 == t)
    for n in range(LEVELS):
        b = 2 ** n
        odd = (t // b) % 2 == 1
        out[f"hg_f{n}"] = (s // b == t // b) & np.where(odd, s <= t, s > t)
    for n in range(LEVELS):
        out[f"hg_b{n}"] = out[f"hg_f{n}"][::-1, ::-1]
    out["aft"] = s > t
    out["bef"] = s < t
    return out


N_BASE = 5 + 2 * LEVELS
FF = 22

FIRST_NAMES = ("neg_f", "neg_b", "rot")
SECOND_NAMES = list(second_tiles())


def const_array(tiles):
    return np.concatenate([np.asarray(m, np.float32) for m in tiles.values()], axis=1)


def rope_tables():
    pos = np.arange(SEQ)
    inv = 10000.0 ** (-np.arange(0, 64, 2, dtype=np.float32) / np.float32(64))
    ang = np.zeros((P, SEQ), np.float32)
    for f in range(P):
        where = (pos // 64) if f < 64 else (pos % 64)
        ang[f] = where.astype(np.float32) * inv[f % 32]
    return np.concatenate([np.cos(ang), np.sin(ang)], axis=1).astype(np.float32)


class Chain:

    def __init__(self, eng, sem):
        self.eng, self.sem, self.n = eng, sem, {}

    def __call__(self, ins, event=None):
        event = event or self.sem
        ins.then_inc(event, 1)
        self.n[event.num] = self.n.get(event.num, 0) + 1
        self.eng.wait_ge(event, self.n[event.num])


def inverse_root(nc, pool, C, x, ready, done, n=1):
    pool.wait_ge(ready, n)
    nc.gpsimd.tensor_tensor(x, x, C("mhalf")[:, 0:1].to_broadcast(list(x.shape)), ALU.pow).then_inc(done, 1)
    pool.wait_ge(done, n)


def column_sums(nc, C, out, x, n):
    for i in range(n):
        last = nc.tensor.matmul(out[:, i:i + 1], x[:, P * i:P * i + P], C("ones")[:, 0:1], start=True, stop=True)
    return last


def spread(nc, C, out, cols, n):
    for i in range(n):
        last = nc.tensor.matmul(out[:, P * i:P * i + P], cols[:, i:i + 1].to_broadcast([P, P]), C("ident"),
                                start=True, stop=True)
    return last


@contextmanager
def stage(nc, names):
    with ExitStack() as es:
        s = {n: es.enter_context(nc.semaphore(n)) for n in (names + " act_own dve_own pool_own").split()}
        with nc.Block() as block:
            yield s, block
        for n in s:
            nc.sync.sem_clear(s[n])
        nc.all_engine_barrier()


class Stream:

    def __init__(self, nc, w, sbuf, sems):
        self.nc, self.w, self.sbuf, self.sems = nc, w, sbuf, sems
        self.at, self.set, self.ready = 0, 0, 0

    def slot(self, c):
        return self.sbuf[:, self.set, c, :]

    def loaded(self, c):
        return self.sems[self.set][c]

    def load(self, sp, which, c, index):
        src = self.w[bass.ds(index, 1)].rearrange("a p n -> p (a n)")
        sp.dma_start(self.sbuf[:, which, c, :], src).then_inc(self.sems[which][c], 16)

    def begin(self, per_body):
        sp = self.nc.sync
        for c in range(per_body, self.ready):
            sp.wait_ge(self.sems[self.set][c], 16)
            sp.sem_clear(self.sems[self.set][c])
        self.nc.all_engine_barrier()
        for c in range(self.ready, per_body):
            self.load(sp, self.set, c, self.at + c)
        self.ready = per_body

    def ahead(self, sp, n, offset):
        for c in range(n):
            self.load(sp, 1 - self.set, c, offset + self.at + n + c)

    def turn(self, n):
        for c in range(n):
            self.nc.sync.sem_clear(self.sems[self.set][c])
        self.set = 1 - self.set

    def drain(self):
        for c in range(self.ready):
            self.nc.sync.wait_ge(self.sems[self.set][c], 16)
            self.nc.sync.sem_clear(self.sems[self.set][c])
        self.nc.all_engine_barrier()

    def bodies(self, count, per_body, body):
        self.begin(per_body)
        if count >= 2:
            with self.nc.Fori(0, count // 2) as i:
                for half in range(2):
                    body(i * 2 + half, (i * 2 + half) * per_body)
                    self.turn(per_body)
        if count % 2:
            body(count - 1, (count - 1) * per_body)
            self.turn(per_body)
        self.at += count * per_body

    def groups(self, count, per_group, s, block, visitors):
        first = self.set

        @block.sync
        def _(sp):
            def visit(g, h, r):
                other = (first + h + 1) % 2
                if not (isinstance(g, int) and g == 0):
                    sp.wait_ge(s["used"], g)
                if isinstance(g, int) and g == count - 1:
                    for c in range(SLOTS):
                        sp.sem_clear(self.sems[other][c])
                for c in range(per_group):
                    self.load(sp, other, c, g * per_group + (self.at + per_group + c))
            walk(sp, count, visit)

        for decorate, run in visitors:
            decorate(run)

    def wait(self, pe, h, r, c):
        pe.wait_ge(self.sems[(self.set + h) % 2][c], r * 16 + 16)

    def chunk(self, h, c):
        return self.sbuf[:, (self.set + h) % 2, c, :]

    def passed(self, count, per_group):
        for c in range(per_group):
            self.nc.sync.sem_clear(self.sems[(self.set + count - 1) % 2][c])
        self.nc.all_engine_barrier()
        self.set = (self.set + count) % 2
        self.at += count * per_group


class Beside:

    def __init__(self, nc, st, src, dst, per_body, places, s, n, half_tanh=False):
        self.nc, self.st, self.src, self.dst, self.per_body, self.places, self.s, self.n = nc, st, src, dst, per_body, places, s, n
        self.how = {"func": ACT.Tanh, "scale": 0.5} if half_tanh else {"func": ACT.Copy}
        self.summed = self.copied = 0

    def sum_tile(self, pe):
        c = self.summed
        if c == self.per_body:
            return
        pe.wait_ge(self.st.loaded(c), 16)
        if c >= len(self.places):
            pe.wait_ge(self.s["x_out"], c + 1 - len(self.places))
        accumulate(self.nc, self.places[c % len(self.places)], [self.st.slot(c)[:, P * k:P * k + P] for k in range(KT)],
                   [self.src(k) for k in range(KT)]).then_inc(self.s["x_summed"], 1)
        self.summed += 1

    def copy_tile(self, act, link):
        c = self.copied
        if c == self.per_body:
            return
        act.wait_ge(self.s["x_summed"], c + 1)
        out = self.dst[:, bass.ds(self.n * self.per_body + c, 1), :].rearrange("p a t -> p (a t)")
        link(self.nc.scalar.activation(out, self.places[c % len(self.places)], **self.how), self.s["x_out"])
        self.copied += 1


def walk(eng, count, visit):
    for g in range(min(count, 2)):
        visit(g, g % 2, 0)
    pairs = (count - 3) // 2
    if pairs >= 2:
        with eng.Fori(0, pairs) as i:
            for h in range(2):
                visit(i * 2 + (2 + h), h, i + 1)
    for g in range(2 + 2 * pairs if pairs >= 2 else 2, count):
        visit(g, g % 2, g // 2)


def accumulate(nc, out, lhs, rhs):
    n = len(lhs)
    for k in range(n):
        last = nc.tensor.matmul(out, lhs[k], rhs[k], start=(k == 0), stop=(k == n - 1))
    return last


def modulation(nc, st, bank, C, silu_c, rows, mod, bias_cols):

    count = 6
    st.begin(4)
    with stage(nc, "used rows_out turned added") as (s, block):
        def tensor(pe):
            def turn(g, h):
                pe.wait_ge(s["rows_out"], g + 1)
                for j in range(4):
                    mm = nc.tensor.matmul(bank[2 + h][:, 2 * j:2 * j + 2], rows[:, 512 * h + P * j:512 * h + P * j + P],
                                          C("ident")[0:2, 0:2], start=(j == 0), stop=(j == 3), skip_group_check=True)
                mm.then_inc(s["turned"], 1)

            def visit(g, h, r):
                for k in range(KT):
                    if k % 2 == 0:
                        st.wait(pe, h, r, k // 2)
                    at = 512 * (k % 2)
                    mm = nc.tensor.matmul(bank[h][0:2, :], silu_c[:, k, :], st.chunk(h, k // 2)[:, at:at + 512],
                                          start=(k == 0), stop=(k == KT - 1))
                mm.then_inc(s["used"], 1)
                if g >= 1:
                    if g >= 3:
                        pe.wait_ge(s["added"], g - 2)
                    turn(g - 1, 1 - h)
            walk(pe, count, visit)
            pe.wait_ge(s["added"], count - 2)
            turn(count - 1, (count - 1) % 2)

        def vector(dve):
            link = Chain(dve, s["dve_own"])

            def add(g, h):
                dve.wait_ge(s["turned"], g + 1)
                link(nc.vector.tensor_tensor(mod[:, 4 * g:4 * g + 4, :], bank[2 + h][:, 0:8].rearrange("p (j c) -> p j c", c=2),
                                             bias_cols[:, 4 * g:4 * g + 4].unsqueeze(2).to_broadcast([P, 4, 2]), ALU.add), s["added"])

            def visit(g, h, r):
                dve.wait_ge(s["used"], g + 1)
                link(nc.vector.tensor_copy(rows[:, 512 * h:512 * h + 512], bank[h][0:2, :]), s["rows_out"])
                if g >= 1:
                    add(g - 1, 1 - h)
            walk(dve, count, visit)
            add(count - 1, (count - 1) % 2)

        st.groups(count, 4, s, block, ((block.tensor, tensor), (block.vector, vector)))
    st.passed(count, 4)


def feature_norm(nc, bank, C, h, u, g_cols, mod, streams, sq, rs, gs):
    lo, n = streams[0][0], sum(x[1] for x in streams)
    tiles = n // P
    with stage(nc, "squared added summed mean root spread") as (s, block):
        @block.gpsimd
        def _(pool):
            inverse_root(nc, pool, C, rs[:, 0:tiles], s["mean"], s["root"])

        @block.scalar
        def _(act):
            for k in range(KT):
                nc.scalar.activation(sq[:, k, 0:n], h[:, k, lo:lo + n], ACT.Square).then_inc(s["squared"], 1)

        @block.tensor
        def _(pe):
            pe.wait_ge(s["added"], KT - 1)
            column_sums(nc, C, bank[0], sq[:, 0, :], tiles).then_inc(s["summed"], 1)
            pe.wait_ge(s["root"], 1)
            spread(nc, C, bank[1], rs, tiles).then_inc(s["spread"], 1)

        @block.vector
        def _(dve):
            link = Chain(dve, s["dve_own"])
            if mod is not None:
                for _, _, m in streams:
                    link(nc.vector.tensor_scalar(gs[:, :, m], mod[:, 8:16, m], 1.0, None, ALU.add))
                    link(nc.vector.tensor_tensor(gs[:, :, m], gs[:, :, m], g_cols, ALU.mult))
            for k in range(1, KT):
                dve.wait_ge(s["squared"], k + 1)
                link(nc.vector.tensor_tensor(sq[:, 0, 0:n], sq[:, 0, 0:n], sq[:, k, 0:n], ALU.add), s["added"])
            dve.wait_ge(s["summed"], 1)
            link(nc.vector.tensor_scalar(rs[:, 0:tiles], bank[0][:, 0:tiles], 1.0 / D, EPS, ALU.mult, ALU.add), s["mean"])
            dve.wait_ge(s["spread"], 1)
            for k in range(KT):
                for t0, tn, m in streams:
                    scale = gs[:, k, m:m + 1] if mod is not None else g_cols[:, k:k + 1]
                    link(nc.vector.scalar_tensor_tensor(u[:, k, t0:t0 + tn], h[:, k, t0:t0 + tn], scale,
                                                        bank[1][:, t0 - lo:t0 - lo + tn], ALU.mult, ALU.mult))
                    if mod is not None:
                        link(nc.vector.tensor_scalar(u[:, k, t0:t0 + tn], u[:, k, t0:t0 + tn], mod[:, k, m:m + 1],
                                                     None, ALU.add))


def linear(nc, st, bank, count, per_body, src, n_tok, evacuate, k_tiles=KT):
    held = k_tiles if k_tiles < 8 else -(-k_tiles // 8) * 8
    tiles = per_body * 8 // held

    banks = min(8, 2 * tiles)

    def before(q):
        if q >= banks:
            return banks
        return 2 * tiles - banks * ((2 * tiles - 1 - q) // banks)

    st.begin(per_body)
    with stage(nc, "used summed evacuated") as (s, block):
        def tensor(pe):
            def visit(g, h, r):
                for m in range(tiles):
                    q = h * tiles + m
                    if not (isinstance(g, int) and g * tiles + m < before(q)):
                        pe.wait_ge(s["evacuated"], g * tiles + (m + 1 - before(q)))
                    for k in range(k_tiles):
                        c, b = (m * held + k) // 8, (m * held + k) % 8
                        if b == 0 or k == 0:
                            st.wait(pe, h, r, c)
                        mm = nc.tensor.matmul(bank[q % banks][:, 0:n_tok], st.chunk(h, c)[:, P * b:P * b + P], src(k),
                                              start=(k == 0), stop=(k == k_tiles - 1))
                    mm.then_inc(s["summed"] if m < tiles - 1 else s["used"], 1)
            walk(pe, count, visit)

        def vector(dve):
            def visit(g, h, r):
                for m in range(tiles):
                    if m == tiles - 1:
                        dve.wait_ge(s["used"], g + 1)
                    else:
                        dve.wait_ge(s["summed"], g * (tiles - 1) + (m + 1))
                    evacuate(g * tiles + m, bank[(h * tiles + m) % banks]).then_inc(s["evacuated"], 1)
            walk(dve, count, visit)
            dve.wait_ge(s["evacuated"], count * tiles)

        st.groups(count, per_body, s, block, ((block.tensor, tensor), (block.vector, vector)))
    st.passed(count, per_body)


G, NGC, BETA, NEG_EG, EG, BEND, GL = range(7)
QUANT = 7
PER_HEAD = QUANT * 4 * TT


def delta_gates(nc, bank, C, u, w_ab, dt_rows, a_rows, sc, tmp):
    x, e, r, lg, gx = (tmp[:, i, :] for i in range(5))
    q3 = lambda a: a.rearrange("p (t c) -> p t c", t=TT)

    def put(q, src, direction):
        out = sc[:, :, :].rearrange("p h (q j d t) -> p h q j d t", q=QUANT, j=2, d=2)[:, :, q, :, direction, :]
        inp = src.rearrange("p (t d h j) -> p d h j t", t=TT, d=2, j=2)[:, direction]
        return nc.vector.tensor_copy(out, inp)

    with stage(nc, "ab x_ready e_ready ln_ready g_ready sums ex th_ready a_ready done") as (s, block):
        @block.tensor
        def _(pe):
            for t in range(TT):
                for k in range(KT):
                    mm = nc.tensor.matmul(bank[0][:, 64 * t:64 * t + 64], u[:, k, P * t:P * t + P], w_ab[:, k, :],
                                          start=(t == 0 and k == 0), stop=(k == KT - 1), skip_group_check=True)
            mm.then_inc(s["ab"], 1)
            pe.wait_ge(s["g_ready"], 1)
            for t in range(TT):
                for d in range(2):
                    col = 32 * t + 16 * d
                    nc.tensor.matmul(bank[1][:, col:col + 16], C("tri_b" if d else "tri_f"), lg[:, col:col + 16],
                                     start=(col == 0), stop=True, skip_group_check=True)
            mm = nc.tensor.matmul(bank[2][:, 0:128], C("ones"), lg, start=True, stop=True)
            mm.then_inc(s["sums"], 1)

        ab = bank[0][:, 0:256].rearrange("p (t b c) -> p t b c", t=TT, b=2)

        @block.scalar
        def _(act):
            link = Chain(act, s["act_own"])
            act.wait_ge(s["ab"], 1)
            link(nc.scalar.activation(q3(r), ab[:, :, 0, :], ACT.Tanh, scale=0.5), s["th_ready"])
            link(nc.scalar.activation(a_rows, a_rows, ACT.Exp), s["a_ready"])
            act.wait_ge(s["x_ready"], 1)
            link(nc.scalar.activation(e, gx, ACT.Exp), s["e_ready"])
            act.wait_ge(s["x_ready"], 2)
            link(nc.scalar.activation(gx, lg, ACT.Ln), s["ln_ready"])
            act.wait_ge(s["ex"], 1)
            link(nc.scalar.activation(e, bank[1][:, 0:128], ACT.Exp), s["e_ready"])
            link(nc.scalar.activation(x, gx, ACT.Exp), s["e_ready"])
            link(nc.scalar.activation(gx, bank[2][:, 0:128], ACT.Exp), s["e_ready"])

        @block.vector
        def _(dve):
            link = Chain(dve, s["dve_own"])
            dve.wait_ge(s["th_ready"], 1)
            link(nc.vector.tensor_tensor(q3(x), ab[:, :, 1, :], dt_rows.unsqueeze(1).to_broadcast([P, TT, 32]), ALU.add))
            link(nc.vector.scalar_tensor_tensor(gx, x, -1.0, x, ALU.mult, ALU.min), s["x_ready"])
            dve.wait_ge(s["e_ready"], 1)
            link(nc.vector.tensor_scalar(lg, e, 1.0, None, ALU.add), s["x_ready"])
            dve.wait_ge(s["ln_ready"], 1)
            link(nc.vector.tensor_scalar(lg, lg, -1.0, 1.0, ALU.mult, ALU.add))
            link(nc.vector.tensor_tensor(lg, lg, e, ALU.add))
            link(nc.vector.tensor_tensor(lg, lg, gx, ALU.add))
            link(nc.vector.scalar_tensor_tensor(lg, x, 0.0, lg, ALU.max, ALU.add))
            dve.wait_ge(s["a_ready"], 1)
            link(nc.vector.scalar_tensor_tensor(q3(lg), q3(lg), -1.0, a_rows.unsqueeze(1).to_broadcast([P, TT, 32]),
                                                ALU.mult, ALU.mult), s["g_ready"])
            link(nc.vector.tensor_scalar(r, r, 0.5, 0.5, ALU.mult, ALU.add))
            dve.wait_ge(s["sums"], 1)
            for d in range(2):
                link(put(G, lg, d))
                link(put(BETA, r, d))
            link(nc.vector.tensor_scalar(lg, bank[1][:, 0:128], -1.0, None, ALU.mult))
            for d in range(2):
                link(put(NGC, lg, d))
            link(nc.vector.tensor_tensor(gx, lg, bank[2][:, 0:128], ALU.add), s["ex"])
            dve.wait_ge(s["e_ready"], 4)
            for d in range(2):
                link(put(EG, e, d))
                link(put(GL, gx, d))
            link(nc.vector.tensor_scalar(e, e, -1.0, None, ALU.mult))
            link(nc.vector.tensor_tensor(x, x, r, ALU.mult))
            for d in range(2):
                link(put(NEG_EG, e, d))
                link(put(BEND, x, d))


def delta_heads(nc, st, bank, C, u, sc, conv_cols, o_cols, gated, spare):
    order = ((0, 1, 2, 3), (1, 0, 3, 2))
    with ExitStack() as es:
        sb = lambda name, shape: es.enter_context(nc.sbuf_tensor(name, shape, F32))
        raw = sb("raw", [P, 4, 2, SEQ + 4])
        acc = sb("acc", [P, 4, TOK])
        y = sb("y", [P, 4, TOK])
        zs_of = [sb(f"zs{i}", [P, 2, TOK]) for i in range(2)]
        rn = sb("rn", [P, 2, TOK])
        qn = sb("qn", [P, TOK])
        kn = sb("kn", [P, TOK])
        v_t = sb("v_t", [P, TT, 2, P])
        k_t = sb("k_t", [P, TT, P])
        gram_kq = sb("gram_kq", [P, 2, TOK])
        gram, kq = gram_kq[:, 0, :], gram_kq[:, 1, :]
        dec = sb("dec", [P, 2, TOK])
        a_t = sb("a_t", [P, 4, TOK])
        zt = a_t[:, 0:2, :]
        qkd = spare[:, 4:8, :]
        inv = acc
        inv_t = sb("inv_t", [P, 4, TOK])
        prod = y
        hs = sb("hs", [P, PER_HEAD])
        hc = sb("hc", [P, 20])
        state = sb("state", [P, 2, 2 * P])
        resid = rn[:, 0, :].rearrange("p (d e) -> p d e", d=2)
        vn = sb("vn", [P, 2, 2 * P])
        ve = sb("ve", [P, 2, 2 * P])
        qs = rn[:, 1, :].rearrange("p (d e) -> p d e", d=2)
        od = spare[:, 0:4, :].rearrange("p (d a) t -> p d (a t)", d=2).rearrange("p d (t e) -> p d t e", t=TT)
        ms = sb("ms", [P, 2 * TT])
        rc = sb("rc", [P, 2 * TT])
        short = es.enter_context(nc.sbuf_tensor("short", [P, 3 * P], mybir.dt.bfloat16))
        th = y
        sq = gram_kq[:, :, :].rearrange("p a t -> p (a t)")
        o_sq = dec[:, :, :].rearrange("p a e -> p (a e)")

        def col(q, c, t):
            at = q * 4 * TT + c * TT + t
            return hs[:, at:at + 1]

        def tile(a, t):
            return a[:, P * t:P * t + P]

        four = lambda a: a.rearrange("p (t e) -> p t e", t=TT)
        wide = lambda name: C(name).unsqueeze(1).to_broadcast([P, TT, P])

        with stage(nc, "padded") as (s, block):
            @block.gpsimd
            def _(pool):
                nc.gpsimd.memset(raw[:, :, :, :], 0.0).then_inc(s["padded"], 1)
                pool.wait_ge(s["padded"], 1)

            @block.vector
            def _(dve):
                link = Chain(dve, s["dve_own"])
                for n, name in enumerate(("ident", "neg_f", "neg_b")):
                    link(nc.vector.tensor_copy(short[:, P * n:P * n + P], C(name)))

        class Front:

            def __init__(self, s, zs, places):
                self.s, self.zs, self.places, self.at = s, zs, places, 0

            def products(self, pe, count):
                for at in range(self.at, self.at + count):
                    m, k = at // KT, at % KT
                    if k == 0:
                        pe.wait_ge(st.loaded(m), 16)
                        if m >= len(self.places):
                            pe.wait_ge(self.s["raw_out"], m + 1 - len(self.places))
                    mm = nc.tensor.matmul(self.places[m % len(self.places)][:, :], st.slot(m)[:, P * k:P * k + P], u[:, k, :],
                                          start=(k == 0), stop=(k == KT - 1))
                    if k == KT - 1:
                        mm.then_inc(self.s["proj"], 1)
                self.at += count

            def keep(self, act, link, m):
                act.wait_ge(self.s["proj"], m + 1)
                bank_m = self.places[m % len(self.places)]
                link(nc.scalar.activation(raw[:, m, :, 2:SEQ + 2], bank_m[:, :].rearrange("p (a t) -> p a t", a=2),
                                          ACT.Copy), self.s["raw_out"])

            def tanh(self, act, link, m):
                act.wait_ge(self.s["conv"], m + 1)
                link(nc.scalar.activation(th[:, m, :], acc[:, m, :], ACT.Tanh, scale=0.5), self.s["tanh"])

            def gate(self, act, link, j):
                act.wait_ge(self.s["proj"], 5 + j)
                bank_m = self.places[(4 + j) % len(self.places)]
                link(nc.scalar.activation(self.zs[:, j, :], bank_m[:, :], ACT.Copy))
                link(nc.scalar.activation(zt[:, j, :], bank_m[:, :], ACT.Tanh, scale=0.5))

            def conv(self, dve, link, m):
                dve.wait_ge(self.s["raw_out"], m + 1)
                out = acc[:, m, :].rearrange("p (a t) -> p a t", a=2)
                link(nc.vector.tensor_scalar(out, raw[:, m, :, 0:SEQ], hc[:, 5 * m:5 * m + 1], None, ALU.mult))
                for i in range(1, 5):
                    link(nc.vector.scalar_tensor_tensor(out, raw[:, m, :, i:i + SEQ], hc[:, 5 * m + i:5 * m + i + 1],
                                                        out, ALU.mult, ALU.add), self.s["conv"] if i == 4 else None)

            def silu(self, dve, link, m):
                dve.wait_ge(self.s["tanh"], m + 1)
                link(nc.vector.scalar_tensor_tensor(y[:, m, :], th[:, m, :], 1.0, acc[:, m, :], ALU.add, ALU.mult),
                     self.s["silu"])

            def square(self, act, link, m):
                act.wait_ge(self.s["silu"], m + 1)
                link(nc.scalar.activation(sq[:, TOK * m:TOK * m + TOK], y[:, m, :], ACT.Square), self.s["squared"])

            def sums(self, pe, where):
                pe.wait_ge(self.s["squared"], 2)
                column_sums(nc, C, where, sq, 2 * TT).then_inc(self.s["ssum"], 1)

            def mean(self, dve, link, where):
                dve.wait_ge(self.s["ssum"], 1)
                link(nc.vector.tensor_scalar(rc[:, :], where[:, 0:2 * TT], 4 * EPS, None, ALU.add), self.s["mean"])

        st.begin(DN_GROUP)
        with stage(nc, "proj raw_out conv tanh silu squared ssum mean root") as (s, block):
            front = Front(s, zs_of[0], bank[0:6])

            @block.sync
            def _(sp):
                st.ahead(sp, DN_GROUP, 0)

            @block.tensor
            def _(pe):
                front.products(pe, DN_GROUP * KT)
                front.sums(pe, bank[6])

            @block.gpsimd
            def _(pool):
                inverse_root(nc, pool, C, rc[:, :], s["mean"], s["root"])

            @block.scalar
            def _(act):
                link = Chain(act, s["act_own"])
                front.keep(act, link, 0)
                front.keep(act, link, 1)
                front.tanh(act, link, 0)
                front.keep(act, link, 2)
                front.tanh(act, link, 1)
                front.keep(act, link, 3)
                front.tanh(act, link, 2)
                front.gate(act, link, 0)
                front.square(act, link, 0)
                front.square(act, link, 1)
                front.tanh(act, link, 3)
                front.gate(act, link, 1)

            @block.vector
            def _(dve):
                link = Chain(dve, s["dve_own"])
                link(nc.vector.tensor_copy(hc[:, :], conv_cols[:, 0:20]))
                front.conv(dve, link, 0)
                for m in range(1, 4):
                    front.conv(dve, link, m)
                    front.silu(dve, link, m - 1)
                front.silu(dve, link, 3)
                front.mean(dve, link, bank[6])
        st.turn(DN_GROUP)
        st.at += DN_GROUP
        heads = []

        def body(n, offset, more=True):
            zs = zs_of[len(heads) % 2]
            heads.append(n)
            names = ("proj raw_out conv tanh silu squared ssum kq_norm turned turned_out grams kq_done scal "
                     "rows dec_ready dec_used a_done p_ready bc_done t_ready zero ks_done qs_done r_ready "
                     "qs_out x_done vn_ready os_done s_ready o_sum o_sqd o_norm o_turned z_ready mean root spread o_mean o_root t_turned t_out")
            with stage(nc, names) as (s, block):
                front = Front(s, zs_of[len(heads) % 2], bank[5:8])

                @block.sync
                def _(sp):
                    if more:
                        st.ahead(sp, DN_GROUP, offset)

                @block.gpsimd
                def _(pool):
                    link = Chain(pool, s["pool_own"])
                    link(nc.gpsimd.memset(state[:, :, :], 0.0), s["zero"])
                    for j in range(2):
                        link(nc.gpsimd.tensor_tensor(zt[:, j, :], zt[:, j, :], zs[:, j, :], ALU.mult))
                        link(nc.gpsimd.tensor_tensor(zs[:, j, :], zs[:, j, :], zt[:, j, :], ALU.add), s["z_ready"])
                    inverse_root(nc, pool, C, ms[:, :], s["o_mean"], s["o_root"])
                    if more:
                        inverse_root(nc, pool, C, rc[:, :], s["mean"], s["root"])

                @block.tensor
                def _(pe):
                    def rows(c):
                        d, b = c % 2, bank[c % 2]
                        nc.tensor.matmul(four(b[:, :]), short[:, 0:P],
                                         short[:, P + P * d:2 * P + P * d].unsqueeze(1).to_broadcast([P, TT, P]), start=True,
                                         stop=False, skip_group_check=True)
                        for t in range(TT):
                            mm = nc.tensor.matmul(tile(b, t), col(G, c, t).to_broadcast([P, P]),
                                                  C("tri_b" if d else "tri_f"), start=False, stop=True,
                                                  skip_group_check=True)
                        mm.then_inc(s["rows"], 1)

                    for m in range(2):
                        spread(nc, C, bank[2 + m], rc[:, TT * m:TT * m + TT], TT).then_inc(s["spread"], 1)
                    pe.wait_ge(s["scal"], 1)
                    rows(0)
                    pe.wait_ge(s["kq_norm"], 1)
                    for t in range(TT):
                        mm = nc.tensor.transpose(tile(bank[6], t), tile(kn, t), C("ident"))
                    mm.then_inc(s["turned"], 1)
                    for t in range(TT):
                        mm = nc.tensor.matmul(tile(bank[7], t), tile(kn, t), tile(kn, t), start=True, stop=True)
                    mm.then_inc(s["grams"], 1)
                    pe.wait_ge(s["kq_norm"], 2)
                    for t in range(TT):
                        mm = nc.tensor.matmul(tile(bank[2], t), tile(kn, t), tile(qn, t), start=True, stop=True)
                    mm.then_inc(s["grams"], 1)
                    rows(1)
                    for j in range(2):
                        for t in range(TT):
                            mm = nc.tensor.transpose(tile(bank[4 + j], t), tile(y[:, 2 + j, :], t), C("ident"))
                        mm.then_inc(s["turned"], 1)
                    for c in range(2, 4):
                        pe.wait_ge(s["dec_ready"], c - 1)
                        rows(c)
                    for c in range(4):
                        pe.wait_ge(s["dec_used"], c + 1)
                        if c == 0:
                            pe.wait_ge(s["kq_done"], 2)
                        pe.wait_ge(s["dec_ready"], 4)
                        for t in range(TT):
                            mm = nc.tensor.transpose(tile(bank[c], t), tile(a_t[:, c, :], t), C("ident"))
                        mm.then_inc(s["a_done"], 1)
                    pe.wait_ge(s["turned_out"], 3)

                    def border(lv, c):
                        pe.wait_ge(s["t_ready"], 4 * lv + c - 3)
                        for t in range(TT):
                            mm = nc.tensor.matmul(tile(bank[c], t), tile(a_t[:, c, :], t), tile(inv[:, c, :], t), start=True, stop=True)
                        mm.then_inc(s["a_done"], 1)

                    def update(lv, c):
                        q = 4 * lv + c
                        pe.wait_ge(s["p_ready"], q - 3)
                        if q >= 6:
                            pe.wait_ge(s["t_ready"], q - 1)
                        pe.wait_ge(s["t_out"], 4 * (LEVELS - 1) if lv == LEVELS - 1 else q - 3)
                        for t in range(TT):
                            if lv < LEVELS - 1:
                                mm = nc.tensor.matmul(tile(bank[4 + c % 2], t), tile(inv_t[:, c, :], t),
                                                      tile(prod[:, c, :], t), start=True, stop=True)
                            else:
                                mm = nc.tensor.matmul(tile(bank[6 + c % 2], t), tile(prod[:, c, :], t),
                                                      tile(inv_t[:, c, :], t), start=True, stop=True)
                        mm.then_inc(s["bc_done"], 1)

                    def turn(lv, c):
                        q = 4 * lv + c
                        pe.wait_ge(s["t_ready"], q + 1)
                        if q >= 2:
                            pe.wait_ge(s["t_out"], q - 1)
                        for t in range(TT):
                            mm = nc.tensor.transpose(tile(bank[6 + c % 2], t), tile(inv[:, c, :], t), C("ident"))
                        mm.then_inc(s["t_turned"], 1)

                    for c in range(3):
                        turn(0, c)
                    for lv in range(1, LEVELS):
                        for c in range(4):
                            border(lv, c)
                            if c == 0:
                                turn(lv - 1, 3)
                        for c in range(4):
                            update(lv, c)
                            if lv < LEVELS - 1 and c >= 1:
                                turn(lv, c - 1)
                    pe.wait_ge(s["t_ready"], 4 * LEVELS)
                    for step in range(TT):
                        for d in range(2):
                            r, t = 2 * step + d, order[d][step]
                            if step == 0:
                                pe.wait_ge(s["zero"], 1)
                            else:
                                pe.wait_ge(s["s_ready"], r - 1)
                                pe.wait_ge(s["qs_out"], 2 * step)
                            at = 2 * P * d
                            nc.tensor.matmul(bank[0][:, at:at + 2 * P], tile(kn, t), state[:, d, :],
                                             start=True, stop=True).then_inc(s["ks_done"], 1)
                            nc.tensor.matmul(bank[1][:, at:at + 2 * P], tile(qn, t), state[:, d, :],
                                             start=True, stop=True).then_inc(s["qs_done"], 1)
                        if more:
                            front.products(pe, 3)
                        for d in range(2):
                            r, t = 2 * step + d, order[d][step]
                            pe.wait_ge(s["r_ready"], r + 1)
                            for j in range(2):
                                mm = nc.tensor.matmul(tile(bank[2], 2 * d + j), tile(inv_t[:, 2 * j + d, :], t),
                                                      tile(resid[:, d, :], j), start=True, stop=True)
                            mm.then_inc(s["x_done"], 1)
                        if more:
                            front.products(pe, 3)
                        for d in range(2):
                            r, t = 2 * step + d, order[d][step]
                            pe.wait_ge(s["vn_ready"], r + 1)
                            for j in range(2):
                                nc.tensor.matmul(tile(bank[3 + d], j), tile(qkd[:, 2 * j + d, :], t),
                                                 tile(vn[:, d, :], j), start=True, stop=True)
                            nc.tensor.matmul(bank[3 + d][:, 2 * P:4 * P], k_t[:, t, :], ve[:, d, :],
                                             start=True, stop=True).then_inc(s["os_done"], 1)
                        if more:
                            front.products(pe, 3)
                    if more:
                        front.products(pe, DN_GROUP * KT - 9 * TT)
                        front.sums(pe, bank[2])
                    pe.wait_ge(s["o_norm"], 1)
                    for j in range(2):
                        for t in range(TT):
                            mm = nc.tensor.transpose(tile(bank[j], t), od[:, 0, t, P * j:P * j + P], C("ident"))
                        mm.then_inc(s["o_turned"], 1)

                @block.scalar
                def _(act):
                    link = Chain(act, s["act_own"])

                    def decays(c):
                        act.wait_ge(s["rows"], c + 1)
                        if c >= 2:
                            act.wait_ge(s["dec_used"], c - 1)
                        for t in range(TT):
                            link(nc.scalar.activation(tile(dec[:, c % 2, :], t), tile(bank[c % 2], t), ACT.Exp,
                                                      bias=col(NGC, c, t)), s["dec_ready"] if t == TT - 1 else None)

                    decays(0)
                    act.wait_ge(s["grams"], 1)
                    link(nc.scalar.activation(gram[:, :], bank[7][:, :], ACT.Copy), s["kq_done"])
                    act.wait_ge(s["grams"], 2)
                    link(nc.scalar.activation(kq[:, :], bank[2][:, :], ACT.Copy), s["kq_done"])
                    decays(1)
                    decays(2)
                    act.wait_ge(s["turned"], 1)
                    link(nc.scalar.activation(k_t[:, :, :], four(bank[6][:, :]), ACT.Copy), s["turned_out"])
                    decays(3)
                    for j in range(2):
                        act.wait_ge(s["turned"], j + 2)
                        link(nc.scalar.activation(v_t[:, :, j, :], four(bank[4 + j][:, :]), ACT.Copy, scale=0.5), s["turned_out"])
                    for j in range(4 * (LEVELS - 1)):
                        act.wait_ge(s["t_turned"], j + 1)
                        link(nc.scalar.activation(inv_t[:, j % 4, :], bank[6 + j % 2][:, :], ACT.Copy), s["t_out"])
                    for step in range(TT):
                        act.wait_ge(s["qs_done"], 2 * step + 2)
                        for d in range(2):
                            r, t = 2 * step + d, order[d][step]
                            for j in range(2):
                                link(nc.scalar.activation(tile(qs[:, d, :], j), tile(bank[1], 2 * d + j), ACT.Copy,
                                                          scale=col(EG, 2 * j + d, t)), s["qs_out"] if j else None)
                        if more and step >= 1:
                            front.keep(act, link, step - 1)
                        act.wait_ge(s["x_done"], 2 * step + 2)
                        for d in range(2):
                            r, t = 2 * step + d, order[d][step]
                            for j in range(2):
                                link(nc.scalar.activation(tile(vn[:, d, :], j), tile(bank[2], 2 * d + j), ACT.Copy,
                                                          scale=col(BETA, 2 * j + d, t)))
                                link(nc.scalar.activation(tile(ve[:, d, :], j), tile(bank[2], 2 * d + j), ACT.Copy,
                                                          scale=col(BEND, 2 * j + d, t)), s["vn_ready"] if j else None)
                        if more and step >= 2:
                            front.tanh(act, link, step - 2)
                    if more:
                        front.keep(act, link, 3)
                    act.wait_ge(s["o_sum"], 1)
                    link(nc.scalar.activation(o_sq, od[:, 0, :, :].rearrange("p t e -> p (t e)"), ACT.Square), s["o_sqd"])
                    if more:
                        front.square(act, link, 0)
                        front.square(act, link, 1)
                        front.tanh(act, link, 2)
                        front.tanh(act, link, 3)
                        act.wait_ge(s["z_ready"], 2)
                        front.gate(act, link, 0)
                        front.gate(act, link, 1)

                @block.vector
                def _(dve):
                    link = Chain(dve, s["dve_own"])
                    link(nc.vector.tensor_copy(hs[:, :], sc[:, bass.ds(n, 1), :].rearrange("p a c -> p (a c)")), s["scal"])
                    if more:
                        link(nc.vector.tensor_copy(hc[:, :], conv_cols[:, bass.ds(n * 20 + 20, 20)]))

                    def scale(m, out, factor):
                        dve.wait_ge(s["spread"], m + 1)
                        link(nc.vector.scalar_tensor_tensor(out[:, :], y[:, m, :], factor, bank[2 + m][:, :], ALU.mult, ALU.mult),
                             s["kq_norm"])

                    scale(0, kn, 1.0)
                    scale(1, qn, P ** -0.5)
                    for c in range(4):
                        if c == 0:
                            dve.wait_ge(s["kq_done"], 2)
                            dve.wait_ge(s["z_ready"], 2)
                        dve.wait_ge(s["dec_ready"], c + 1)
                        for t in range(TT):
                            link(nc.vector.scalar_tensor_tensor(tile(a_t[:, c, :], t), tile(gram, t), col(BETA, c, t),
                                                                tile(dec[:, c % 2, :], t), ALU.mult, ALU.mult))
                        link(nc.vector.tensor_tensor(qkd[:, c, :], kq[:, :], dec[:, c % 2, :], ALU.mult), s["dec_used"])
                    for c in range(4):
                        dve.wait_ge(s["a_done"], c + 1)
                        link(nc.vector.tensor_tensor(four(inv[:, c, :]), four(bank[c][:, :]), wide(f"lev_{'fb'[c % 2]}0"), ALU.mult))
                        link(nc.vector.tensor_tensor(four(inv[:, c, :]), wide("ident"), four(inv[:, c, :]), ALU.subtract), s["t_ready"])
                    for lv in range(1, LEVELS):
                        for c in range(4):
                            dve.wait_ge(s["a_done"], 4 * lv + c + 1)
                            link(nc.vector.tensor_tensor(four(prod[:, c, :]), four(bank[c][:, :]),
                                                         wide(f"lev_{'fb'[c % 2]}{lv}"), ALU.mult), s["p_ready"])
                        for c in range(4):
                            dve.wait_ge(s["bc_done"], 4 * lv + c - 3)
                            if lv < LEVELS - 1:
                                link(nc.vector.tensor_tensor(inv[:, c, :], inv[:, c, :], bank[4 + c % 2][:, :], ALU.subtract), s["t_ready"])
                            else:
                                link(nc.vector.tensor_tensor(inv_t[:, c, :], inv_t[:, c, :], bank[6 + c % 2][:, :], ALU.subtract), s["t_ready"])
                    for step in range(TT):
                        dve.wait_ge(s["ks_done"], 2 * step + 2)
                        for d in range(2):
                            r, t = 2 * step + d, order[d][step]
                            for j in range(2):
                                link(nc.vector.scalar_tensor_tensor(tile(resid[:, d, :], j), tile(bank[0], 2 * d + j),
                                                                    col(NEG_EG, 2 * j + d, t), v_t[:, t, j, :], ALU.mult, ALU.add),
                                     s["r_ready"] if j else None)
                        if more and step == 3:
                            front.silu(dve, link, 0)
                            front.conv(dve, link, 2)
                        for d in range(2):
                            r, t = 2 * step + d, order[d][step]
                            dve.wait_ge(s["os_done"], r + 1)
                            dve.wait_ge(s["qs_out"], r + 1)
                            for j in range(2):
                                link(nc.vector.scalar_tensor_tensor(tile(state[:, d, :], j), tile(state[:, d, :], j),
                                                                    col(GL, 2 * j + d, t), tile(bank[3 + d], 2 + j), ALU.mult, ALU.add))
                            link(nc.vector.tensor_tensor(od[:, d, t, :], bank[3 + d][:, 0:2 * P], qs[:, d, :], ALU.add), s["s_ready"])
                        if more and step in (1, 2):
                            front.conv(dve, link, step - 1)
                    o3 = od[:, 0, :, :].rearrange("p t (j e) -> p (t j) e", j=2)
                    link(nc.vector.tensor_tensor(od[:, 0, :, :], od[:, 0, :, :], od[:, 1, :, :], ALU.add), s["o_sum"])
                    if more:
                        front.silu(dve, link, 1)
                    dve.wait_ge(s["o_sqd"], 1)
                    link(nc.vector.tensor_reduce(ms[:, :], o_sq.rearrange("p (a e) -> p a e", e=P), AX.X, ALU.add))
                    link(nc.vector.tensor_scalar(ms[:, :], ms[:, :], 1.0 / P, EPS, ALU.mult, ALU.add), s["o_mean"])
                    if more:
                        front.conv(dve, link, 3)
                        front.silu(dve, link, 2)
                    dve.wait_ge(s["o_root"], 1)
                    link(nc.vector.tensor_tensor(o3, o3, ms[:, :].unsqueeze(2).to_broadcast([P, 2 * TT, P]), ALU.mult), s["o_norm"])
                    if more:
                        front.silu(dve, link, 3)
                        front.mean(dve, link, bank[2])
                    for j in range(2):
                        dve.wait_ge(s["o_turned"], j + 1)
                        dve.wait_ge(s["z_ready"], j + 1)
                        out = gated[:, bass.ds(n * 2 + j, 1), :].rearrange("p a t -> p (a t)")
                        link(nc.vector.scalar_tensor_tensor(out, bank[j][:, :], o_cols, zs[:, j, :], ALU.mult, ALU.mult))

        st.bodies(QK_HEADS - 1, DN_GROUP, body)
        body(QK_HEADS - 1, 0, more=False)


def attention_keys(nc, bank, C, pkv, kg, rope, kf, v_t, sq, rs):
    with stage(nc, "sq sm kn rot turned mean root") as (s, block):
        @block.gpsimd
        def _(pool):
            inverse_root(nc, pool, C, rs[:, 0:ATT_KV * TT], s["mean"], s["root"])

        @block.scalar
        def _(act):
            link = Chain(act, s["act_own"])
            for h in range(ATT_KV):
                link(nc.scalar.activation(sq[:, TOK * h:TOK * h + TOK], pkv[:, h, :], ACT.Square), s["sq"])
            for h in range(ATT_KV):
                act.wait_ge(s["turned"], h + 1)
                link(nc.scalar.activation(v_t[:, h, :, :], bank[4 + h][:, :].rearrange("p (t e) -> p t e", t=TT), ACT.Copy))

        @block.tensor
        def _(pe):
            for h in range(ATT_KV):
                for t in range(TT):
                    mm = nc.tensor.transpose(bank[4 + h][:, P * t:P * t + P], pkv[:, ATT_KV + h, P * t:P * t + P], C("ident"))
                mm.then_inc(s["turned"], 1)
            pe.wait_ge(s["sq"], 2)
            column_sums(nc, C, bank[7], sq, ATT_KV * TT).then_inc(s["sm"], 1)
            pe.wait_ge(s["root"], 1)
            for h in range(ATT_KV):
                spread(nc, C, bank[h], rs[:, TT * h:TT * h + TT], TT).then_inc(s["sm"], 1)
            for h in range(ATT_KV):
                pe.wait_ge(s["kn"], h + 1)
                nc.tensor.matmul(bank[2 + h][:, 0:SEQ], C("rot"), kf[:, h, CTX:TOK], start=True, stop=True).then_inc(s["rot"], 1)

        @block.vector
        def _(dve):
            link = Chain(dve, s["dve_own"])
            dve.wait_ge(s["sm"], 1)
            link(nc.vector.tensor_scalar(rs[:, 0:ATT_KV * TT], bank[7][:, 0:ATT_KV * TT], 1.0 / P, EPS, ALU.mult, ALU.add), s["mean"])
            for h in range(ATT_KV):
                dve.wait_ge(s["sm"], h + 2)
                link(nc.vector.scalar_tensor_tensor(kf[:, h, :], pkv[:, h, :], kg, bank[h][:, :], ALU.mult, ALU.mult), s["kn"])
            for h in range(ATT_KV):
                dve.wait_ge(s["rot"], h + 1)
                link(nc.vector.tensor_tensor(rs[:, 0:SEQ], bank[2 + h][:, 0:SEQ], rope[:, SEQ:2 * SEQ], ALU.mult))
                link(nc.vector.tensor_tensor(kf[:, h, CTX:TOK], kf[:, h, CTX:TOK], rope[:, 0:SEQ], ALU.mult))
                link(nc.vector.tensor_tensor(kf[:, h, CTX:TOK], kf[:, h, CTX:TOK], rs[:, 0:SEQ], ALU.add))


def attention_heads(nc, bank, C, pqz, qg, rope, kf, v_t, gated):
    with ExitStack() as es:
        sb = lambda name, shape: es.enter_context(nc.sbuf_tensor(name, shape, F32))
        q = sb("att_q", [P, 2, SEQ])
        qsq = sb("att_qsq", [P, 2 * SEQ])
        rs = sb("att_rs", [P, 2 * SEQ])
        z = sb("att_z", [P, 2, SEQ])
        zt = sb("att_zt", [P, 2, SEQ])
        v = sb("att_v", [P, TT, P])
        pr = sb("att_pr", [P, 4, TOK])
        pt = sb("att_pt", [P, 2, TT, SEQ])
        mx = sb("att_mx", [P, 4])
        sm = sb("att_sm", [P, 4])
        flat = lambda a: a[:, :, :].rearrange("p a t -> p (a t)")
        two = lambda a: a.rearrange("p (a t) -> p a t", a=2)

        with nc.Fori(0, ATT_Q // 2) as i:
            names = "q_in q_sq q_sum q_norm q_rot q_ready scores negmax exped probs turned turned_out out z_ready mean root"
            with stage(nc, names) as (s, block):
                @block.gpsimd
                def _(pool):
                    inverse_root(nc, pool, C, rs[:, 0:4], s["mean"], s["root"])

                @block.tensor
                def _(pe):
                    pe.wait_ge(s["q_sq"], 1)
                    column_sums(nc, C, bank[2], qsq, 4).then_inc(s["q_sum"], 1)
                    pe.wait_ge(s["root"], 1)
                    spread(nc, C, bank[0], rs, 4).then_inc(s["q_sum"], 1)
                    pe.wait_ge(s["q_norm"], 1)
                    nc.tensor.matmul(bank[1][:, :], C("rot"), flat(q), start=True, stop=True).then_inc(s["q_rot"], 1)
                    pe.wait_ge(s["q_ready"], 1)
                    for n in range(4):
                        nc.tensor.matmul(bank[n][:, :], q[:, n // 2, P * (n % 2):P * (n % 2) + P],
                                         kf[:, bass.ds(i // 2, 1), :].rearrange("p a t -> p (a t)"),
                                         start=True, stop=True).then_inc(s["scores"], 1)
                    for n in range(4):
                        pe.wait_ge(s["probs"], n + 1)
                        if n >= 2:
                            pe.wait_ge(s["turned_out"], n - 1)
                        for t in range(TT):
                            mm = nc.tensor.transpose(bank[4 + n % 2][:, P * t:P * t + P], pr[:, n, P * t:P * t + P], C("ident"))
                        mm.then_inc(s["turned"], 1)
                    for j in range(2):
                        pe.wait_ge(s["turned_out"], 2 * j + 2)
                        accumulate(nc, bank[6 + j][:, 0:SEQ], [v[:, t, :] for t in range(TT)],
                                   [pt[:, j, t, :] for t in range(TT)]).then_inc(s["out"], 1)

                @block.scalar
                def _(act):
                    link = Chain(act, s["act_own"])
                    act.wait_ge(s["q_in"], 1)
                    link(nc.scalar.activation(qsq[:, :], flat(q), ACT.Square), s["q_sq"])
                    link(nc.scalar.activation(flat(zt), flat(z), ACT.Tanh, scale=0.5), s["z_ready"])
                    for n in range(4):
                        act.wait_ge(s["negmax"], n + 1)
                        link(nc.scalar.activation(pr[:, n, :], bank[n][:, :], ACT.Exp, bias=mx[:, n:n + 1],
                                                  scale=P ** -0.5, accum_out=sm[:, n:n + 1]), s["exped"])
                    for n in range(4):
                        act.wait_ge(s["turned"], n + 1)
                        t0 = P * (n % 2)
                        link(nc.scalar.activation(pt[:, n // 2, :, t0:t0 + P], bank[4 + n % 2][:, :].rearrange("p (t e) -> p t e", t=TT),
                                                  ACT.Copy), s["turned_out"])

                @block.vector
                def _(dve):
                    link = Chain(dve, s["dve_own"])
                    link(nc.vector.tensor_copy(q[:, :, :], pqz[:, bass.ds(i * 2, 2), :]))
                    link(nc.vector.tensor_copy(z[:, :, :], pqz[:, bass.ds(i * 2 + ATT_Q, 2), :]), s["q_in"])
                    link(nc.vector.tensor_copy(v[:, :, :], v_t[:, bass.ds(i // 2, 1), :, :].rearrange("p a t e -> p (a t) e")))
                    dve.wait_ge(s["q_sum"], 1)
                    link(nc.vector.tensor_scalar(rs[:, 0:4], bank[2][:, 0:4], 1.0 / P, EPS, ALU.mult, ALU.add), s["mean"])
                    dve.wait_ge(s["q_sum"], 2)
                    link(nc.vector.scalar_tensor_tensor(flat(q), flat(q), qg, bank[0][:, :], ALU.mult, ALU.mult), s["q_norm"])
                    dve.wait_ge(s["q_rot"], 1)
                    link(nc.vector.tensor_tensor(two(rs[:, :]), two(bank[1][:, :]), rope[:, SEQ:2 * SEQ].unsqueeze(1).to_broadcast([P, 2, SEQ]), ALU.mult))
                    link(nc.vector.tensor_tensor(q[:, :, :], q[:, :, :], rope[:, 0:SEQ].unsqueeze(1).to_broadcast([P, 2, SEQ]), ALU.mult))
                    link(nc.vector.tensor_tensor(flat(q), flat(q), rs[:, :], ALU.add), s["q_ready"])
                    for n in range(4):
                        dve.wait_ge(s["scores"], n + 1)
                        link(nc.vector.reduce_max(mx[:, n:n + 1], bank[n][:, :], AX.X))
                        link(nc.vector.tensor_scalar(mx[:, n:n + 1], mx[:, n:n + 1], -P ** -0.5, None, ALU.mult), s["negmax"])
                    dve.wait_ge(s["z_ready"], 1)
                    link(nc.vector.scalar_tensor_tensor(flat(z), flat(zt), 1.0, flat(z), ALU.add, ALU.mult))
                    for n in range(4):
                        dve.wait_ge(s["exped"], n + 1)
                        link(nc.vector.reciprocal(sm[:, n:n + 1], sm[:, n:n + 1]))
                        link(nc.vector.tensor_scalar(pr[:, n, :], pr[:, n, :], sm[:, n:n + 1], None, ALU.mult), s["probs"])
                    for j in range(2):
                        dve.wait_ge(s["out"], j + 1)
                        link(nc.vector.scalar_tensor_tensor(gated[:, bass.ds(i * 2 + j, 1), 0:SEQ].rearrange("p a t -> p (a t)"),
                                                            bank[6 + j][:, 0:SEQ], 0.5, z[:, j, :], ALU.mult, ALU.mult))


SSM_HEADS = 16
RW = 4
HG = 4
ST = SEQ // P
RWKV_DECAY = 0.6065306597
RWKV_LN_EPS = 64e-5


def flat(a):
    return a.rearrange("p a b -> p (a b)")


def sigmoid_of_tanh(nc, out, th):
    return nc.vector.tensor_scalar(out, th, 0.5, 0.5, ALU.mult, ALU.add)


S_AC, S_DT = range(2)
S_PER_HEAD = 2 * 2 * ST


def ssd_steps(nc, bank, C, u, w_dt, dt_rows, a_rows, sc, tmp):
    n = ST * 32
    x, e, lg, gx, dt = (tmp[:, i, 0:n] for i in range(5))
    q3 = lambda a: a.rearrange("p (t c) -> p t c", t=ST)

    def put(q, src, d):
        out = sc[:, :, :].rearrange("p h (q d t) -> p q d h t", q=2, d=2)[:, q, d, :, :]
        return nc.vector.tensor_copy(out, src.rearrange("p (t d h) -> p d h t", t=ST, d=2)[:, d])

    with stage(nc, "raw x_ready e_ready ln_ready g_ready sums a_ready") as (s, block):
        @block.tensor
        def _(pe):
            for t in range(ST):
                for k in range(KT):
                    mm = nc.tensor.matmul(bank[0][:, 32 * t:32 * t + 32], u[:, k, CTX + P * t:CTX + P * t + P], w_dt[:, k, :],
                                          start=(t == 0 and k == 0), stop=(k == KT - 1), skip_group_check=True)
            mm.then_inc(s["raw"], 1)
            pe.wait_ge(s["g_ready"], 1)
            for d in range(2):
                for t in range(ST):
                    for src in range(ST):
                        if (src > t) if d == 0 else (src < t):
                            continue
                        w = "ones" if src != t else ("tri_b" if d else "tri_f")
                        at = 32 * t + 16 * d
                        mm = nc.tensor.matmul(bank[1][:, at:at + 16], C(w), gx[:, 32 * src + 16 * d:32 * src + 16 * d + 16],
                                              start=(d == 0 and t == 0 and src == 0), stop=True, skip_group_check=True)
            mm.then_inc(s["sums"], 1)

        @block.scalar
        def _(act):
            link = Chain(act, s["act_own"])
            link(nc.scalar.activation(a_rows, a_rows, ACT.Exp), s["a_ready"])
            act.wait_ge(s["x_ready"], 1)
            link(nc.scalar.activation(e, gx, ACT.Exp), s["e_ready"])
            act.wait_ge(s["x_ready"], 2)
            link(nc.scalar.activation(gx, lg, ACT.Ln), s["ln_ready"])

        @block.vector
        def _(dve):
            link = Chain(dve, s["dve_own"])
            dve.wait_ge(s["raw"], 1)
            link(nc.vector.tensor_tensor(q3(x), q3(bank[0][:, 0:n]), dt_rows.unsqueeze(1).to_broadcast([P, ST, 32]), ALU.add))
            link(nc.vector.scalar_tensor_tensor(gx, x, -1.0, x, ALU.mult, ALU.min), s["x_ready"])
            dve.wait_ge(s["e_ready"], 1)
            link(nc.vector.tensor_scalar(lg, e, 1.0, None, ALU.add), s["x_ready"])
            dve.wait_ge(s["ln_ready"], 1)
            link(nc.vector.tensor_scalar(lg, lg, -1.0, 1.0, ALU.mult, ALU.add))
            link(nc.vector.tensor_tensor(lg, lg, e, ALU.add))
            link(nc.vector.tensor_tensor(lg, lg, gx, ALU.add))
            link(nc.vector.scalar_tensor_tensor(dt, x, 0.0, lg, ALU.max, ALU.add))
            dve.wait_ge(s["a_ready"], 1)
            link(nc.vector.scalar_tensor_tensor(q3(gx), q3(dt), -1.0, a_rows.unsqueeze(1).to_broadcast([P, ST, 32]),
                                                ALU.mult, ALU.mult), s["g_ready"])
            dve.wait_ge(s["sums"], 1)
            for d in range(2):
                link(put(S_AC, bank[1][:, 0:n], d))
                link(put(S_DT, dt, d))


def ssd_conv(nc, st, bank, p, conv_cols, bias_cols, work, src, beside):
    raw, acc, th, hc = work
    with stage(nc, "padded") as (s, block):
        @block.gpsimd
        def _(pool):
            nc.gpsimd.memset(raw[:, :, :], 0.0).then_inc(s["padded"], 1)
            pool.wait_ge(s["padded"], 1)

    def body(i, offset):
        tile = lambda m: p[:, bass.ds(i * 6 + (8 + m), 1), :].rearrange("p a t -> p (a t)")
        with stage(nc, "kept conv tanh x_summed x_out") as (s, block):
            extra = Beside(nc, st, src, beside, 4, [bank[m][:, 0:SEQ] for m in range(4)], s, i)

            @block.sync
            def _(sp):
                st.ahead(sp, 4, offset)

            @block.tensor
            def _(pe):
                for _ in range(4):
                    extra.sum_tile(pe)

            @block.scalar
            def _(act):
                link = Chain(act, s["act_own"])
                for m in range(6):
                    link(nc.scalar.activation(raw[:, m, 2:SEQ + 2], tile(m), ACT.Copy), s["kept"])
                for m in range(6):
                    act.wait_ge(s["conv"], m + 1)
                    link(nc.scalar.activation(th[:, m, :], acc[:, m, :], ACT.Tanh, scale=0.5), s["tanh"])
                    if m >= 2:
                        extra.copy_tile(act, link)

            @block.vector
            def _(dve):
                link = Chain(dve, s["dve_own"])
                link(nc.vector.tensor_copy(hc[:, 0:30], conv_cols(i)))
                link(nc.vector.tensor_copy(hc[:, 30:36], bias_cols(i)))

                def silu(m):
                    dve.wait_ge(s["tanh"], m + 1)
                    link(sigmoid_of_tanh(nc, th[:, m, :], th[:, m, :]))
                    link(nc.vector.tensor_tensor(tile(m), th[:, m, :], acc[:, m, :], ALU.mult))

                for m in range(6):
                    dve.wait_ge(s["kept"], m + 1)
                    w = lambda j: hc[:, 5 * m + j:5 * m + j + 1]
                    link(nc.vector.tensor_scalar(acc[:, m, :], raw[:, m, 0:SEQ], w(0), hc[:, 30 + m:31 + m], ALU.mult, ALU.add))
                    for j in range(1, 5):
                        link(nc.vector.scalar_tensor_tensor(acc[:, m, :], raw[:, m, j:j + SEQ], w(j), acc[:, m, :],
                                                            ALU.mult, ALU.add), s["conv"] if j == 4 else None)
                    if m:
                        silu(m - 1)
                silu(5)

    st.bodies(2, 4, body)


def ssd_heads(nc, st, bank, C, cs, p, sc, d_cols, ys, work, src, beside):
    cb, x_t, e, m_t, xl, hs, th, z, dl = work
    wide = lambda a: a.rearrange("p (s t) -> p s t", s=2)
    with stage(nc, "cb_done turned out") as (s, block):
        @block.tensor
        def _(pe):
            for g in range(2):
                for t in range(ST):
                    mm = nc.tensor.matmul(bank[g][:, SEQ * t:SEQ * t + SEQ], p[:, 16 + g, P * t:P * t + P], p[:, 18 + g, :],
                                          start=True, stop=True)
                mm.then_inc(s["cb_done"], 1)
            for t in range(ST):
                for k in range(KT):
                    mm = nc.tensor.transpose(bank[2 + 2 * t + k // 4][:, P * (k % 4):P * (k % 4) + P], p[:, 8 + k, P * t:P * t + P],
                                             C("ident"))
                    if k % 4 == 3:
                        mm.then_inc(s["turned"], 1)

        @block.scalar
        def _(act):
            link = Chain(act, s["act_own"])
            for n in range(4):
                act.wait_ge(s["turned"], n + 1)
                link(nc.scalar.activation(x_t[:, n // 2, 512 * (n % 2):512 * (n % 2) + 512], bank[2 + n][:, :], ACT.Copy))

        @block.vector
        def _(dve):
            link = Chain(dve, s["dve_own"])
            for g in range(2):
                dve.wait_ge(s["cb_done"], g + 1)
                for d in range(2):
                    link(nc.vector.tensor_tensor(cb[:, d, g, :], bank[g][:, :], cs(f"ssd_order{4 * d}", 4), ALU.mult))

    def col(hh, q, d, t):
        at = hh * S_PER_HEAD + q * 2 * ST + d * ST + t
        return hs[:, at:at + 1]

    heads = 4

    def body(i, offset):
        with stage(nc, "local rows gaps decays weights ys_done tanh z_in x_summed x_out") as (s, block):
            extra = Beside(nc, st, src, beside, 4, [bank[6][:, 0:SEQ], bank[7][:, 0:SEQ]], s, i)

            @block.sync
            def _(sp):
                st.ahead(sp, 4, offset)

            @block.tensor
            def _(pe):
                def products(hh):
                    pe.wait_ge(s["weights"], hh + 1)
                    for t in range(ST):
                        at = 64 * (hh % 2)
                        mm = nc.tensor.matmul(bank[4 + hh // 2][at:at + 64, 0:SEQ], xl[:, t, 64 * hh:64 * hh + 64],
                                              m_t[:, hh, SEQ * t:SEQ * t + SEQ], start=(t == 0), stop=(t == ST - 1))
                    if hh % 2:
                        mm.then_inc(s["ys_done"], 1)

                pe.wait_ge(s["local"], 1)
                for n in range(2 * heads):
                    if n >= 4:
                        pe.wait_ge(s["gaps"], n - 3)
                    for t in range(ST):
                        mm = nc.tensor.matmul(bank[n % 4][:, P * t:P * t + P], col(n // 2, S_AC, n % 2, t).to_broadcast([P, P]),
                                              C("ident"), start=True, stop=True)
                    mm.then_inc(s["rows"], 1)
                    if n == 3:
                        extra.sum_tile(pe)
                extra.sum_tile(pe)
                products(0)
                extra.sum_tile(pe)
                products(1)
                products(2)
                extra.sum_tile(pe)
                products(3)

            @block.scalar
            def _(act):
                link = Chain(act, s["act_own"])
                act.wait_ge(s["z_in"], 1)
                link(nc.scalar.activation(flat(th[:, :, :]), flat(z[:, :, :]), ACT.Tanh, scale=0.5), s["tanh"])
                for n in range(2 * heads):
                    act.wait_ge(s["gaps"], n + 1)
                    link(nc.scalar.activation(e[:, n, :], e[:, n, :], ACT.Exp), s["decays"])
                    if n >= 4:
                        extra.copy_tile(act, link)

            @block.vector
            def _(dve):
                link = Chain(dve, s["dve_own"])

                def gaps(n):
                    dve.wait_ge(s["rows"], n + 1)
                    for t in range(ST):
                        link(nc.vector.tensor_scalar(e[:, n, SEQ * t:SEQ * t + SEQ], bank[n % 4][:, 0:SEQ], col(n // 2, S_AC, n % 2, t),
                                                     0.0, ALU.subtract, ALU.min), s["gaps"] if t else None)

                def weights(hh):
                    dve.wait_ge(s["decays"], 2 * hh + 2)
                    for d in range(2):
                        for t in range(ST):
                            at = slice(SEQ * t, SEQ * t + SEQ)
                            out = e[:, 2 * hh + 1, at] if d else m_t[:, hh, at]
                            link(nc.vector.scalar_tensor_tensor(out, e[:, 2 * hh + d, at], col(hh, S_DT, d, t),
                                                                cb[:, d, bass.ds(i // 2, 1), at].rearrange("p a t -> p (a t)"),
                                                                ALU.mult, ALU.mult))
                    link(nc.vector.tensor_tensor(m_t[:, hh, :], m_t[:, hh, :], e[:, 2 * hh + 1, :], ALU.add), s["weights"])

                link(nc.vector.tensor_copy(hs[:, :], sc[:, bass.ds(i * heads, heads), :].rearrange("p a c -> p (a c)")), s["local"])
                link(nc.vector.tensor_copy(z[:, :, :], p[:, bass.ds(i * 2, 2), :]), s["z_in"])
                for n in range(4):
                    gaps(n)
                link(nc.vector.tensor_copy(xl[:, :, :], x_t[:, :, bass.ds(i * (2 * P), 2 * P)]))
                weights(0)
                gaps(4)
                gaps(5)
                weights(1)
                gaps(6)
                gaps(7)
                weights(2)
                link(nc.vector.tensor_copy(dl[:, :], d_cols(i)))
                dve.wait_ge(s["tanh"], 1)
                link(sigmoid_of_tanh(nc, flat(th[:, :, :]), flat(th[:, :, :])))
                link(nc.vector.tensor_tensor(z[:, :, :], z[:, :, :], th[:, :, :], ALU.mult))
                weights(3)
                for j in range(2):
                    dve.wait_ge(s["ys_done"], j + 1)
                    link(nc.vector.scalar_tensor_tensor(th[:, j, :], p[:, bass.ds(i * 2 + (8 + j), 1), :].rearrange("p a t -> p (a t)"),
                                                        dl[:, j:j + 1], bank[4 + j][:, 0:SEQ], ALU.mult, ALU.add))
                    link(nc.vector.tensor_tensor(ys[:, bass.ds(i * 2 + j, 1), :].rearrange("p a t -> p (a t)"), th[:, j, :], z[:, j, :],
                                                 ALU.mult))

    st.bodies(SSM_HEADS // heads, 4, body)


def rwkv_inputs(nc, bank, C, p, ps, tmp, mu0, mu1, w_up, g_up, a_up, vecs, w0_rows, lw, g_t, aa, kk, rc, bonus):
    a0, k_k, k_a, r_k = vecs
    n = 14
    c0 = rc[:, 16:30]
    r, k = ps[:, 0:4, :], ps[:, 4:8, :]
    over = lambda v, w: v.unsqueeze(2).to_broadcast([P, v.shape[1], w])
    order = [12, 13] + list(range(12))
    names = ("c0_ready own shifted tanh gd lw_raw lw_in lw_th a_raw a_in a_th g_raw kk_raw kk_sq kk_sum mean root spread rk_ready "
             "bonus_done")
    with stage(nc, names) as (s, block):
        @block.gpsimd
        def _(pool):
            inverse_root(nc, pool, C, rc[:, 0:16], s["mean"], s["root"])

        @block.tensor
        def _(pe):
            pe.wait_ge(s["tanh"], 1)
            pe.wait_ge(s["shifted"], 2)
            for q in range(4):
                nc.tensor.matmul(bank[q][:, :], ps[0:64, 12, P * (q % 2):P * (q % 2) + P], w_up[:, q // 2, :],
                                 start=True, stop=True).then_inc(s["lw_raw"], 1)
            for m in range(RW):
                if m % 2 == 0:
                    pe.wait_ge(s["lw_in"], 2 + m)
                nc.tensor.matmul(bank[4 + m // 2][:, SEQ * (m % 2):SEQ * (m % 2) + SEQ], a_up[64:128, P * m:P * m + P],
                                 ps[64:128, 12, :], start=True, stop=True).then_inc(s["a_raw"], 1)
            pe.wait_ge(s["gd"], 1)
            for t in range(ST):
                nc.tensor.matmul(bank[6 + t][:, :], ps[:, 13, P * t:P * t + P], g_up[:, :], start=True, stop=True).then_inc(s["g_raw"], 1)
            pe.wait_ge(s["kk_sq"], 1)
            pe.wait_ge(s["lw_in"], 4)
            for t in range(ST):
                for m in range(RW):
                    mm = nc.tensor.matmul(bank[0][:, 8 * t + 2 * m:8 * t + 2 * m + 2], tmp[:, m, P * t:P * t + P],
                                          C("halves")[:, 0:2], start=True, stop=True)
            mm.then_inc(s["kk_sum"], 1)
            pe.wait_ge(s["root"], 1)
            for m in range(RW):
                for t in range(ST):
                    at = SEQ * (m % 2) + P * t
                    for hh in range(2):
                        mm = nc.tensor.matmul(bank[1 + m // 2][64 * hh:64 * hh + 64, at:at + P],
                                              rc[:, 8 * t + 2 * m + hh:8 * t + 2 * m + hh + 1].to_broadcast([P, 64]), C("ident"),
                                              start=True, stop=True)
                if m % 2:
                    mm.then_inc(s["spread"], 1)
            pe.wait_ge(s["rk_ready"], 1)
            for t in range(ST):
                for m in range(RW):
                    mm = nc.tensor.matmul(bank[3][:, 8 * t + 2 * m:8 * t + 2 * m + 2], tmp[:, m, P * t:P * t + P],
                                          C("halves")[:, 0:2], start=True, stop=True)
            mm.then_inc(s["bonus_done"], 1)

        @block.scalar
        def _(act):
            link = Chain(act, s["act_own"])
            act.wait_ge(s["c0_ready"], 1)
            for m in order:
                link(nc.scalar.activation(ps[:, m, :], p[:, m, :], ACT.Copy, scale=c0[:, m:m + 1]), s["own"])
            act.wait_ge(s["shifted"], 2)
            link(nc.scalar.activation(ps[0:64, 12, :], ps[0:64, 12, :], ACT.Tanh), s["tanh"])
            link(nc.scalar.activation(ps[:, 13, :], ps[:, 13, :], ACT.Tanh, scale=0.5), s["tanh"])
            for q in range(4):
                act.wait_ge(s["lw_in"], q + 1)
                link(nc.scalar.activation(lw[:, q // 2, q % 2, :], lw[:, q // 2, q % 2, :], ACT.Tanh, scale=0.5), s["lw_th"])
            act.wait_ge(s["a_in"], 4)
            link(nc.scalar.activation(aa, aa, ACT.Tanh, scale=0.5), s["a_th"])
            for t in range(ST):
                act.wait_ge(s["g_raw"], t + 1)
                link(nc.scalar.activation(g_t[:, t, :], bank[6 + t][:, :], ACT.Copy))
            act.wait_ge(s["kk_raw"], 1)
            link(nc.scalar.activation(tmp[:, 0:4, :], kk, ACT.Square), s["kk_sq"])

        @block.vector
        def _(dve):
            link = Chain(dve, s["dve_own"])
            link(nc.vector.tensor_tensor(c0, mu0, mu1, ALU.add))
            link(nc.vector.tensor_scalar(c0, c0, -1.0, 1.0, ALU.mult, ALU.add), s["c0_ready"])
            for m in order:
                dve.wait_ge(s["own"], order.index(m) + 1)
                link(nc.vector.scalar_tensor_tensor(ps[:, m, 1:SEQ], p[:, m, 0:SEQ - 1], mu0[:, m:m + 1], ps[:, m, 1:SEQ],
                                                    ALU.mult, ALU.add))
                link(nc.vector.scalar_tensor_tensor(ps[:, m, 0:SEQ - 1], p[:, m, 1:SEQ], mu1[:, m:m + 1], ps[:, m, 0:SEQ - 1],
                                                    ALU.mult, ALU.add), s["shifted"])
            link(nc.vector.tensor_tensor(kk[:, :, :], k, over(k_k, SEQ), ALU.mult), s["kk_raw"])
            dve.wait_ge(s["tanh"], 2)
            link(sigmoid_of_tanh(nc, ps[:, 13, :], ps[:, 13, :]), s["gd"])
            for q in range(4):
                dve.wait_ge(s["lw_raw"], q + 1)
                link(nc.vector.tensor_tensor(lw[:, q // 2, q % 2, :], bank[q][:, :], w0_rows[:, q // 2, :], ALU.add), s["lw_in"])
            for m in range(RW):
                dve.wait_ge(s["a_raw"], 2 * (m // 2) + 2)
                link(nc.vector.tensor_scalar(aa[:, m, :], bank[4 + m // 2][:, SEQ * (m % 2):SEQ * (m % 2) + SEQ], a0[:, m:m + 1], None,
                                             ALU.add), s["a_in"])
            dve.wait_ge(s["lw_th"], 4)
            every = lw[:, :, :, :].rearrange("p d t c -> p (d t c)")
            link(nc.vector.tensor_scalar(every, every, -0.5 * RWKV_DECAY, -0.5 * RWKV_DECAY, ALU.mult, ALU.add))
            dve.wait_ge(s["a_th"], 1)
            link(sigmoid_of_tanh(nc, aa, aa))
            dve.wait_ge(s["kk_sum"], 1)
            link(nc.vector.tensor_scalar(rc[:, 0:16], bank[0][:, 0:16], 1e-12, None, ALU.add), s["mean"])
            link(nc.vector.scalar_tensor_tensor(tmp[:, 0:4, :], aa[:, :, :], 1.0, over(k_a, SEQ), ALU.subtract, ALU.mult))
            link(nc.vector.scalar_tensor_tensor(k, tmp[:, 0:4, :], 1.0, k, ALU.add, ALU.mult))
            link(nc.vector.tensor_tensor(tmp[:, 0:4, :], r, k, ALU.mult))
            link(nc.vector.tensor_tensor(tmp[:, 0:4, :], tmp[:, 0:4, :], over(r_k, SEQ), ALU.mult), s["rk_ready"])
            for m in range(0, RW, 2):
                dve.wait_ge(s["spread"], m // 2 + 1)
                link(nc.vector.tensor_tensor(kk[:, m:m + 2, :], kk[:, m:m + 2, :],
                                             bank[1 + m // 2][:, :].rearrange("p (a t) -> p a t", a=2), ALU.mult))
            link(nc.vector.tensor_tensor(aa[:, :, :], aa[:, :, :], kk[:, :, :], ALU.mult))
            dve.wait_ge(s["bonus_done"], 1)
            link(nc.vector.tensor_copy(bonus[:, :], bank[3][:, 0:16]))


def rwkv_heads(nc, st, bank, C, cs, ps, lw, aa, kk, y_all, v_all, work, src, beside):
    (lwl, e_in, e_ex, e_neg, ka, ki, kw_rw, grams, inv, inv_t, prod, ka_t, k_t, v_t, v_half, p_half, rr, sb) = work
    yd = e_ex[:, :, :].rearrange("p d (t c) -> p d t c", t=ST)
    chunks = 4
    levels = LEVELS - 1
    order = (range(chunks), range(chunks - 1, -1, -1))
    with stage(nc, "clear") as (s, block):
        @block.gpsimd
        def _(pool):
            for x in (v_half, p_half, rr):
                nc.gpsimd.memset(x[:, :], 0.0).then_inc(s["clear"], 1)
            pool.wait_ge(s["clear"], 3)

    def unit(d, hh, t):
        return (d * 2 + hh) * 2 + t

    def tile(a, n):
        return a[:, P * n:P * n + P]

    def part(a, at, half):
        return a[64 * half:64 * half + 64, at:at + P]

    row = lambda src, i: src[:, bass.ds(i, 1), :].rearrange("p a t -> p (a t)")
    four = lambda a: a.rearrange("p (t e) -> p t e", t=4)

    def body(i, offset):
        names = ("local sums exps keys_ready masked grams_done turned turned_out v_ready a_done p_ready bc_done t_ready "
                 "zero z_done r_ready pm_done ph_ready y_done y_out ds_done s_ready x_summed x_out")
        with stage(nc, names) as (s, block):
            extra = Beside(nc, st, src, beside, 3, [bank[5][:, 0:SEQ], bank[6][:, 0:SEQ]], s, i)

            @block.sync
            def _(sp):
                st.ahead(sp, 3, offset)

            @block.gpsimd
            def _(pool):
                link = Chain(pool, s["pool_own"])
                link(nc.gpsimd.memset(sb[:, :, :], 0.0), s["zero"])

            @block.tensor
            def _(pe):
                pe.wait_ge(s["local"], 1)
                for d in range(2):
                    for x in range(2):
                        for t in range(ST):
                            at = SEQ * x + P * t
                            mm = nc.tensor.matmul(bank[d][:, at:at + P], lwl[:, d, t, :], C(f"rw{4 * d + x}"), start=True, stop=True)
                    mm.then_inc(s["sums"], 1)
                pe.wait_ge(s["local"], 2)
                for t in range(ST):
                    mm = nc.tensor.transpose(tile(bank[2], t), v_half[:, P * (4 + t):P * (5 + t)], C("ident"))
                mm.then_inc(s["turned"], 1)
                for d in range(2):
                    pe.wait_ge(s["keys_ready"], d + 1)
                    for t in range(ST):
                        nc.tensor.transpose(tile(bank[3 + d], t), tile(ka[:, d, :], t), C("ident"))
                        mm = nc.tensor.transpose(tile(bank[3 + d], 2 + t), tile(ki[:, d, :], t), C("ident"))
                    mm.then_inc(s["turned"], 1)
                for d in range(2):
                    for hh in range(2):
                        for t in range(ST):
                            n = unit(d, hh, t)
                            if n >= 3:
                                pe.wait_ge(s["masked"], n - 2)
                            b = bank[5 + n % 3]
                            lo = slice(64 * hh, 64 * hh + 64)
                            rhs = kw_rw[lo, d, :, P * t:P * t + P]
                            nc.tensor.matmul(b[:, 0:SEQ].rearrange("p (x t) -> p x t", x=2), ka[lo, d, P * t:P * t + P], rhs,
                                             start=True, stop=True)
                            nc.tensor.matmul(b[:, SEQ:2 * SEQ].rearrange("p (x t) -> p x t", x=2), ki[lo, d, P * t:P * t + P], rhs,
                                             start=True, stop=True).then_inc(s["grams_done"], 1)
                pe.wait_ge(s["masked"], 8)
                pe.wait_ge(s["turned_out"], 3)
                for lv in range(levels):
                    for d in range(2):
                        if lv:
                            pe.wait_ge(s["t_ready"], 2 * (lv - 1) + d + 1)
                        for n in range(4):
                            rhs = C("ident") if lv == 0 else tile(inv[:, d, :], n)
                            mm = nc.tensor.matmul(tile(bank[d], n), grams[:, 4 * d + n, 0:P], rhs, start=True, stop=True)
                        mm.then_inc(s["a_done"], 1)
                    for d in range(2):
                        pe.wait_ge(s["p_ready"], 2 * lv + d + 1)
                        if 0 < lv < levels - 1:
                            for n in range(4):
                                nc.tensor.matmul(tile(bank[2 + d], n), tile(inv_t[:, d, :], n), tile(prod[:, d, :], n), start=True, stop=True)
                        for n in range(4):
                            rhs = C("ident") if lv == 0 else tile(inv_t[:, d, :], n)
                            mm = nc.tensor.matmul(tile(bank[4 + d], n), tile(prod[:, d, :], n), rhs, start=True, stop=True)
                        mm.then_inc(s["bc_done"], 1)
                pe.wait_ge(s["t_ready"], 2 * levels)
                for step in range(chunks):
                    for d in range(2):
                        r, c = 2 * step + d, order[d][step]
                        t = c // 2
                        if step == 0:
                            pe.wait_ge(s["zero"], 1)
                        else:
                            pe.wait_ge(s["s_ready"], r - 1)
                        nc.tensor.matmul(bank[0][:, P * d:P * d + P], kw_rw[:, d, 0, P * t:P * t + P], sb[:, d, :], start=True, stop=False,
                                         skip_group_check=True)
                        for hh in range(2):
                            mm = nc.tensor.matmul(bank[0][:, P * d + 64 * hh:P * d + 64 * hh + 64], grams[:, unit(d, hh, t), SEQ:SEQ + P],
                                                  v_t[:, t, 64 * hh:64 * hh + 64], start=False, stop=True, skip_group_check=True)
                        mm.then_inc(s["z_done"], 1)
                    if step < 3:
                        extra.sum_tile(pe)
                    for d in range(2):
                        r, c = 2 * step + d, order[d][step]
                        t = c // 2
                        pe.wait_ge(s["r_ready"], r + 1)
                        for hh in range(2):
                            mm = nc.tensor.matmul(bank[1][:, P * d + 64 * hh:P * d + 64 * hh + 64], tile(inv_t[:, d, :], 2 * hh + t),
                                                  rr[:, P * d + 64 * hh:P * d + 64 * hh + 64], start=True, stop=True,
                                                  skip_group_check=True)
                        mm.then_inc(s["pm_done"], 1)
                    for d in range(2):
                        r, c = 2 * step + d, order[d][step]
                        t, half = c // 2, c % 2
                        ph = P * (2 * d + half)
                        pe.wait_ge(s["ph_ready"], r + 1)
                        nc.tensor.matmul(bank[3][:, P * d:P * d + P], C("ident"), sb[:, d, :], start=True, stop=False)
                        nc.tensor.matmul(bank[3][:, P * d:P * d + P], ka_t[:, d, t, :], p_half[:, ph:ph + P], start=False, stop=False)
                        nc.tensor.matmul(bank[3][:, P * d:P * d + P], k_t[:, d, t, :], v_half[:, P * c:P * c + P], start=False,
                                         stop=True).then_inc(s["ds_done"], 1)
                        nc.tensor.matmul(bank[2][:, P * d:P * d + P], kw_rw[:, d, 1, P * t:P * t + P], sb[:, d, :], start=True, stop=False,
                                         skip_group_check=True)
                        for hh in range(2):
                            n, cols = unit(d, hh, t), slice(64 * hh, 64 * hh + 64)
                            nc.tensor.matmul(bank[2][:, P * d + 64 * hh:P * d + 64 * hh + 64], grams[:, n, P:2 * P], p_half[:, ph + 64 * hh:ph + 64 * hh + 64],
                                             start=False, stop=False, skip_group_check=True)
                            mm = nc.tensor.matmul(bank[2][:, P * d + 64 * hh:P * d + 64 * hh + 64], grams[:, n, 3 * P:4 * P], v_t[:, t, cols],
                                                  start=False, stop=True, skip_group_check=True)
                        mm.then_inc(s["y_done"], 1)

            @block.scalar
            def _(act):
                link = Chain(act, s["act_own"])
                for d in range(2):
                    act.wait_ge(s["sums"], d + 1)
                    link(nc.scalar.activation(e_ex[:, d, :], bank[d][:, 0:SEQ], ACT.Exp))
                    link(nc.scalar.activation(e_in[:, d, :], bank[d][:, SEQ:2 * SEQ], ACT.Exp))
                    link(nc.scalar.activation(e_neg[:, d, :], bank[d][:, SEQ:2 * SEQ], ACT.Exp, scale=-1.0), s["exps"])
                act.wait_ge(s["turned"], 1)
                link(nc.scalar.activation(v_t[:, :, :], bank[2][:, 0:SEQ].rearrange("p (t e) -> p t e", t=ST), ACT.Copy), s["turned_out"])
                for d in range(2):
                    act.wait_ge(s["turned"], d + 2)
                    link(nc.scalar.activation(ka_t[:, d, :, :], bank[3 + d][:, 0:SEQ].rearrange("p (t e) -> p t e", t=ST), ACT.Copy))
                    link(nc.scalar.activation(k_t[:, d, :, :], bank[3 + d][:, SEQ:2 * SEQ].rearrange("p (t e) -> p t e", t=ST), ACT.Copy),
                         s["turned_out"])
                for step in range(chunks):
                    for d in range(2):
                        r, c = 2 * step + d, order[d][step]
                        half = c % 2
                        act.wait_ge(s["pm_done"], 2 * step + 2)
                        ph = P * (2 * d + half)
                        if r >= 4:
                            act.wait_ge(s["y_done"], r - 3)
                        link(nc.scalar.activation(part(p_half, ph, half), part(bank[1], P * d, half), ACT.Copy), s["ph_ready"])
                    for d in range(2):
                        r, c = 2 * step + d, order[d][step]
                        t, half = c // 2, c % 2
                        act.wait_ge(s["y_done"], 2 * step + 2)
                        link(nc.scalar.activation(yd[64 * half:64 * half + 64, d, t, :], part(bank[2], P * d, half), ACT.Copy), s["y_out"])
                    extra.copy_tile(act, link)

            @block.vector
            def _(dve):
                link = Chain(dve, s["dve_own"])
                link(nc.vector.tensor_copy(lwl[:, :, :, :].rearrange("p d t c -> p (d t) c"),
                                           lw[:, :, :, bass.ds(i * P, P)].rearrange("p d t c -> p (d t) c")), s["local"])
                link(nc.vector.tensor_copy(v_half[:, 4 * P:4 * P + SEQ], row(ps[:, 8:12, :], i)), s["local"])
                for d in range(2):
                    dve.wait_ge(s["exps"], d + 1)
                    link(nc.vector.tensor_tensor(ka[:, d, :], row(aa, i), e_neg[:, d, :], ALU.mult))
                    link(nc.vector.tensor_tensor(ki[:, d, :], row(ps[:, 4:8, :], i), e_neg[:, d, :], ALU.mult))
                    link(nc.vector.tensor_tensor(kw_rw[:, d, 0, :], row(kk, i), e_ex[:, d, :], ALU.mult))
                    link(nc.vector.tensor_tensor(kw_rw[:, d, 1, :], row(ps[:, 0:4, :], i), e_in[:, d, :], ALU.mult), s["keys_ready"])
                for n in range(8):
                    dve.wait_ge(s["grams_done"], n + 1)
                    link(nc.vector.tensor_tensor(grams[:, n, :], bank[5 + n % 3][:, :], cs(f"rw{4 * (n // 4)}", 4), ALU.mult), s["masked"])
                dve.wait_ge(s["turned_out"], 1)
                for t in range(ST):
                    for half in range(2):
                        link(nc.vector.tensor_copy(part(v_half, P * (2 * t + half), half), v_t[64 * half:64 * half + 64, t, :]))
                link(nc.vector.tensor_copy(v_all[:, :, bass.ds(i * P, P)], v_t[:, :, :]))
                for lv in range(levels):
                    for d in range(2):
                        dve.wait_ge(s["a_done"], 2 * lv + d + 1)
                        link(nc.vector.tensor_tensor(four(prod[:, d, :]), four(bank[d][:, :]),
                                                     C(f"lev_{'fb'[d]}{lv}").unsqueeze(1).to_broadcast([P, 4, P]), ALU.mult), s["p_ready"])
                    for d in range(2):
                        dve.wait_ge(s["bc_done"], 2 * lv + d + 1)
                        eye = C("ident").unsqueeze(1).to_broadcast([P, 4, P])
                        if lv == 0:
                            link(nc.vector.tensor_tensor(four(inv[:, d, :]), eye, four(prod[:, d, :]), ALU.subtract))
                        elif lv < levels - 1:
                            link(nc.vector.tensor_tensor(inv[:, d, :], inv[:, d, :], bank[2 + d][:, :], ALU.subtract))
                        link(nc.vector.tensor_tensor(four(inv_t[:, d, :]), eye if lv == 0 else four(inv_t[:, d, :]),
                                                     four(bank[4 + d][:, :]), ALU.subtract), s["t_ready"])
                for step in range(chunks):
                    for d in range(2):
                        r, c = 2 * step + d, order[d][step]
                        half = c % 2
                        dve.wait_ge(s["z_done"], 2 * step + 2)
                        link(nc.vector.tensor_scalar(part(rr, P * d, half), part(bank[0], P * d, half), -1.0, None, ALU.mult), s["r_ready"])
                    for d in range(2):
                        r, c = 2 * step + d, order[d][step]
                        last = 64 * c + (0 if d else 63)
                        dve.wait_ge(s["ds_done"], 2 * step + 2)
                        dve.wait_ge(s["y_done"], 2 * step + 2)
                        link(nc.vector.scalar_tensor_tensor(sb[:, d, :], bank[3][:, P * d:P * d + P], e_in[:, d, last:last + 1], C("half"),
                                                            ALU.mult, ALU.mult), s["s_ready"])
                dve.wait_ge(s["y_out"], 8)
                link(nc.vector.tensor_tensor(y_all[:, :, bass.ds(i * P, P)], yd[:, 0, :, :], yd[:, 1, :, :], ALU.add))

    st.bodies(RW, 3, body)


def rwkv_output(nc, st, bank, C, y, v_all, g_t, bonus, ln_rows, sq, st16, out, u, ff):
    st.begin(4)
    heads = ST * 8
    y3 = y[:, :, :].rearrange("p t (h e) -> p (t h) e", e=64)
    v3 = v_all[:, :, :].rearrange("p t (h e) -> p (t h) e", e=64)
    s3 = sq[:, :, :].rearrange("p t (h e) -> p (t h) e", e=64)
    over = lambda c: c.unsqueeze(2).to_broadcast([P, heads, 64])
    rows = lambda j: ln_rows[:, j, :].unsqueeze(1).to_broadcast([P, ST, 512])
    with stage(nc, "centred squared mean root ready turned used") as (s, block):
        @block.gpsimd
        def _(pool):
            inverse_root(nc, pool, C, st16[:, 0:16], s["mean"], s["root"])

        @block.scalar
        def _(act):
            link = Chain(act, s["act_own"])
            act.wait_ge(s["centred"], 1)
            link(nc.scalar.activation(flat(sq[:, :, :]), flat(y[:, :, :]), ACT.Square), s["squared"])
            for d in range(2):
                act.wait_ge(s["used"], d + 1)
                for t in range(ST):
                    link(nc.scalar.activation(ff[:, 4 * d + 2 * t:4 * d + 2 * t + 2, :],
                                              bank[4 + 2 * d + t][:, :].rearrange("p (a c) -> p a c", a=2), ACT.Copy))
            for n in range(2):
                act.wait_ge(s["turned"], n + 1)
                link(nc.scalar.activation(flat(out[:, 2 * n:2 * n + 2, :]), bank[n][:, :], ACT.Copy))

        def tensor(pe):
            def visit(g, h, r):
                for k in range(KT):
                    if k % 2 == 0:
                        st.wait(pe, h, r, k // 2)
                    at = 512 * (k % 2)
                    for t in range(ST):
                        mm = nc.tensor.matmul(bank[4 + 2 * h + t][:, :], u[:, k, CTX + P * t:CTX + P * t + P],
                                              st.chunk(h, k // 2)[:, at:at + 512], start=(k == 0), stop=(k == KT - 1))
                mm.then_inc(s["used"], 1)
            walk(pe, 2, visit)
            pe.wait_ge(s["ready"], 1)
            for m in range(RW):
                for t in range(ST):
                    at = SEQ * (m % 2) + P * t
                    mm = nc.tensor.transpose(bank[m // 2][:, at:at + P], y[:, t, P * m:P * m + P], C("ident"))
                if m % 2:
                    mm.then_inc(s["turned"], 1)

        @block.vector
        def _(dve):
            link = Chain(dve, s["dve_own"])
            link(nc.vector.tensor_reduce(st16[:, 16:32], y3, AX.X, ALU.add))
            link(nc.vector.tensor_scalar(st16[:, 16:32], st16[:, 16:32], 1.0 / 64, None, ALU.mult))
            link(nc.vector.tensor_tensor(y3, y3, over(st16[:, 16:32]), ALU.subtract), s["centred"])
            link(nc.vector.tensor_tensor(v3, v3, over(bonus[:, :]), ALU.mult))
            dve.wait_ge(s["squared"], 1)
            link(nc.vector.tensor_reduce(st16[:, 0:16], s3, AX.X, ALU.add))
            link(nc.vector.tensor_scalar(st16[:, 0:16], st16[:, 0:16], 1.0 / 64, RWKV_LN_EPS, ALU.mult, ALU.add), s["mean"])
            dve.wait_ge(s["root"], 1)
            link(nc.vector.tensor_tensor(y3, y3, over(st16[:, 0:16]), ALU.mult))
            link(nc.vector.tensor_tensor(y[:, :, :], y[:, :, :], rows(0), ALU.mult))
            link(nc.vector.tensor_tensor(y[:, :, :], y[:, :, :], rows(1), ALU.add))
            link(nc.vector.tensor_tensor(y[:, :, :], y[:, :, :], v_all[:, :, :], ALU.add))
            link(nc.vector.tensor_tensor(y[:, :, :], y[:, :, :], g_t[:, :, :], ALU.mult), s["ready"])

        st.groups(2, 4, s, block, ((block.tensor, tensor),))
    st.passed(2, 4)


def hgrn_forget(nc, bank, C, ff, lf, kf, lb, om):
    with stage(nc, "diff exped lb_ready sig ff_ready one_less turned kept") as (s, block):
        @block.tensor
        def _(pe):
            for d in range(2):
                pe.wait_ge(s["one_less"], d + 1)
                for m in range(HG):
                    for t in range(ST):
                        at = SEQ * (m % 2) + P * t
                        mm = nc.tensor.transpose(bank[2 * d + m // 2][:, at:at + P], lf[:, d, t, P * m:P * m + P], C("ident"))
                    if m % 2:
                        mm.then_inc(s["turned"], 1)

        @block.scalar
        def _(act):
            link = Chain(act, s["act_own"])
            for d in range(2):
                link(nc.scalar.activation(ff[:, 4 * d:4 * d + 4, :], ff[:, 4 * d:4 * d + 4, :], ACT.Sigmoid), s["sig"])
            act.wait_ge(s["diff"], 1)
            link(nc.scalar.activation(lb, lb, ACT.Exp), s["exped"])
            for n in range(4):
                act.wait_ge(s["turned"], n + 1)
                link(nc.scalar.activation(flat(kf[:, n // 2, 2 * (n % 2):2 * (n % 2) + 2, :]), bank[n][:, :], ACT.Copy), s["kept"])
            act.wait_ge(s["ff_ready"], 1)
            for d in range(2):
                link(nc.scalar.activation(lf[:, d, :, :].rearrange("p t (a c) -> p (t a) c", a=2), ff[:, 4 * d:4 * d + 4, :], ACT.Ln))

        @block.vector
        def _(dve):
            link = Chain(dve, s["dve_own"])
            link(nc.vector.tensor_tensor(lb, lb, lb, ALU.subtract), s["diff"])
            dve.wait_ge(s["exped"], 1)
            link(nc.vector.reciprocal(om, lb))
            link(nc.vector.tensor_tensor(om, om, lb, ALU.mult))
            link(nc.vector.tensor_tensor(lb, om, om, ALU.subtract))
            link(nc.vector.tensor_scalar(om, lb, -1.0, 1.0, ALU.mult, ALU.add))
            wide = lambda a: a.rearrange("p (a c) -> p a c", a=2).unsqueeze(1).to_broadcast([P, ST, 2, SEQ])
            for d in range(2):
                dve.wait_ge(s["sig"], d + 1)
                x = ff[:, 4 * d:4 * d + 4, :].rearrange("p (t a) c -> p t a c", a=2)
                link(nc.vector.tensor_tensor(x, x, wide(om), ALU.mult))
                link(nc.vector.tensor_tensor(x, x, wide(lb), ALU.add))
                link(nc.vector.tensor_scalar(lf[:, d, :, :].rearrange("p t (a c) -> p t a c", a=2), x, -1.0, 1.0, ALU.mult, ALU.add), s["one_less"])
                link(nc.vector.tensor_scalar(x, x, 2.0 ** -63, None, ALU.max))
            dve.wait_ge(s["kept"], 4)
            link(nc.vector.tensor_copy(om, lb), s["ff_ready"])


def hgrn_heads(nc, st, bank, C, cs, p, lf, kf, w_cols, yh, work, src, beside):
    lfl, q2, kl, e, qe, ke, sc, tmp, it, ib, ob, osq, rc, gg, gt, wl = work
    d2 = lambda a: a.rearrange("p (d t) -> p d t", d=2)
    row = lambda src, i: src[:, bass.ds(i, 1), :].rearrange("p a t -> p (a t)")
    def body(i, offset):
        names = ("local sums exped pair scored masked added turned turned_out x_ready out o_in o_sq o_sum mean root "
                 "spread g_in tanh x_summed x_out")
        with stage(nc, names) as (s, block):
            extra = Beside(nc, st, src, beside, 6, [bank[4][:, 0:SEQ], bank[5][:, 0:SEQ]], s, i, half_tanh=True)

            @block.sync
            def _(sp):
                st.ahead(sp, 6, offset)

            @block.gpsimd
            def _(pool):
                link = Chain(pool, s["pool_own"])
                for n in range(LEVELS + 1):
                    pool.wait_ge(s["masked"], n + 1)
                    if n == 0:
                        link(nc.gpsimd.tensor_copy(sc[:, :], tmp[:, 0, :]), s["added"])
                    else:
                        link(nc.gpsimd.tensor_tensor(sc[:, :], sc[:, :], tmp[:, n % 2, :], ALU.add), s["added"])
                inverse_root(nc, pool, C, rc[:, :], s["mean"], s["root"])

            @block.tensor
            def _(pe):
                pe.wait_ge(s["local"], 4)
                for t in range(ST):
                    mm = nc.tensor.transpose(bank[6][:, P * t:P * t + P], it[:, P * t:P * t + P], C("ident"))
                mm.then_inc(s["turned"], 1)

                def sums(n):
                    if n >= 2:
                        pe.wait_ge(s["exped"], n - 1)
                    for d in range(2):
                        for t in range(ST):
                            at = SEQ * d + P * t
                            if n < LEVELS:
                                rhs = C(f"hg_{'fb'[d]}{n}")
                            elif d == 0:
                                rhs = C("tri_f") if t else C("aft")
                            else:
                                rhs = C("bef") if t else C("tri_b")
                            mm = nc.tensor.matmul(bank[n % 2][:, at:at + P], lfl[:, d, t, :], rhs, start=True, stop=True)
                    mm.then_inc(s["sums"], 1)

                def scores(n, ks, qs):
                    if n >= 2:
                        pe.wait_ge(s["masked"], n - 1)
                    for d in range(2):
                        for t in range(ST):
                            at = SEQ * d + P * t
                            mm = nc.tensor.matmul(bank[2 + n % 2][:, at:at + P], ks[:, at:at + P], qs[:, at:at + P], start=True, stop=True)
                    mm.then_inc(s["scored"], 1)

                scores(0, kl, q2)
                sums(0)
                for n in range(LEVELS):
                    sums(n + 1)
                    if n < 6:
                        extra.sum_tile(pe)
                    pe.wait_ge(s["pair"], n + 1)
                    scores(n + 1, ke[:, n % 2, :], qe[:, n % 2, :])
                pe.wait_ge(s["pair"], LEVELS + 1)
                pe.wait_ge(s["masked"], LEVELS)
                pe.wait_ge(s["x_out"], 6)
                kx, qx = ke[:, LEVELS % 2, :], qe[:, LEVELS % 2, :]
                nc.tensor.matmul(bank[4][:, 0:P], kx[:, 0:P], qx[:, P:2 * P], start=True, stop=True)
                nc.tensor.matmul(bank[4][:, P:2 * P], kx[:, 3 * P:4 * P], qx[:, 2 * P:3 * P], start=True, stop=True).then_inc(s["scored"], 1)
                pe.wait_ge(s["x_ready"], 1)
                pe.wait_ge(s["turned_out"], 1)
                for t in range(ST):
                    nc.tensor.matmul(bank[5][:, P * t:P * t + P], ib[:, t, :], tmp[:, 0, P * t:P * t + P], start=(t == 0), stop=False,
                                     skip_group_check=True)
                    cross = tmp[:, 1, P:2 * P] if t == 0 else tmp[:, 1, 0:P]
                    mm = nc.tensor.matmul(bank[5][:, P * t:P * t + P], ib[:, 1 - t, :], cross, start=False, stop=True, skip_group_check=True)
                mm.then_inc(s["out"], 1)
                pe.wait_ge(s["o_sq"], 1)
                column_sums(nc, C, bank[6], osq, ST).then_inc(s["o_sum"], 1)
                pe.wait_ge(s["root"], 1)
                spread(nc, C, bank[7], rc, ST).then_inc(s["spread"], 1)

            @block.scalar
            def _(act):
                link = Chain(act, s["act_own"])
                act.wait_ge(s["turned"], 1)
                link(nc.scalar.activation(ib[:, :, :], bank[6][:, 0:SEQ].rearrange("p (t e) -> p t e", t=ST), ACT.Copy), s["turned_out"])
                act.wait_ge(s["g_in"], 1)
                link(nc.scalar.activation(gt[:, :], gg[:, :], ACT.Tanh, scale=0.5), s["tanh"])
                for n in range(LEVELS + 1):
                    act.wait_ge(s["sums"], n + 1)
                    if n >= 2:
                        act.wait_ge(s["pair"], n - 1)
                    link(nc.scalar.activation(e[:, n % 2, :], bank[n % 2][:, :], ACT.Exp), s["exped"])
                    if n:
                        extra.copy_tile(act, link)
                act.wait_ge(s["o_in"], 1)
                link(nc.scalar.activation(osq[:, :], ob[:, :], ACT.Square), s["o_sq"])

            @block.vector
            def _(dve):
                link = Chain(dve, s["dve_own"])
                link(nc.vector.tensor_copy(lfl[:, :, :, :].rearrange("p d t c -> p (d t) c"),
                                           lf[:, :, :, bass.ds(i * P, P)].rearrange("p d t c -> p (d t) c")), s["local"])
                link(nc.vector.tensor_copy(d2(q2[:, :]), row(p[:, 0:4, :], i).unsqueeze(1).to_broadcast([P, 2, SEQ])), s["local"])
                link(nc.vector.tensor_copy(d2(kl[:, :]), kf[:, :, bass.ds(i, 1), :].rearrange("p d a t -> p (d a) t")), s["local"])
                link(nc.vector.tensor_copy(it[:, :], row(p[:, 4:8, :], i)), s["local"])
                link(nc.vector.tensor_copy(gg[:, :], row(p[:, 8:12, :], i)), s["g_in"])
                link(nc.vector.tensor_copy(wl[:, :], w_cols(i)))
                dve.wait_ge(s["scored"], 1)
                link(nc.vector.tensor_tensor(tmp[:, 0, :].rearrange("p (t e) -> p t e", t=4), bank[2][:, :].rearrange("p (t e) -> p t e", t=4),
                                             C("ident").unsqueeze(1).to_broadcast([P, 4, P]), ALU.mult), s["masked"])
                for n in range(LEVELS + 1):
                    dve.wait_ge(s["exped"], n + 1)
                    if n >= 2:
                        dve.wait_ge(s["scored"], n)
                    link(nc.vector.tensor_tensor(qe[:, n % 2, :], q2[:, :], e[:, n % 2, :], ALU.mult))
                    link(nc.vector.tensor_tensor(ke[:, n % 2, :], kl[:, :], e[:, n % 2, :], ALU.mult), s["pair"])
                    if n < LEVELS:
                        m = n + 1
                        dve.wait_ge(s["scored"], m + 1)
                        if m >= 2:
                            dve.wait_ge(s["added"], m - 1)
                        for d in range(2):
                            lev = C(f"lev_{'bf'[d]}{n}").unsqueeze(1).to_broadcast([P, 2, P])
                            at = slice(SEQ * d, SEQ * d + SEQ)
                            link(nc.vector.tensor_tensor(tmp[:, m % 2, at].rearrange("p (t e) -> p t e", t=2),
                                                         bank[2 + m % 2][:, at].rearrange("p (t e) -> p t e", t=2), lev, ALU.mult),
                                 s["masked"] if d else None)
                dve.wait_ge(s["added"], LEVELS + 1)
                link(nc.vector.tensor_tensor(tmp[:, 0, 0:SEQ], sc[:, 0:SEQ], sc[:, SEQ:2 * SEQ], ALU.add))
                dve.wait_ge(s["scored"], LEVELS + 2)
                link(nc.vector.tensor_copy(tmp[:, 1, 0:SEQ], bank[4][:, 0:SEQ]), s["x_ready"])
                dve.wait_ge(s["tanh"], 1)
                link(sigmoid_of_tanh(nc, gt[:, :], gt[:, :]))
                link(nc.vector.tensor_tensor(gg[:, :], gg[:, :], gt[:, :], ALU.mult))
                dve.wait_ge(s["out"], 1)
                link(nc.vector.tensor_copy(ob[:, :], bank[5][:, 0:SEQ]), s["o_in"])
                dve.wait_ge(s["o_sum"], 1)
                link(nc.vector.tensor_scalar(rc[:, :], bank[6][:, 0:ST], 1.0 / P, EPS, ALU.mult, ALU.add), s["mean"])
                dve.wait_ge(s["spread"], 1)
                link(nc.vector.scalar_tensor_tensor(ob[:, :], ob[:, :], wl[:, 0:1], bank[7][:, 0:SEQ], ALU.mult, ALU.mult))
                link(nc.vector.tensor_tensor(row(yh, i), ob[:, :], gg[:, :], ALU.mult))

    st.bodies(HG, 6, body)


def start_loads(nc, pairs, sem):
    for dst, src in pairs:
        nc.sync.dma_start(dst, src).then_inc(sem, 16)
    return 16 * len(pairs)


def finish_loads(nc, total, sem):
    nc.sync.wait_ge(sem, total)
    nc.sync.sem_clear(sem)
    nc.all_engine_barrier()


def load_all(nc, pairs, sem):
    finish_loads(nc, start_loads(nc, pairs, sem), sem)


def build(nc, a, out, col_at):
    with ExitStack() as top:
        used = {}

        def sb(name, shape, es=top):
            used[name] = used.get(name, 0) + 1
            return es.enter_context(nc.sbuf_tensor(f"{name}_{used[name]}", shape, F32))

        bank = [top.enter_context(nc.psum_tensor(f"bank{i}", [P, 512], F32)) for i in range(8)]
        w_sems = [[top.enter_context(nc.semaphore(f"w{i}_{c}")) for c in range(SLOTS)] for i in range(2)]
        small = top.enter_context(nc.semaphore("small"))
        w_ring = sb("w_ring", [P, 2, SLOTS, CHUNK])
        h = sb("h", [P, KT, TOK])
        u = sb("u", [P, KT, TOK])
        cols = sb("cols", [P, a["cols"].shape[1]])
        st = Stream(nc, a["w"], w_ring, w_sems)

        def cc(name, n0=0, n1=None):
            lo, n = col_at[name]
            return cols[:, lo + n0:lo + (n if n1 is None else n1)]

        base = sb("const_base", [P, N_BASE * P])

        def tiles_of(names, part):
            def cs(name, n):
                if name in SECOND_NAMES[:N_BASE]:
                    k = SECOND_NAMES.index(name)
                    return base[:, P * k:P * (k + n)]
                k = names.index(name)
                return part[:, P * k:P * (k + n)]
            return (lambda name: cs(name, 1)), cs

        with ExitStack() as es:
            const = sb("const_first", [P, len(FIRST_NAMES) * P], es)
            C, _ = tiles_of(FIRST_NAMES, const)
            gated = sb("gated", [P, 2 * KT, TOK], es)
            load_all(nc, [(h[:, :, :], a["h"].rearrange("p (k t) -> p k t", k=KT)), (cols[:, :], a["cols"]),
                          (base[:, :], a["const2"][:, 0:N_BASE * P]), (const[:, :], a["const"])], small)

            def modulate(layer, es2):
                with ExitStack() as e3:
                    mod = sb(f"mod{layer}", [P, 24, 2], es2)
                    rows = sb("mod_rows", [2, 1024], e3)
                    sc_t = sb("silu_c", [P, KT, 2], e3)
                    sq = sb("sq", [P, KT, TOK], e3)
                    rs = sb("rs", [P, TOK], e3)
                    gs = sb("gs", [P, KT, 2], e3)
                    with stage(nc, "th") as (s, block):
                        @block.scalar
                        def _(act):
                            nc.scalar.activation(sc_t[:, :, :].rearrange("p k c -> p (k c)"), cc("c"), ACT.Tanh, scale=0.5).then_inc(s["th"], 1)

                        @block.vector
                        def _(dve):
                            link = Chain(dve, s["dve_own"])
                            dve.wait_ge(s["th"], 1)
                            f = sc_t[:, :, :].rearrange("p k c -> p (k c)")
                            link(nc.vector.tensor_scalar(f, f, 0.5, 0.5, ALU.mult, ALU.add))
                            link(nc.vector.tensor_tensor(f, f, cc("c"), ALU.mult))
                    modulation(nc, st, bank, C, sc_t, rows, mod, cc("ada_b", 24 * layer, 24 * layer + 24))
                    feature_norm(nc, bank, C, h, u, cc("norm_g", 8 * layer, 8 * layer + 8), mod,
                                 ((0, CTX, 1), (CTX, SEQ, 0)), sq, rs, gs)
                return mod

            with ExitStack() as l0:
                mod = modulate(0, l0)
                sc = sb("sc", [P, QK_HEADS, PER_HEAD], l0)
                o_cols = sb("o_cols", [P, 1], l0)
                with ExitStack() as e3:
                    w_ab = sb("w_ab", [P, KT, 64], e3)
                    gate_rows = sb("gate_rows", [P, 2, 32], e3)
                    tmp = sb("gate_tmp", [P, 5, P], e3)
                    load_all(nc, [(w_ab[:, :, :], a["w_ab"].rearrange("p (k c) -> p k c", k=KT)),
                                  (gate_rows[:, :, :].rearrange("p a c -> p (a c)"), a["rows"][:, 0:64].to_broadcast([P, 64]))], small)
                    delta_gates(nc, bank, C, u, w_ab, gate_rows[:, 0, :], gate_rows[:, 1, :], sc, tmp)
                with stage(nc, "half") as (s, block):
                    @block.vector
                    def _(dve):
                        nc.vector.tensor_scalar(o_cols[:, :], cc("dn_o"), 0.5, None, ALU.mult).then_inc(s["half"], 1)
                        dve.wait_ge(s["half"], 1)
                delta_heads(nc, st, bank, C, u, sc, cc("conv"), o_cols[:, 0:1], gated, h)
                load_all(nc, [(h[:, :, :], a["h"].rearrange("p (k t) -> p k t", k=KT))], small)
                residual_linear(nc, st, bank, 4, 4, gated, 16, h, mod, ((0, CTX, 1), (CTX, SEQ, 0)), 0)
            with ExitStack() as l1:
                mod = modulate(1, l1)
                pqz = sb("pqz", [P, 2 * ATT_Q, SEQ], l1)
                pkv = sb("pkv", [P, 2 * ATT_KV, TOK], l1)
                kf = sb("kf", [P, ATT_KV, TOK], l1)
                v_t = sb("v_t1", [P, ATT_KV, TT, P], l1)
                rope = sb("rope", [P, 2 * SEQ], l1)
                loads = start_loads(nc, [(rope[:, :], a["rope"])], small)
                project(nc, st, bank, 4, 4, lambda k: u[:, k, CTX:TOK], SEQ, pqz)
                project(nc, st, bank, 1, 4, lambda k: u[:, k, :], TOK, pkv)
                finish_loads(nc, loads, small)
                with ExitStack() as e3:
                    sq = sb("sq1", [P, 2 * TOK], e3)
                    rs = sb("rs1", [P, TOK], e3)
                    attention_keys(nc, bank, C, pkv, cc("kg"), rope, kf, v_t, sq, rs)
                attention_heads(nc, bank, C, pqz, cc("qg"), rope, kf, v_t, gated)
                residual_linear(nc, st, bank, 2, 4, gated, 8, h, mod, ((CTX, SEQ, 0),), CTX)
            with ExitStack() as e3:
                sq = sb("sq2", [P, KT, TOK], e3)
                rs = sb("rs2", [P, TOK], e3)
                feature_norm(nc, bank, C, h, h, cc("final_g"), None, ((CTX, SEQ, 0),), sq, rs, None)

        latent = lambda k: u[:, k, CTX:TOK]
        ys = u[:, :, 0:CTX]
        spare = h[:, :, 0:CTX]
        yr = sb("yr", [P, RW, SEQ])

        def const_part(first, n, es2):
            at = SECOND_NAMES.index(first)
            part = sb("const_part", [P, n * P], es2)
            C, cs = tiles_of(SECOND_NAMES[at:at + n], part)
            return C, cs, (part[:, :], a["const2"][:, P * at:P * (at + n)])

        C, _ = tiles_of((), None)

        def norm(src, dst, g, first):
            with ExitStack() as e3:
                sq = sb("sq3", [P, KT, SEQ], e3)
                rs = sb("rs3", [P, SEQ], e3)
                feature_norm(nc, bank, C, src, dst, g, None, ((first, SEQ, 0),), sq, rs, None)

        norm(h, u, cc("norm1_w"), CTX)

        p_rw = p_hg = sb("p_next", [P, 16, SEQ])
        with ExitStack() as es:
            C2, cs, pair = const_part("ssd_order0", 8, es)
            p = sb("p_ssd", [P, 20, SEQ], es)
            sc = sb("sc_ssd", [P, SSM_HEADS, S_PER_HEAD], es)
            with ExitStack() as e3:
                w_dt = sb("w_dt", [P, KT, 32], e3)
                dt_rows = sb("dt_rows", [P, 2, 32], e3)
                tmp = sb("dt_tmp", [P, 5, 32 * ST], e3)
                loads = start_loads(nc, [pair, (w_dt[:, :, :].rearrange("p k c -> p (k c)"), a["w_dt"]),
                                         (dt_rows[:, :, :].rearrange("p a c -> p (a c)"), a["rows"][:, 64:128].to_broadcast([P, 64]))], small)
                project(nc, st, bank, 3, 4, latent, SEQ, p[:, 8:20, :])
                finish_loads(nc, loads, small)
                ssd_steps(nc, bank, C2, u, w_dt, dt_rows[:, 0, :], dt_rows[:, 1, :], sc, tmp)
            with ExitStack() as e3:
                work = [sb(n, [P] + d, e3) for n, d in (
                    ("ssd_raw", [6, SEQ + 4]), ("ssd_acc", [6, SEQ]), ("ssd_tanh", [6, SEQ]), ("ssd_hc", [36]))]
                ssd_conv(nc, st, bank, p, lambda i: cols[:, bass.ds(i * 30 + col_at["ssm_conv"][0], 30)],
                         lambda i: cols[:, bass.ds(i * 6 + col_at["ssm_conv_b"][0], 6)], work, latent, p[:, 0:8, :])
            with ExitStack() as e3:
                work = [sb(n, [P] + d, e3) for n, d in (
                    ("ssd_cb", [2, 2, 512]), ("ssd_x", [ST, D]), ("ssd_e", [8, 512]), ("ssd_m", [4, 512]), ("ssd_xl", [ST, 2 * P]),
                    ("ssd_hs", [4 * S_PER_HEAD]), ("ssd_th", [2, SEQ]), ("ssd_z", [2, SEQ]), ("ssd_d", [2]))]
                ssd_heads(nc, st, bank, C2, cs, p, sc, lambda i: cols[:, bass.ds(i * 2 + col_at["ssm_d"][0], 2)], ys, work,
                          latent, p_rw)

        with ExitStack() as es:
            C2, cs, pair = const_part("rw0", 10, es)
            ps = sb("ps_rw", [P, 14, SEQ], es)
            lw = sb("lw_rw", [P, 2, ST, 512], es)
            g_t = sb("g_rw", [P, ST, 512], es)
            bonus = sb("bonus_rw", [P, 16], es)
            aa, kk = spare[:, 0:4, :], spare[:, 4:8, :]
            with ExitStack() as e3:
                tmp = sb("tmp_rw", [P, 14, SEQ], e3)
                up = sb("up_rw", [P, 2, 512], e3)
                a_up = sb("a_up", [P, 512], e3)
                g_up = sb("g_up", [P, 512], e3)
                w0_rows = sb("w0_rows", [P, 2, 512], e3)
                rc = sb("rc_rw", [P, 32], e3)
                loads = start_loads(nc, [pair, (up[0:64, :, :].rearrange("p a c -> p (a c)"), a["w_up"]), (a_up[64:128, :], a["a_up"]),
                              (g_up[:, :], a["g_up"]),
                              (w0_rows[:, :, :].rearrange("p a c -> p (a c)"), a["rows"][:, 128:1152].to_broadcast([P, 1024]))], small)
                norm(u, u, cc("ssm_norm_w"), 0)
                finish_loads(nc, loads, small)
                rwkv_inputs(nc, bank, C2, p_rw, ps, tmp, cc("rwkv_mu", 0, 14), cc("rwkv_mu", 14, 28), up[0:64], g_up, a_up,
                            [cc(n) for n in ("a0", "k_k", "k_a", "r_k")], w0_rows, lw, g_t, aa, kk, rc, bonus)
            y_all = sb("y_rw", [P, ST, 512], es)
            v_all = sb("v_rw", [P, ST, 512], es)
            with ExitStack() as e3:
                work = [sb("rw_" + n, [P] + d, e3) for n, d in (
                    ("lwl", [2, ST, P]), ("e_in", [2, SEQ]), ("e_ex", [2, SEQ]), ("e_neg", [2, SEQ]), ("ka", [2, SEQ]),
                    ("ki", [2, SEQ]), ("kw_rw", [2, 2, SEQ]), ("grams", [8, 512]), ("inv", [2, 512]), ("inv_t", [2, 512]),
                    ("prod", [2, 512]), ("ka_t", [2, ST, P]), ("k_t", [2, ST, P]), ("v_t", [ST, P]), ("v_half", [6 * P]),
                    ("p_half", [4 * P]), ("rr", [2 * P]), ("sb", [2, P]))]
                rwkv_heads(nc, st, bank, C2, cs, ps, lw, aa, kk, y_all, v_all, work, latent, p_hg)
            with ExitStack() as e3:
                ln_rows = sb("ln_rows", [P, 2, 512], e3)
                sq = sb("sq_rw", [P, ST, 512], e3)
                st16 = sb("st_rw", [P, 32], e3)
                load_all(nc, [(ln_rows[:, :, :].rearrange("p a c -> p (a c)"), a["rows"][:, 1152:2176].to_broadcast([P, 1024]))], small)
                rwkv_output(nc, st, bank, C2, y_all, v_all, g_t, bonus, ln_rows, sq, st16, yr, u, spare)

        yh = sb("yh", [P, HG, SEQ])
        gates = sb("gates", [P, 24, SEQ])
        with ExitStack() as es:
            C2, cs, pair = const_part("hg_f0", 16, es)
            lf = sb("lf_hg", [P, 2, ST, 512], es)
            kf = sb("kf_hg", [P, 2, HG, SEQ], es)
            with ExitStack() as e3:
                lb = sb("lb_hg", [P, 512], e3)
                om = sb("om_hg", [P, 512], e3)
                load_all(nc, [pair, (lb[:, :], a["rows"][:, 2176:2688].to_broadcast([P, 512]))], small)
                hgrn_forget(nc, bank, C2, spare, lf, kf, lb[:, :], om[:, :])
            with ExitStack() as e3:
                work = [sb("hg_" + n, [P] + d, e3) for n, d in (
                    ("lfl", [2, ST, P]), ("q2", [512]), ("kl", [512]), ("e", [2, 512]), ("qe", [2, 512]), ("ke", [2, 512]),
                    ("sc", [512]), ("tmp", [2, 512]), ("it", [SEQ]), ("ib", [ST, P]), ("ob", [SEQ]), ("osq", [SEQ]),
                    ("rc", [ST]), ("gg", [SEQ]), ("gt", [SEQ]), ("wl", [1]))]
                hgrn_heads(nc, st, bank, C2, cs, p_hg, lf, kf, lambda i: cols[:, bass.ds(i + col_at["hgrn_norm_w"][0], 1)], yh, work,
                           latent, gates)

        with ExitStack() as es:
            for b, (src, tiles, count) in enumerate(((ys, 8, 2), (yr, 4, 1), (yh, 4, 1))):
                gated_linear(nc, st, bank, count, 4, src, tiles, gates[:, 8 * b:8 * b + 8, :])
            mixed = gates[:, 0:8, :]
            with stage(nc, "") as (s, block):
                @block.vector
                def _(dve):
                    link = Chain(dve, s["dve_own"])
                    link(nc.vector.tensor_scalar(mixed, mixed, 0.5, None, ALU.mult))
                    for b in (1, 2):
                        link(nc.vector.scalar_tensor_tensor(mixed, gates[:, 8 * b:8 * b + 8, :], 0.5, mixed, ALU.mult, ALU.add))
            residual_linear(nc, st, bank, 2, 4, mixed, KT, h, None, ((CTX, SEQ, 0),), CTX)

        norm(h, u, cc("norm2_w"), CTX)
        with ExitStack() as es:
            ffn = sb("ffn", [P, FF, SEQ], es)
            ffn_tanh = sb("ffn_tanh", [P, 2, 2, SEQ], es)
            swiglu(nc, st, bank, latent, ffn, ffn_tanh)
            residual_linear(nc, st, bank, 4, 6, ffn, FF, h, None, ((CTX, SEQ, 0),), CTX)
        norm(h, u, cc("final_norm_w"), CTX)
        st.drain()
        finish(nc, out, u[:, :, CTX:TOK])


def swiglu(nc, st, bank, src, out, th):
    count = FF // 2
    st.begin(4)
    with stage(nc, "used tanh doubled done") as (s, block):
        def tensor(pe):
            def visit(g, h, r):
                if not isinstance(g, int) or g >= 2:
                    pe.wait_ge(s["done"], g * 2 - 2)
                for m in range(4):
                    st.wait(pe, h, r, m)
                    mm = accumulate(nc, bank[4 * h + m][:, 0:SEQ], [st.chunk(h, m)[:, P * k:P * k + P] for k in range(KT)],
                                    [src(k) for k in range(KT)])
                mm.then_inc(s["used"], 1)
            walk(pe, count, visit)

        def scalar(act):
            def visit(g, h, r):
                act.wait_ge(s["used"], g + 1)
                if not isinstance(g, int) or g >= 2:
                    act.wait_ge(s["done"], g * 2 - 2)
                for m in range(2):
                    nc.scalar.activation(th[:, h, m, :], bank[4 * h + m][:, 0:SEQ], ACT.Tanh, scale=0.5).then_inc(s["tanh"], 1)
            walk(act, count, visit)

        def vector(dve):
            def visit(g, h, r):
                for m in range(2):
                    dve.wait_ge(s["tanh"], g * 2 + 2)
                    nc.vector.scalar_tensor_tensor(th[:, h, m, :], th[:, h, m, :], 1.0, bank[4 * h + m][:, 0:SEQ],
                                                   ALU.add, ALU.mult).then_inc(s["doubled"], 1)
                    dve.wait_ge(s["doubled"], g * 2 + (m + 1))
                    nc.vector.scalar_tensor_tensor(out[:, bass.ds(g * 2 + m, 1), :].rearrange("p a t -> p (a t)"), th[:, h, m, :], 0.5,
                                                   bank[4 * h + 2 + m][:, 0:SEQ], ALU.mult, ALU.mult).then_inc(s["done"], 1)
            walk(dve, count, visit)
            dve.wait_ge(s["done"], 2 * count)

        st.groups(count, 4, s, block, ((block.tensor, tensor), (block.scalar, scalar), (block.vector, vector)))
    st.passed(count, 4)


def gated_linear(nc, st, bank, count, per_body, src, k_tiles, gates):
    def evacuate(m, ps):
        dst = gates[:, bass.ds(m, 1), :].rearrange("p a t -> p (a t)")
        return nc.vector.scalar_tensor_tensor(dst, dst, 1.0, ps[:, 0:SEQ], ALU.add, ALU.mult)
    linear(nc, st, bank, count, per_body, lambda k: src[:, k, :], SEQ, evacuate, k_tiles)


def project(nc, st, bank, count, per_body, src, n_tok, dst):
    def evacuate(m, ps):
        out = dst[:, bass.ds(m, 1), 0:n_tok].rearrange("p a t -> p (a t)")
        return nc.vector.tensor_copy(out, ps[:, 0:n_tok])
    linear(nc, st, bank, count, per_body, src, n_tok, evacuate)


def residual_linear(nc, st, bank, count, per_body, src, k_tiles, h, mod, streams, lo):
    n_tok = sum(x[1] for x in streams)

    def evacuate(m, ps):
        for t0, tn, c in streams:
            dst = h[:, bass.ds(m, 1), t0:t0 + tn].rearrange("p a t -> p (a t)")
            if mod is None:
                last = nc.vector.tensor_tensor(dst, ps[:, t0 - lo:t0 - lo + tn], dst, ALU.add)
            else:
                last = nc.vector.scalar_tensor_tensor(dst, ps[:, t0 - lo:t0 - lo + tn],
                                                      mod[:, bass.ds(m + 16, 1), c], dst, ALU.mult, ALU.add)
        return last
    linear(nc, st, bank, count, per_body, lambda k: src[:, k, 0:n_tok], n_tok, evacuate, k_tiles)


def finish(nc, out, src):
    n = src.shape[1] * SEQ
    with stage(nc, "stored") as (s, block):
        @block.sync
        def _(sp):
            sp.dma_start(out[:, 0:n].rearrange("p (k t) -> p k t", t=SEQ), src).then_inc(s["stored"], 16)
            sp.wait_ge(s["stored"], 16)


def fm(w, cols=None):
    k, m = w.shape
    return w.reshape(k // P, P, m // P, P).transpose(2, 1, 0, 3).reshape(m // P, P, k)


def fm_tiles(w):
    k, m = w.shape
    t = w.reshape(k // P, P, m // P, P).transpose(2, 0, 1, 3).reshape(-1, 8, P, P)
    return t.transpose(0, 2, 1, 3).reshape(-1, P, CHUNK)


def half_chunks(w):
    k, m = w.shape
    t = w.reshape(4, P, m // P, P).transpose(2, 0, 1, 3).reshape(-1, 8, P, P)
    return t.transpose(0, 2, 1, 3).reshape(-1, P, CHUNK)


def row_chunks(w):
    k, m = w.shape
    return w.reshape(k // 256, 2, P, m // 512, 512).transpose(3, 0, 2, 1, 4).reshape(-1, P, CHUNK)


def vec(v):
    return np.asarray(v).reshape(-1, P).T


def layout(x):
    f = lambda n: np.asarray(x[n])
    w_in = f("dn_w_in")[0]
    heads = []
    for h in range(QK_HEADS):
        at = [1024 + P * h, P * h, 2048 + 2 * P * h, 2048 + 2 * P * h + P, 4096 + 2 * P * h, 4096 + 2 * P * h + P]
        heads.append(np.concatenate([w_in[:, c:c + P] for c in at], axis=1))
    ada = f("ada_w")
    att = f("att_w_in")[0]
    stream = [row_chunks(ada[0]), fm(np.concatenate(heads, axis=1)), fm_tiles(f("dn_w_out")[0]), row_chunks(ada[1]),
              fm(att[:, 0:1024]), fm(att[:, 1536:2560]), fm(att[:, 1024:1536]), fm(f("att_w_out")[0])]
    stream += second_stream(f)
    stream.append(np.zeros((SLOTS, P, CHUNK), np.float32))
    conv = f("dn_conv_w")[0].T.reshape(32, P, 5)
    order = [t for h in range(QK_HEADS) for t in (8 + h, h, 16 + 2 * h, 17 + 2 * h)]
    conv = conv[order].transpose(1, 0, 2).reshape(P, 160)
    parts = {"c": np.stack([vec(x["c"]), vec(x["c_ctx"])], axis=2).reshape(P, 16), "norm_g": vec(x["norm_g"]),
             "ada_b": vec(x["ada_b"]), "conv": conv, "dn_o": vec(x["dn_o_norm_g"]), "qg": vec(x["att_q_norm_g"]),
             "kg": vec(x["att_k_norm_g"]), "final_g": vec(x["final_norm_g"])}
    parts.update(second_cols(f))
    col_at, at = {}, 0
    for n, v in parts.items():
        col_at[n] = (at, v.shape[1])
        at += v.shape[1]
    rows = [f("dn_dt_bias").reshape(-1), f("dn_a_log").reshape(-1)] + second_rows(f)
    both = np.concatenate([f("ctx")[0], f("x")[0]], axis=0)
    arrays = {
        "w": np.concatenate(stream, axis=0),
        "h": both.T.reshape(KT, P, TOK).transpose(1, 0, 2).reshape(P, KT * TOK),
        "cols": np.concatenate(list(parts.values()), axis=1),
        "rows": np.concatenate(rows)[None, :],
        "w_ab": w_in[:, 6144:6208].reshape(KT, P, 64).transpose(1, 0, 2).reshape(P, KT * 64),
        "const": const_array({n: const_tiles()[n] for n in FIRST_NAMES}),
        "rope": rope_tables(),
    }
    arrays.update(second_arrays(f))
    return {n: np.ascontiguousarray(v) for n, v in arrays.items()}, col_at


def second_stream(f):
    w = f("w_in_2")[0]
    rw, hg = 2592, 4384
    pad = np.zeros((D, 2 * P), np.float32)
    w_ff = f("ffn_w_in_2")[0].reshape(D, 2, FF // 2, 2 * P)
    pairs = w_ff.transpose(0, 2, 1, 3).reshape(D, 2 * FF * P)
    down = np.concatenate([f("ffn_w_down_2")[0], np.zeros((2 * P, D), np.float32)], axis=0)
    return [fm(w[:, 1024:2560]), fm(w[:, 0:1024]), fm(np.concatenate([w[:, rw:rw + 1792], pad], axis=1)),
            fm(np.concatenate([w[:, hg:hg + 512], w[:, hg + 1536:hg + 2560]], axis=1)), row_chunks(w[:, hg + 512:hg + 1536]),
            fm(w[:, 6944:10016]), fm(f("w_branch_ssm_2")[0]), half_chunks(f("w_branch_rwkv_2")[0]),
            half_chunks(f("w_branch_hgrn_2")[0]), fm(f("w_out_2")[0]), fm(pairs), fm_tiles(down)]


def second_cols(f):
    conv = f("ssm_conv_w_2")[0][:, 0, :].T.reshape(12, P, 5).transpose(1, 0, 2).reshape(P, 60)
    out = {"norm1_w": vec(f("norm1_w_2")), "ssm_conv": conv, "ssm_conv_b": vec(f("ssm_conv_b_2")),
           "ssm_d": vec(np.repeat(f("ssm_d_2")[0], 64)), "ssm_norm_w": vec(f("ssm_norm_w_2")),
           "rwkv_mu": vec(f("rwkv_mu_2")[0])}
    for n in ("a0", "k_k", "k_a", "r_k"):
        out[n] = vec(f(f"rwkv_{n}_2"))
    for n in ("hgrn_norm_w", "norm2_w", "final_norm_w"):
        out[n] = vec(f(n + "_2"))
    return out


def second_rows(f):
    names = ("ssm_dt_bias", "ssm_a_log", "rwkv_w0", "rwkv_ln_w", "rwkv_ln_b", "hgrn_lb_logits")
    return [f(n + "_2").reshape(-1) for n in names]


def second_arrays(f):
    return {"w_dt": f("w_in_2")[0][:, 2560:2592].reshape(KT, P, 32).transpose(1, 0, 2).reshape(P, KT * 32),
            "w_up": f("rwkv_w_up_2")[0].transpose(1, 0, 2).reshape(64, 1024), "a_up": f("rwkv_a_up_2")[0],
            "g_up": f("rwkv_g_up_2")[0], "const2": const_array(second_tiles())}


def kernel(**inputs):
    from concourse import bacc
    from concourse.bass_utils import run_bass_kernel_spmd

    arrays, col_at = layout(inputs)
    nc = bacc.Bacc("TRN2", target_bir_lowering=False, num_devices=1)
    a = {n: nc.dram_tensor(f"in_{n}", v.shape, F32, kind="ExternalInput").ap() for n, v in arrays.items()}
    out = nc.dram_tensor("out", (P, KT * SEQ), F32, kind="ExternalOutput").ap()
    build(nc, a, out, col_at)
    r = run_bass_kernel_spmd(nc, [{f"in_{n}": v for n, v in arrays.items()}], core_ids=[0])
    got = r.results[0]["out"]
    return got.reshape(P, KT, SEQ).transpose(1, 0, 2).reshape(D, SEQ).T[None]
```
